# Optimizing a Trainium2 kernel written in Bass

```python
import math
import jax
import jax.numpy as jnp
from jax import lax
import numpy as np

D_MODEL = 2048
BATCH = 1
SEQ = 256
DEPTH = 2

MLA_HEADS = 8
Q_LORA = 512
KV_LORA = 512
NOPE_DIM = 128
ROPE_DIM = 64
V_DIM = 128
ROPE_THETA = 10000.0
DIL_HEADS = 8
DIL_HEAD_DIM = 128
DIL_BRANCHES = ((128, 1), (512, 4), (2048, 16))
DIL_WIDTH = DIL_HEADS * DIL_HEAD_DIM
BLK = 128
IN_COLS = Q_LORA + KV_LORA + ROPE_DIM + 3 * DIL_WIDTH
MIX_WIDTH = MLA_HEADS * V_DIM + DIL_WIDTH
S5_GROUP = 16
S5_GROUPS = D_MODEL // S5_GROUP
S5_STATE = 64
FFN_HIDDEN = -(-8 * D_MODEL // (3 * 256)) * 256
PLE_DIM = 256
DEEPNORM_ALPHA = (2.0 * DEPTH) ** 0.25
DEEPNORM_BETA = (8.0 * DEPTH) ** -0.25
NEG = -1e30

kernel_name = 'hybrid_mla_dilated_s5_block'

def _layernorm(x, g, b, eps=1e-5):
    xf = x.astype(jnp.float32)
    mu = xf.mean(-1, keepdims=True)
    var = jnp.square(xf - mu).mean(-1, keepdims=True)
    y = (xf - mu) * lax.rsqrt(var + eps) * g.astype(jnp.float32) + b.astype(jnp.float32)
    return y.astype(x.dtype)

def _rmsnorm(x, g, eps=1e-6):
    xf = x.astype(jnp.float32)
    y = xf * lax.rsqrt(jnp.square(xf).mean(-1, keepdims=True) + eps) * g.astype(jnp.float32)
    return y.astype(x.dtype)

def _rope(t, positions):
    half = t.shape[-1] // 2
    inv_freq = ROPE_THETA ** (-jnp.arange(half, dtype=jnp.float32) / half)
    ang = positions.astype(jnp.float32)[..., None] * inv_freq
    cos, sin = jnp.cos(ang)[:, :, None, :], jnp.sin(ang)[:, :, None, :]
    t1, t2 = t[..., :half], t[..., half:]
    return jnp.concatenate([t1 * cos - t2 * sin, t1 * sin + t2 * cos], axis=-1).astype(t.dtype)

def _alibi_slopes(n):
    return jnp.asarray(2.0 ** (-8.0 * np.arange(1, n + 1) / n), dtype=jnp.float32)

def _mla_causal(q, k, v):
    B, S, H, Dqk = q.shape
    nb = S // BLK
    scale = Dqk ** -0.5
    qb = q.reshape(B, nb, BLK, H, Dqk).transpose(1, 0, 2, 3, 4)
    kpos = jnp.arange(S)

    def block(args):
        qblk, bi = args
        s = jnp.einsum('bqhd,bkhd->bhqk', qblk, k).astype(jnp.float32) * scale
        qpos = bi * BLK + jnp.arange(BLK)
        s = jnp.where(kpos[None, :] <= qpos[:, None], s, NEG)
        pr = jax.nn.softmax(s, axis=-1).astype(v.dtype)
        return jnp.einsum('bhqk,bkhd->bqhd', pr, v)

    out = lax.map(block, (qb, jnp.arange(nb)))
    return out.transpose(1, 0, 2, 3, 4).reshape(B, S, H * v.shape[-1])

def _dilated_branch(q, k, v, window, dilation, slopes):
    B, S, H, Dh = q.shape
    d = dilation
    L = S // d
    steps = window // d
    nb = -(-L // BLK)
    Lp = nb * BLK

    def to_classes(t):
        t = t.reshape(B, L, d, H, Dh).transpose(0, 2, 1, 3, 4).reshape(B * d, L, H, Dh)
        return jnp.pad(t, ((0, 0), (0, Lp - L), (0, 0), (0, 0)))

    def windows(t):
        tb = jnp.pad(t, ((0, 0), (BLK, 0), (0, 0), (0, 0))).reshape(B * d, nb + 1, BLK, H, Dh)
        return jnp.concatenate([tb[:, :-1], tb[:, 1:]], axis=2)

    qb = to_classes(q).reshape(B * d, nb, BLK, H, Dh)
    kw = windows(to_classes(k))
    vw = windows(to_classes(v))
    s = jnp.einsum('zbqhd,zbkhd->zbhqk', qb, kw).astype(jnp.float32) * (Dh ** -0.5)
    qi = jnp.arange(BLK)[:, None]
    ki = jnp.arange(2 * BLK)[None, :]
    dist = qi + BLK - ki
    kabs = jnp.arange(nb)[:, None, None] * BLK + ki[None] - BLK
    valid = (dist >= 0)[None] & (dist <= steps)[None] & (kabs >= 0)
    bias = -slopes[:, None, None] * (d * dist).astype(jnp.float32)[None]
    s = jnp.where(valid[None, :, None], s + bias[None, None], NEG)
    m = s.max(-1, keepdims=True)
    e = jnp.exp(s - m)
    l = e.sum(-1, keepdims=True)
    o = jnp.einsum('zbhqk,zbkhd->zbqhd', (e / l).astype(v.dtype), vw)
    lse = (m + jnp.log(l))[..., 0]
    o = o.reshape(B * d, Lp, H, Dh)[:, :L].reshape(B, d, L, H, Dh).transpose(0, 2, 1, 3, 4).reshape(B, S, H, Dh)
    lse = lse.transpose(0, 1, 3, 2).reshape(B * d, Lp, H)[:, :L].reshape(B, d, L, H).transpose(0, 2, 1, 3).reshape(B, S, H)
    return o, lse

def _hybrid_attention(h, positions, w_in, q_norm, w_q_b, kv_norm, w_kv_b, w_out):
    B, S, _ = h.shape
    splits = list(np.cumsum([Q_LORA, KV_LORA, ROPE_DIM, DIL_WIDTH, DIL_WIDTH]))
    q_lat, kv_lat, k_pe, qd, kd, vd = jnp.split(h @ w_in, splits, axis=-1)
    q = (_rmsnorm(q_lat, q_norm) @ w_q_b).reshape(B, S, MLA_HEADS, NOPE_DIM + ROPE_DIM)
    q = jnp.concatenate([q[..., :NOPE_DIM], _rope(q[..., NOPE_DIM:], positions)], axis=-1)
    kv = (_rmsnorm(kv_lat, kv_norm) @ w_kv_b).reshape(B, S, MLA_HEADS, NOPE_DIM + V_DIM)
    k_pe = jnp.broadcast_to(_rope(k_pe[:, :, None, :], positions), (B, S, MLA_HEADS, ROPE_DIM))
    k = jnp.concatenate([kv[..., :NOPE_DIM], k_pe], axis=-1)
    out_a = _mla_causal(q, k, kv[..., NOPE_DIM:])
    qd = qd.reshape(B, S, DIL_HEADS, DIL_HEAD_DIM)
    kd = kd.reshape(B, S, DIL_HEADS, DIL_HEAD_DIM)
    vd = vd.reshape(B, S, DIL_HEADS, DIL_HEAD_DIM)
    slopes = _alibi_slopes(DIL_HEADS)
    outs, lses = [], []
    for window, dilation in DIL_BRANCHES:
        o_g, lse_g = _dilated_branch(qd, kd, vd, window, dilation, slopes)
        outs.append(o_g)
        lses.append(lse_g)
    wts = jax.nn.softmax(jnp.stack(lses), axis=0)
    out_b = jnp.einsum('gbsh,gbshd->bshd', wts, jnp.stack(outs).astype(jnp.float32))
    out_b = out_b.astype(h.dtype).reshape(B, S, DIL_WIDTH)
    return jnp.concatenate([out_a, out_b], axis=-1) @ w_out

def _s5_glu(h, a_re, a_im, log_dt, b_re, b_im, c_re, c_im, d_skip, w_glu):
    B, S, D = h.shape
    f32 = jnp.float32
    u = h.astype(f32).reshape(B, S, S5_GROUPS, S5_GROUP)
    A = lax.complex(a_re.astype(f32), a_im.astype(f32))
    dt = jnp.exp(log_dt.astype(f32))[:, None]
    A_bar = jnp.exp(A * dt)
    B_bar = ((A_bar - 1.0) / A)[..., None] * lax.complex(b_re.astype(f32), b_im.astype(f32))
    C_mat = lax.complex(c_re.astype(f32), c_im.astype(f32))
    bu = jnp.einsum('bsgc,gpc->bsgp', u.astype(jnp.complex64), B_bar)
    a = jnp.broadcast_to(A_bar, bu.shape)

    def combine(left, right):
        a_l, b_l = left
        a_r, b_r = right
        return a_r * a_l, a_r * b_l + b_r

    _, states = lax.associative_scan(combine, (a, bu), axis=1)
    y = jnp.einsum('bsgp,gcp->bsgc', states, C_mat).real.reshape(B, S, D)
    y = y + d_skip.astype(f32) * h.astype(f32)
    z = jax.nn.gelu(y).astype(h.dtype)
    val, gate = jnp.split(z @ w_glu, 2, axis=-1)
    return val * jax.nn.sigmoid(gate)

def _swiglu(h, w_in, w_out):
    g, u = jnp.split(h @ w_in, 2, axis=-1)
    return (jax.nn.silu(g) * u) @ w_out

def setup_inputs(seed: int = 0) -> dict:
    key = jax.random.key(seed)
    ks = iter(jax.random.split(key, 40))
    ne, no = (DEPTH + 1) // 2, DEPTH // 2
    f32 = jnp.float32

    def nrm(shape, scale):
        return jax.random.normal(next(ks), shape, f32) * scale

    x = nrm((BATCH, SEQ, D_MODEL), 1.0)
    p = nrm((DEPTH, BATCH, SEQ, PLE_DIM), 1.0)
    positions = jnp.broadcast_to(jnp.arange(SEQ, dtype=jnp.int32), (BATCH, SEQ))
    attn_w_in = nrm((ne, D_MODEL, IN_COLS), D_MODEL ** -0.5)
    mla_q_norm = 1.0 + nrm((ne, Q_LORA), 0.02)
    mla_w_q_b = nrm((ne, Q_LORA, MLA_HEADS * (NOPE_DIM + ROPE_DIM)), Q_LORA ** -0.5)
    mla_kv_norm = 1.0 + nrm((ne, KV_LORA), 0.02)
    mla_w_kv_b = nrm((ne, KV_LORA, MLA_HEADS * (NOPE_DIM + V_DIM)), KV_LORA ** -0.5)
    attn_w_out = nrm((ne, MIX_WIDTH, D_MODEL), MIX_WIDTH ** -0.5 * DEEPNORM_BETA)
    s5_a_re = -0.5 + nrm((no, S5_GROUPS, S5_STATE), 0.01)
    s5_a_im = math.pi * jnp.arange(S5_STATE, dtype=f32) + nrm((no, S5_GROUPS, S5_STATE), 0.01)
    s5_log_dt = jax.random.uniform(next(ks), (no, S5_GROUPS), f32, math.log(1e-3), math.log(1e-1))
    s5_b_re = nrm((no, S5_GROUPS, S5_STATE, S5_GROUP), (2 * S5_GROUP) ** -0.5)
    s5_b_im = nrm((no, S5_GROUPS, S5_STATE, S5_GROUP), (2 * S5_GROUP) ** -0.5)
    s5_c_re = nrm((no, S5_GROUPS, S5_GROUP, S5_STATE), (2 * S5_STATE) ** -0.5)
    s5_c_im = nrm((no, S5_GROUPS, S5_GROUP, S5_STATE), (2 * S5_STATE) ** -0.5)
    s5_d = nrm((no, D_MODEL), 1.0)
    s5_w_glu = jnp.concatenate([nrm((no, D_MODEL, D_MODEL), D_MODEL ** -0.5 * DEEPNORM_BETA),
                                nrm((no, D_MODEL, D_MODEL), D_MODEL ** -0.5)], axis=-1)
    ln1_g = 1.0 + nrm((DEPTH, D_MODEL), 0.02)
    ln1_b = nrm((DEPTH, D_MODEL), 0.02)
    ffn_w_in = nrm((DEPTH, D_MODEL, 2 * FFN_HIDDEN), D_MODEL ** -0.5)
    ffn_w_out = nrm((DEPTH, FFN_HIDDEN, D_MODEL), FFN_HIDDEN ** -0.5 * DEEPNORM_BETA)
    ple_w = nrm((DEPTH, PLE_DIM, D_MODEL), PLE_DIM ** -0.5)
    ple_gate_w = nrm((DEPTH, D_MODEL, D_MODEL), D_MODEL ** -0.5)
    ln2_g = 1.0 + nrm((DEPTH, D_MODEL), 0.02)
    ln2_b = nrm((DEPTH, D_MODEL), 0.02)
    return {'x': x, 'p': p, 'positions': positions,
            'attn_w_in': attn_w_in, 'mla_q_norm': mla_q_norm, 'mla_w_q_b': mla_w_q_b,
            'mla_kv_norm': mla_kv_norm, 'mla_w_kv_b': mla_w_kv_b, 'attn_w_out': attn_w_out,
            's5_a_re': s5_a_re, 's5_a_im': s5_a_im, 's5_log_dt': s5_log_dt,
            's5_b_re': s5_b_re, 's5_b_im': s5_b_im, 's5_c_re': s5_c_re, 's5_c_im': s5_c_im,
            's5_d': s5_d, 's5_w_glu': s5_w_glu,
            'ln1_g': ln1_g, 'ln1_b': ln1_b, 'ffn_w_in': ffn_w_in, 'ffn_w_out': ffn_w_out,
            'ple_w': ple_w, 'ple_gate_w': ple_gate_w, 'ln2_g': ln2_g, 'ln2_b': ln2_b}

def reference(x, p, positions, attn_w_in, mla_q_norm, mla_w_q_b, mla_kv_norm, mla_w_kv_b, attn_w_out,
              s5_a_re, s5_a_im, s5_log_dt, s5_b_re, s5_b_im, s5_c_re, s5_c_im, s5_d, s5_w_glu,
              ln1_g, ln1_b, ffn_w_in, ffn_w_out, ple_w, ple_gate_w, ln2_g, ln2_b):
    h = x
    for i in range(DEPTH):
        j = i // 2
        if i % 2 == 0:
            mix = _hybrid_attention(h, positions, attn_w_in[j], mla_q_norm[j], mla_w_q_b[j],
                                    mla_kv_norm[j], mla_w_kv_b[j], attn_w_out[j])
        else:
            mix = _s5_glu(h, s5_a_re[j], s5_a_im[j], s5_log_dt[j], s5_b_re[j], s5_b_im[j],
                          s5_c_re[j], s5_c_im[j], s5_d[j], s5_w_glu[j])
        h = _layernorm(DEEPNORM_ALPHA * h + mix, ln1_g[i], ln1_b[i])
        ple = (p[i] @ ple_w[i]) * jax.nn.sigmoid(h @ ple_gate_w[i])
        h = _layernorm(DEEPNORM_ALPHA * h + _swiglu(h, ffn_w_in[i], ffn_w_out[i]) + ple, ln2_g[i], ln2_b[i])
    return h


_drawn_inputs = setup_inputs


def setup_inputs(seed=0):
    import zlib

    import numpy as np

    out = dict(_drawn_inputs(seed))
    spreads = {}
    factors = {'mla_q_norm': 8.0,
     'mla_kv_norm': 8.0,
     's5_a_re': 64.0,
     's5_a_im': 64.0,
     's5_log_dt': 64.0,
     's5_b_re': 64.0,
     's5_b_im': 64.0,
     's5_c_re': 64.0,
     's5_c_im': 64.0}
    for name, (base, spread) in spreads.items():
        noise = np.random.default_rng([zlib.crc32(name.encode()), seed]).standard_normal(out[name].shape)
        drawn = base * np.exp(spread * noise) if base else spread * noise
        out[name] = jnp.asarray(drawn.astype(out[name].dtype))
    for name, factor in factors.items():
        out[name] = (out[name] * factor).astype(out[name].dtype)
    return out
```

```python
from contextlib import ExitStack

import numpy as np

import concourse.bass as bass
from concourse import mybir

F32 = mybir.dt.float32
F32R = mybir.dt.float32r
I32 = mybir.dt.int32
ALU = mybir.AluOpType
ACT = mybir.ActivationFunctionType
AX_X = mybir.AxisListType.X

P = 128
TOK = 256
TT = TOK // P
D = 2048
KT = D // P
WB = 512
RING = 4
LAT = 512
HEADS = 8
HD = 128
ROPE = 64
HALF = ROPE // 2
FFN = 5632
FA, FB = 12, 10
PLE = 256
LAYERS = 2
ALPHA = float((2.0 * LAYERS) ** 0.25)
MLA_SCALE = float((HD + ROPE) ** -0.5)
DIL_SCALE = float(HD ** -0.5)
SLOPES = [2.0 ** (-(h + 1)) for h in range(HEADS)]
GROUP = 16
PAIRS = D // GROUP // 2
SEG = 64
SEGS = TOK // SEG
ROUND = 12582912.0

PHASES = {}
_c = _b = 0
for _name, _n, _per in [("win", 8, 8), ("kpe", 1, 8), ("qb", 3, 2), ("kvb", 4, 2), ("wout", 4, 8),
                        ("ple0", 4, 1), ("gate0", 4, 8), ("inA0", FA, 8), ("outA0", 4, FA), ("inB0", FB, 8), ("outB0", 4, FB),
                        ("glu", 8, 8),
                        ("ple1", 4, 1), ("gate1", 4, 8), ("inA1", FA, 8), ("outA1", 4, FA), ("inB1", FB, 8), ("outB1", 4, FB)]:
    PHASES[_name] = (_n, _per, _c, _b)
    _c += _n * _per
    _b += _n if not _name.startswith("ple") else 0


def lin(const, coef=0, i=None):
    return const if i is None else i * coef + const


def blocks(eng, n, body):
    body(0, None)
    if n >= 6:
        with eng.Fori(0, (n - 2) // 2) as i:
            body(1, i)
            body(2, i)
    else:
        for k in range(1, n - 1):
            body(k, None)
    body(n - 1, None)


def build(nc, t, out):
    KB = 1024
    base = 16512
    with ExitStack() as ctx:
        def at(name, shape, kb, dt=F32):
            return nc.alloc_sbuf_tensor_at(name, shape, dt, offset=base + int(kb * KB))

        def sem(name):
            return ctx.enter_context(nc.semaphore(name))

        RAW = at("raw", [P, RING, 2, WB], 0)
        WH = at("w_hi", [P, RING, 2, WB], 16, F32R)
        WL = at("w_lo", [P, RING, 2, WB], 32, F32R)
        XH = at("x_hi", [P, KT, TOK], 48, F32R)
        XL = at("x_lo", [P, KT, TOK], 64, F32R)
        RES = at("res", [P, TT, D], 80)
        GB = at("gb", [P, 2, D], 96)
        HH = at("hid_hi", [P, 2 * FA, TOK], 112, F32R)
        HL = at("hid_lo", [P, 2 * FA, TOK], 136, F32R)
        PL = at("ple", [P, TT, D], 160)
        BB = at("s5_b", [P, KT, 2, P], 176)
        QK = at("qk_dil", [P, 2 * HEADS, TOK], 96)
        VD = at("v_dil", [P, TT, HEADS * HD], 112)
        LH = at("lat_hi", [P, 8, TOK], 120, F32R)
        LL = at("lat_lo", [P, 8, TOK], 128, F32R)
        QN = at("q_nope", [P, HEADS, TOK], 136)
        QP = at("q_pe", [P, HEADS // 2, TOK], 144)
        KP = at("k_pe", [P, TOK], 148)
        KN = at("k_nope", [P, HEADS, TOK], 152)
        VM = at("v_mla", [P, TT, HEADS * HD], 160)
        STG = at("stage", [P, 2, TT, WB], 168)
        SM = at("s_masked", [P, 2, 3 * P], 176)
        PR = at("probs", [P, 2, 3 * P], 179)
        PT = at("probs_t", [P, 2, 3 * P], 182)
        NG = at("norm_gain", [P, 2 * LAT], 185)
        CS = at("cos_sin", [P, 2, TT, HALF], 189)
        AT = at("angle_tmp", [P, 4, TT, HALF], 190)
        CC = at("s5_c", [P, PAIRS, 2, 2 * GROUP], 96)
        ST = [at("states0", [P, SEG, 2, PAIRS], 112), at("states1", [P, SEG, 2, PAIRS], 48)]
        HT = at("h_t", [P, KT, TOK], 144)
        BR = at("s5_b_re", [P, KT, P], 112)
        BI = at("s5_b_im", [P, KT, P], 120)
        CR = at("s5_coef_re", [P, KT, P], 128)
        CI = at("s5_coef_im", [P, KT, P], 136)
        TB = at("s5_tmp", [P, KT, P], 144)
        S5 = at("s5_small", [64, 16, P], 152)
        PK = at("p_tok", [P, TT, PLE], 160)
        ID = at("ident", [P, P], 192)
        DM = at("neg_dist", [P, 3 * P], 192.5)
        NM = at("branches", [P, 3 * P], 194)
        CM = at("causal", [P, 3 * P], 195.5)
        GT = at("gated", [P, 2, TT, 256], 197)
        AB = at("a_bar", [P, 4, PAIRS], 201)
        PH = at("p_hi", [P, 2, TOK], 202, F32R)
        PLO = at("p_lo", [P, 2, TOK], 204, F32R)
        BS = at("bn_stats", [P, TT, 8, 6], 206)
        MV = at("mean_var", [P, TT, 2], 206.5)
        SC = at("small", [P, 24], 206.625)
        SI = at("small_int", [P, 8], 206.75, I32)
        SD = at("s5_d", [P, KT], 206.8125)
        PI = at("positions", [P, TT], 206.875, I32)
        MX = at("row_max", [P, 2, 4], 206.9375)
        GTf = GT[:, :, :, :].rearrange("p a t n -> p (a t n)")

        A = ctx.enter_context(nc.psum_tensor("acc", [P, 2, TT, WB], F32))
        TP = ctx.enter_context(nc.psum_tensor("turn", [P, 2, 2, TOK], F32))
        Y = ctx.enter_context(nc.psum_tensor("y", [P, 2, WB], F32))

        coef_dram = nc.dram_tensor("s5_coef", (2, PAIRS, P), F32, kind="Internal").ap()

        raw_full = [sem(f"raw_full{s}") for s in range(RING)]
        hi_ready, lo_ready, w_used = sem("hi_ready"), sem("lo_ready"), sem("w_used")
        x_in, p_in, p1_in, const_in, gb_in, late_in = sem("x_in"), sem("p_in"), sem("p1_in"), sem("const_in"), sem("gb_in"), sem("late_in")
        acc_free = sem("acc_free")
        turn_done = sem("turn_done")
        turn_hi = sem("turn_hi")
        turned = sem("turned")
        staged = sem("staged")
        v_step = sem("v_step")
        sq_sum = sem("sq_sum")
        trig = sem("trig")
        s_done, s_masked, nmax, p_exp, p_ready = sem("s_done"), sem("s_masked"), sem("nmax"), sem("p_exp"), sem("p_ready")
        p_turned, pt_ready, pv_done, mix_hi, mix_ready = sem("p_turned"), sem("pt_ready"), sem("pv_done"), sem("mix_hi"), sem("mix_ready")
        ln_quarter = sem("ln_quarter")
        ple_ready, gate_act, silu_done, hid_ready = sem("ple_ready"), sem("gate_act"), sem("silu_done"), sem("hid_ready")
        glu_step = sem("glu_step")
        tab, coef_out, coef_in, tab_ready = sem("tab"), sem("coef_out"), sem("coef_in"), sem("tab_ready")
        ab_turned, ab_ready, c_in, c_ready = sem("ab_turned"), sem("ab_ready"), sem("c_in"), sem("c_ready")
        bu_done, bu_out, scan, y_done, y_added, z_done = (sem("bu_done"), sem("bu_out"), sem("scan"), sem("y_done"),
                                                          sem("y_added"), sem("z_done"))
        stored = sem("stored")

        TG = {}
        n = 0
        for name, count in [("x", 8), ("p0", 1), ("lat", 4), ("qk", 8), ("kpe", 1), ("qn", 4), ("qp", 2), ("kn", 4),
                            ("ln10", 8), ("hid0", FA + FB), ("ln20", 8), ("p1", 1), ("z", 0), ("ln11", 8),
                            ("hid1", FA + FB)]:
            TG[name] = n
            n += count
        HG = {}
        n = 0
        for name, count in [("x", 8), ("p0", 1), ("lat", 4), ("ln10", 8), ("hid0", FA + FB), ("p1", 1), ("ln11", 8),
                            ("hid1", FA + FB)]:
            HG[name] = n
            n += count

        block = ctx.enter_context(nc.Block())

        @block.sync
        def _(sp):
            sp.dma_start(RES[:], t["x"].rearrange("(t p) n -> p t n", p=P)).then_inc(x_in, 16)
            sp.dma_start(ID[:], t["ident"]).then_inc(x_in, 16)

            def load(w, local, c, coef, i, width):
                if c >= RING:
                    sp.wait_ge(lo_ready, lin(c - RING + 1, coef, i))
                src = w[bass.ds(lin(local, coef, i), 1)].rearrange("a p (k n) -> (a p) k n", k=2)
                sp.dma_start(RAW[:, c % RING, :, 0:width], src).then_inc(raw_full[c % RING], 16)

            def phase(name, weight, width=WB):
                nb, per, c0, _ = PHASES[name]
                w, total = t[weight], nb * per
                first = RING if c0 == 0 else 0
                for j in range(first):
                    load(w, j, j, 0, None, width)
                if (total - first) % RING:
                    for j in range(first, total):
                        load(w, j, c0 + j, 0, None, width)
                elif total - first == RING:
                    for j in range(first, total):
                        load(w, j, c0 + j, 0, None, width)
                else:
                    with sp.Fori(0, (total - first) // RING) as i:
                        for j in range(RING):
                            load(w, first + j, c0 + first + j, RING, i, width)

            phase("win", "w_in")
            phase("kpe", "w_kpe", ROPE)
            phase("qb", "w_qb")
            phase("kvb", "w_kvb")
            phase("wout", "w_out")
            for layer in range(LAYERS):
                if layer:
                    phase("glu", "w_glu")
                for name in ("ple", "gate", "inA", "outA", "inB", "outB"):
                    phase(f"{name}{layer}", f"w_{name}{layer}")

        @block.tensor
        def _(pe):
            def chunk(c, coef, i, hi, lo, kt, depth, acc, width=WB):
                pe.wait_ge(lo_ready, lin(c + 1, coef, i))
                s = c % RING
                for k in range(2):
                    for q in range(TT):
                        cols = slice(q * P, (q + 1) * P)
                        o = A[:, acc, q, 0:width]
                        pe.matmul(o, hi[:, kt + k, cols], WH[:, s, k, 0:width], start=(kt + k == 0), stop=False)
                        pe.matmul(o, hi[:, kt + k, cols], WL[:, s, k, 0:width], start=False, stop=False)
                        last = pe.matmul(o, lo[:, kt + k, cols], WH[:, s, k, 0:width], start=False,
                                         stop=(kt + k == depth - 1))
                last.then_inc(w_used, 1)

            def acc_ready(b, coef=0, i=None):
                if b >= 2:
                    pe.wait_ge(acc_free, lin(b - 1, coef, i))

            def turn(g, src, col, coef=0, i=None):
                if g >= 2:
                    pe.wait_ge(turned, lin(g - 1, coef, i))
                for k in range(2):
                    for q in range(TT):
                        last = pe.transpose(TP[:, g % 2, k, q * P:(q + 1) * P],
                                            src[:, q, col + k * P:col + (k + 1) * P], ID[:])
                last.then_inc(turn_done, 1)

            pe.wait_ge(x_in, 32)
            for g in range(8):
                turn(TG["x"] + g, RES[:], 256 * g)
            pe.wait_ge(p_in, 16)
            turn(TG["p0"], PK[:], 0)

            _, per, c0, b0 = PHASES["win"]
            for b in range(8):
                acc_ready(b0 + b)
                for j in range(per):
                    if b == 0:
                        pe.wait_ge(turned, TG["x"] + j + 1)
                    chunk(c0 + per * b + j, 0, None, XH, XL, 2 * j, KT, (b0 + b) % 2)
                    if j == 3 and 1 <= b <= 6:
                        pe.wait_ge(staged, b)
                        first = TG["lat"] + 2 * (b - 1) if b <= 2 else TG["qk"] + 2 * (b - 3)
                        for g in range(2):
                            turn(first + g, STG[:, (b - 1) % 2], 256 * g)
            _, per, c0, b0 = PHASES["kpe"]
            acc_ready(b0)
            for j in range(per):
                chunk(c0 + j, 0, None, XH, XL, 2 * j, KT, b0 % 2, ROPE)

            QB, KVB = PHASES["qb"], PHASES["kvb"]
            groups = [TG["kpe"], TG["qn"], TG["qn"] + 2, TG["qp"], TG["kn"], TG["kn"] + 2]

            def turn_up(m):
                pe.wait_ge(staged, 7 + m)
                if m == 0:
                    g = TG["kpe"]
                    pe.wait_ge(turned, g - 1)
                    for q in range(TT):
                        last = pe.transpose(TP[:, g % 2, 0, q * P:(q + 1) * P], STG[:, 0, q, 0:P], ID[:])
                    last.then_inc(turn_done, 1)
                else:
                    for g in range(2):
                        turn(groups[m] + g, STG[:, m % 2], 256 * g)

            pe.wait_ge(turned, TG["qk"])
            for b in range(7):
                acc_ready(QB[3] + b)
                for j in range(2):
                    row = 2 * j
                    part = slice(0, 4) if b < 3 else slice(4, 8)
                    chunk(QB[2] + 2 * b + j, 0, None, LH[:, part], LL[:, part], row, 4, (QB[3] + b) % 2)
                if b >= 1 and b <= 6:
                    turn_up(b - 1)

            pe.wait_ge(acc_free, QB[3] + 7)
            pe.wait_ge(turned, TG["ln10"])

            def scores(h):
                if h >= 2:
                    pe.wait_ge(s_masked, h - 1)
                dst = A[:, 0, h % 2]
                for q in range(TT):
                    cols = slice(0, P) if q == 0 else slice(P, 3 * P)
                    keys = slice(0, (q + 1) * P)
                    rows = slice(q * P, (q + 1) * P)
                    if h < HEADS:
                        last = pe.matmul(dst[:, cols], QK[:, h, rows], QK[:, HEADS + h, keys], start=True, stop=True)
                    else:
                        m = h - HEADS
                        half = slice(ROPE * (m % 2), ROPE * (m % 2) + ROPE)
                        pe.matmul(dst[:, cols], QN[:, m, rows], KN[:, m, keys], start=True, stop=False)
                        last = pe.matmul(dst[:, cols], QP[half, m // 2, rows], KP[half, keys], start=False, stop=True)
                last.then_inc(s_done, 1)

            def turn_probs(h):
                pe.wait_ge(p_ready, h + 1)
                if h >= 2:
                    pe.wait_ge(pt_ready, h - 1)
                for n_, s in enumerate([0, 1, 2]):
                    last = pe.transpose(Y[:, h % 2, n_ * P:(n_ + 1) * P], PR[:, h % 2, s * P:(s + 1) * P], ID[:])
                last.then_inc(p_turned, 1)

            def values(h):
                pe.wait_ge(pt_ready, h + 1)
                if h >= 2:
                    pe.wait_ge(mix_ready, h - 1)
                v = VD if h < HEADS else VM
                d = slice((h % HEADS) * HD, (h % HEADS + 1) * HD)
                pe.matmul(A[:, 1, h % 2, 0:TOK], v[:, 0, d], PT[:, h % 2, 0:TOK], start=True, stop=False)
                pe.matmul(A[:, 1, h % 2, P:TOK], v[:, 1, d], PT[:, h % 2, TOK:3 * P], start=False,
                          stop=True).then_inc(pv_done, 1)

            for s in range(2 * HEADS + 2):
                if s < 2 * HEADS:
                    if s == HEADS:
                        pass
                    scores(s)
                if 1 <= s <= 2 * HEADS:
                    turn_probs(s - 1)
                if s >= 2:
                    values(s - 2)

            _, per, c0, b0 = PHASES["wout"]
            for b in range(4):
                if b:
                    acc_ready(b0 + b)
                for j in range(per):
                    if b == 0:
                        pe.wait_ge(mix_ready, 16 if j == 7 else 2 * j + 2)
                    chunk(c0 + per * b + j, 0, None, XH, XL, 2 * j, KT, (b0 + b) % 2)

            def feed_forward(layer):
                _, _, c0, b0 = PHASES[f"ple{layer}"]
                pe.wait_ge(turned, TG[f"p{layer}"] + 1)
                for b in range(4):
                    if b < 2:
                        pe.wait_ge(acc_free, b0 - 1 + b)
                    else:
                        pe.wait_ge(ple_ready, 4 * layer + b - 1)
                    chunk(c0 + b, 0, None, PH, PLO, 0, 2, (b0 + b) % 2)
                _, per, c0, b0 = PHASES[f"gate{layer}"]
                g0 = TG[f"ln1{layer}"]
                for b in range(4):
                    acc_ready(b0 + b)
                    if b < 2:
                        pe.wait_ge(ple_ready, 4 * layer + 3 + b)
                    for j in range(per):
                        if b == 0:
                            if j % 2 == 0:
                                pe.wait_ge(ln_quarter, 8 * layer + j // 2 + 1)
                                turn(g0 + j, RES[:], 256 * j)
                                turn(g0 + j + 1, RES[:], 256 * (j + 1))
                            pe.wait_ge(turned, g0 + j + 1)
                        chunk(c0 + per * b + j, 0, None, XH, XL, 2 * j, KT, (b0 + b) % 2)

                if layer == 0:
                    pe.wait_ge(tab_ready, 1)
                    for n_ in range(2):
                        last = pe.transpose(Y[:, 0, n_ * PAIRS:(n_ + 1) * PAIRS], S5[:, n_, :], ID[0:64, 0:64])
                    last.then_inc(ab_turned, 1)

                def hidden_turn(b, coef=0, i=None):
                    done = (FA + FB) * layer + b
                    pe.wait_ge(hid_ready, lin(done + 1, coef, i))
                    turn(TG[f"hid{layer}"] + b, GT[:, 1], 0, coef, i)

                for part, n_in, first in (("A", FA, 0), ("B", FB, FA)):
                    _, per, c0, b0 = PHASES[f"in{part}{layer}"]

                    def inner(k, i):
                        acc_ready(b0 + k, 2, i)
                        for j in range(per):
                            chunk(c0 + per * k + j, 2 * per, i, XH, XL, 2 * j, KT, (b0 + k) % 2)
                            if j == 3 and k > 0:
                                hidden_turn(first + k - 1, 2, i)
                    blocks(pe, n_in, inner)
                    _, per, c0, b0 = PHASES[f"out{part}{layer}"]
                    for b in range(4):
                        acc_ready(b0 + b)
                        for j in range(per):
                            if b == 0 and j == per - 1:
                                pe.wait_ge(turned, TG[f"hid{layer}"] + first + n_in)
                            elif b == 0 and j == 0:
                                pe.wait_ge(turned, TG[f"hid{layer}"] + first + n_in - 1)
                            chunk(c0 + per * b + j, 0, None, HH, HL, 2 * j, 2 * n_in, (b0 + b) % 2)
                            if b == 0 and j == 3:
                                hidden_turn(first + n_in - 1)

            feed_forward(0)

            for g in range(8):
                if g % 2 == 0:
                    pe.wait_ge(ln_quarter, 4 + g // 2 + 1)
                turn(TG["ln20"] + g, RES[:], 256 * g)
            pe.wait_ge(p1_in, 16)
            turn(TG["p1"], PK[:], 0)
            pe.wait_ge(turned, TG["p1"])
            pe.wait_ge(tab_ready, 2)

            def drive(seg):
                for q in range(4):
                    for r in range(4):
                        n_ = 16 * seg + 4 * q + r
                        if n_ >= 4:
                            pe.wait_ge(bu_out, n_ - 3)
                        rows = slice(32 * r, 32 * r + 32)
                        for a in range(4):
                            for ri in range(2):
                                o = (2 * a + ri) * SEG
                                last = pe.matmul(A[:, r // 2, r % 2, o:o + SEG], BB[rows, 4 * q + a, ri, :],
                                                 HT[rows, 4 * q + a, SEG * seg:SEG * (seg + 1)], start=True, stop=True)
                        last.then_inc(bu_done, 1)

            def read_out(seg):
                pe.wait_ge(scan, 3 * (SEG * (seg + 1) - 1))
                if seg == 0:
                    pe.wait_ge(c_ready, 1)
                    pe.wait_ge(ab_ready, 3)
                else:
                    pe.wait_ge(y_added, 16 * seg)
                s = ST[seg % 2]
                for tile in range(KT):
                    for r in range(4):
                        pair = 4 * tile + r
                        o = Y[32 * r:32 * r + 32, tile // 8, (tile % 8) * SEG:(tile % 8 + 1) * SEG]
                        pe.matmul(o, CC[:, pair, 0, :], s[:, :, 0, pair], start=True, stop=False)
                        last = pe.matmul(o, CC[:, pair, 1, :], s[:, :, 1, pair], start=False, stop=True)
                last.then_inc(y_done, 1)

            drive(0)
            for seg in range(SEGS):
                if seg + 1 < SEGS:
                    drive(seg + 1)
                read_out(seg)

            _, per, c0, b0 = PHASES["glu"]

            def glu(k, i):
                acc_ready(b0 + k, 2, i)
                for j in range(per):
                    if k == 0:
                        pe.wait_ge(z_done, 64 + 2 * j + 2)
                    chunk(c0 + per * k + j, 2 * per, i, XH, XL, 2 * j, KT, (b0 + k) % 2)
            blocks(pe, 8, glu)
            feed_forward(1)

        @block.scalar
        def _(act):
            for dst, name in [(DM[:], "neg_dist"), (NM[:], "branches"), (CM[:], "causal"), (SD[:], "s5_d"), (PI[:], "pos")]:
                act.dma_start(dst, t[name]).then_inc(const_in, 16)
            act.dma_start(NG[:], t["norm_gain"].partition_broadcast(P)).then_inc(const_in, 16)
            for q in range(TT):
                act.dma_start(AT[:, 3, q, :], t["inv_freq"].partition_broadcast(P)).then_inc(const_in, 16)
            act.dma_start(PK[:], t["p"][0].rearrange("(t p) n -> p t n", p=P)).then_inc(p_in, 16)

            def hi(c, coef=0, i=None, width=WB):
                s = c % RING
                act.wait_ge(raw_full[s], lin(16 * (c // RING + 1), 16 * coef // RING, i))
                if c >= RING:
                    act.wait_ge(w_used, lin(c - RING + 1, coef, i))
                act.activation(WH[:, s, :, 0:width], RAW[:, s, :, 0:width], ACT.Copy).then_inc(hi_ready, 1)

            def hi_turned(g, dst, coef=0, i=None):
                act.wait_ge(turn_done, lin(g + 1, coef, i))
                act.activation(dst, TP[:, g % 2], ACT.Copy).then_inc(turn_hi, 1)

            def end(name, b, coef=0, i=None):
                _, per, c0, _ = PHASES[name]
                act.wait_ge(w_used, lin(c0 + per * (b + 1), per * coef, i))

            _, _, c0, b0 = PHASES["win"]
            for g in range(8):
                hi_turned(TG["x"] + g, XH[:, 2 * g:2 * g + 2, :])
                if g < RING:
                    hi(g)
            hi_turned(TG["p0"], PH[:])

            def stage(m, name, b, parity):
                end(name, b)
                if m >= 2:
                    pass
                act.activation(STG[:, m % 2], A[:, parity], ACT.Copy).then_inc(staged, 1)

            def win_end(b):
                end("win", b)
                if b < 2:
                    if b == 0:
                        act.wait_ge(const_in, 8 * 16)
                    else:
                        act.wait_ge(sq_sum, 2 * b)
                    for q in range(TT):
                        act.activation(GTf[:, WB * q:WB * (q + 1)], A[:, b % 2, q], ACT.Square,
                                       accum_out=SC[:, 2 * b + q:2 * b + q + 1]).then_inc(sq_sum, 1)
                elif b < 6:
                    act.wait_ge(turn_done, TG["lat"] + 2 * (b - 1))
                    act.activation(STG[:, b % 2], A[:, b % 2], ACT.Copy).then_inc(staged, 1)
                else:
                    act.activation(VD[:, :, (b - 6) * WB:(b - 5) * WB], A[:, b % 2], ACT.Copy).then_inc(acc_free, 1)

            for b in range(8):
                for j in range(8):
                    c = 8 * b + j
                    if c >= RING:
                        hi(c)
                    if j == 4 and b:
                        win_end(b - 1)
                    if b == 3 and j == 6:
                        act.wait_ge(trig, 1)
                        act.activation(CS[:, 1], AT[:, 0], ACT.Sin).then_inc(trig, 1)
                        act.activation(CS[:, 0], AT[:, 0], ACT.Sin, scale=0.5).then_inc(trig, 1)
                    if b >= 1 and j == 7 and b <= 2:
                        for g in range(2):
                            n_ = 2 * (b - 1) + g
                            hi_turned(TG["lat"] + n_, LH[:, 2 * n_:2 * n_ + 2, :])
            c0 = PHASES["kpe"][2]
            for j in range(8):
                hi(c0 + j, width=ROPE)
                if j == 4:
                    win_end(7)
            QB, KVB = PHASES["qb"], PHASES["kvb"]

            def up_end(m):
                b = m - 1
                act.wait_ge(w_used, QB[2] + 2 * (b + 1))
                if m in (1, 2, 4, 5):
                    if m <= 2:
                        if m == 2:
                            act.wait_ge(turn_done, TG["kpe"] + 1)
                    else:
                        act.wait_ge(turn_done, TG["qn"] + 2 * (m - 2))
                    act.activation(STG[:, m % 2], A[:, (QB[3] + b) % 2], ACT.Copy).then_inc(staged, 1)
                elif m >= 6:
                    act.activation(VM[:, :, (m - 6) * WB:(m - 5) * WB], A[:, (QB[3] + b) % 2],
                                   ACT.Copy).then_inc(acc_free, 1)

            for b in range(7):
                hi(QB[2] + 2 * b)
                hi(QB[2] + 2 * b + 1)
                if b >= 1:
                    up_end(b)
            up_end(7)

            c0 = PHASES["wout"][2]

            def exps(h):
                act.wait_ge(nmax, h + 1)
                if h >= 2:
                    act.wait_ge(p_turned, h - 1)
                scale = DIL_SCALE if h < HEADS else MLA_SCALE
                for q in range(TT):
                    cols = slice(0, P) if q == 0 else slice(P, 3 * P)
                    sums = {} if h < HEADS else {"accum_out": MX[:, h % 2, 2 + q:3 + q]}
                    act.activation(PR[:, h % 2, cols], SM[:, h % 2, cols], ACT.Exp, bias=MX[:, h % 2, q:q + 1],
                                   scale=scale, **sums).then_inc(p_exp, 1)

            def probs_out(h):
                act.wait_ge(p_turned, h + 1)
                if h >= 2:
                    act.wait_ge(pv_done, h - 1)
                act.activation(PT[:, h % 2], Y[:, h % 2, 0:3 * P], ACT.Copy).then_inc(pt_ready, 1)

            def mix_high(h):
                act.wait_ge(pv_done, h + 1)
                act.activation(XH[:, h, :], A[:, 1, h % 2, 0:TOK], ACT.Copy).then_inc(mix_hi, 1)

            for s in range(2 * HEADS + 2):
                if s < 2 * HEADS:
                    exps(s)
                if 1 <= s <= 2 * HEADS:
                    probs_out(s - 1)
                if s >= 2:
                    mix_high(s - 2)
                if 4 <= s < 8:
                    hi(c0 + s - 4)
            for c in range(c0 + 4, c0 + 32):
                hi(c)

            def feed_forward(layer):
                _, _, c0, b0 = PHASES[f"ple{layer}"]
                g0 = PHASES[f"gate{layer}"][2]
                for b in range(4):
                    hi(c0 + b)
                for b in range(4):
                    end(f"ple{layer}", b)
                    act.activation(PL[:, :, b * WB:(b + 1) * WB], A[:, (b0 + b) % 2], ACT.Copy).then_inc(ple_ready, 1)
                    hi(g0 + b)
                for g in range(8):
                    hi_turned(TG[f"ln1{layer}"] + g, XH[:, 2 * g:2 * g + 2, :])
                    if g >= 1 and g < 5:
                        hi(g0 + 3 + g)

                def gate_sigmoid(b):
                    end(f"gate{layer}", b)
                    done = (4 + 4) * layer * 1 + b
                    n_ = 4 * layer + b
                    if n_:
                        act.wait_ge(acc_free, PHASES[f"gate{layer}"][3] + b)
                    act.activation(GT[:, :, :, :].rearrange("p a t n -> p t a n"),
                                   A[:, (PHASES[f"gate{layer}"][3] + b) % 2].rearrange("p t (a n) -> p t a n", a=2),
                                   ACT.Sigmoid).then_inc(gate_act, 1)

                for b in range(1, 4):
                    for j in range(8):
                        hi(g0 + 8 * b + j)
                        if j == 4:
                            gate_sigmoid(b - 1)

                def silu(b, coef=0, i=None):
                    part, k = ("A", b) if b < FA else ("B", b - FA)
                    end(f"in{part}{layer}", k, coef, i)
                    done = (FA + FB) * layer + b
                    if done:
                        act.wait_ge(hid_ready, lin(done, coef, i))
                    parity = (PHASES[f"in{part}{layer}"][3] + k) % 2
                    act.activation(GT[:, 0], A[:, parity, :, 0:256], ACT.Silu).then_inc(silu_done, 1)

                def hidden_hi(b, coef=0, i=None):
                    k = b if b < FA else b - FA
                    if b == 0 and layer == 0:
                        act.wait_ge(tab_ready, 2)
                    hi_turned(TG[f"hid{layer}"] + b, HH[:, bass.ds(lin(2 * k, 2 * coef, i), 2), :], coef, i)

                for part, n_in, first in (("A", FA, 0), ("B", FB, FA)):
                    _, per, c0, _ = PHASES[f"in{part}{layer}"]

                    def inner(k, i):
                        for j in range(per):
                            hi(c0 + per * k + j, 2 * per, i)
                            if k > 0 and j == 4:
                                silu(first + k - 1, 2, i)
                            if k == 0 and j == 4 and part == "A":
                                gate_sigmoid(3)
                            if k > 0 and j == 7:
                                hidden_hi(first + k - 1, 2, i)
                    blocks(act, n_in, inner)
                    nb, per, c0, _ = PHASES[f"out{part}{layer}"]
                    for j in range(8):
                        hi(c0 + j)
                        if j == 4:
                            silu(first + n_in - 1)
                        if j == 7:
                            hidden_hi(first + n_in - 1)
                    rest = nb * per - 8
                    with act.Fori(0, rest // RING) as i:
                        for j in range(RING):
                            hi(c0 + 8 + j, RING, i)

            feed_forward(0)
            c0 = PHASES["glu"][2]
            for j in range(4):
                hi(c0 + j)
            hi_turned(TG["p1"], PH[:])

            def drive_out(seg):
                if seg >= 2:
                    act.wait_ge(y_done, seg - 1)
                    act.wait_ge(scan, 3 * (SEG * (seg - 1) - 1) + 1)
                for q in range(4):
                    for r in range(4):
                        n_ = 16 * seg + 4 * q + r
                        act.wait_ge(bu_done, n_ + 1)
                        dst = ST[seg % 2][:, :, :, 16 * q + r:16 * q + r + 13:4].rearrange("p t c a -> p a c t")
                        act.activation(dst, A[:, r // 2, r % 2].rearrange("p (a c t) -> p a c t", a=4, c=2),
                                       ACT.Copy).then_inc(bu_out, 1)

            def gelu(seg):
                part = HT[:, :, SEG * seg:SEG * (seg + 1)]
                act.wait_ge(y_added, 16 * (seg + 1))
                for a in range(16):
                    act.activation(part[:, a, :], part[:, a, :], ACT.Gelu_apprx_tanh).then_inc(z_done, 1)

            drive_out(0)
            drive_out(1)
            drive_out(2)
            gelu(0)
            drive_out(3)
            for seg in range(1, SEGS):
                gelu(seg)
            act.wait_ge(z_done, 64)
            for g in range(8):
                act.activation(XH[:, 2 * g:2 * g + 2, :], HT[:, 2 * g:2 * g + 2, :], ACT.Copy).then_inc(turn_hi, 1)

            b0 = PHASES["glu"][3]

            def glu_sigmoid(b, coef=0, i=None):
                end("glu", b, coef, i)
                act.wait_ge(acc_free, lin(b0 + b, coef, i))
                act.activation(GT[:, 0], A[:, (b0 + b) % 2, :, 256:512], ACT.Sigmoid).then_inc(gate_act, 1)

            def glu(k, i):
                for j in range(8):
                    if not (k == 0 and j < 4):
                        hi(c0 + 8 * k + j, 16, i)
                    if k > 0 and j == 4:
                        glu_sigmoid(k - 1, 2, i)
            blocks(act, 8, glu)
            glu_sigmoid(7)
            HGO = 8
            feed_forward(1)

        @block.vector
        def _(dve):
            step = [0]

            def link(ins):
                ins.then_inc(v_step, 1)
                step[0] += 1
                dve.wait_ge(v_step, step[0])

            def lo(c, coef=0, i=None, width=WB):
                s = c % RING
                dve.wait_ge(hi_ready, lin(c + 1, coef, i))
                if c >= RING:
                    dve.wait_ge(w_used, lin(c - RING + 1, coef, i))
                dve.tensor_tensor(WL[:, s, :, 0:width], RAW[:, s, :, 0:width], WH[:, s, :, 0:width].bitcast(F32),
                                  ALU.subtract).then_inc(lo_ready, 1)

            hg = [0]

            def lo_turned(g, n_hi, hi_ap, lo_ap, coef=0, i=None):
                dve.wait_ge(turn_hi, lin(n_hi + 1, coef, i))
                dve.tensor_tensor(lo_ap, TP[:, g % 2], hi_ap.bitcast(F32), ALU.subtract).then_inc(turned, 1)

            def whole_turned(g, dst, src=None):
                dve.wait_ge(turn_done, g + 1)
                dve.tensor_copy(dst, TP[:, g % 2] if src is None else src).then_inc(turned, 1)

            def end(name, b, coef=0, i=None):
                _, per, c0, _ = PHASES[name]
                dve.wait_ge(w_used, lin(c0 + per * (b + 1), per * coef, i))

            def rsqrt(v, y, tmp, n_):
                half = SI[:, 0:n_]
                link(dve.tensor_scalar(half, v.bitcast(I32), 1, None, ALU.logical_shift_right))
                link(dve.tensor_scalar(y.bitcast(I32), half, -1.0, float(0x5F3759DF), ALU.mult, ALU.add))
                for _ in range(3):
                    link(dve.scalar_tensor_tensor(tmp, y, -0.5, y, ALU.mult, ALU.mult))
                    link(dve.tensor_tensor(tmp, tmp, v, ALU.mult))
                    link(dve.scalar_tensor_tensor(y, tmp, 1.5, y, ALU.add, ALU.mult))

            for g in range(8):
                lo_turned(TG["x"] + g, HG["x"] + g, XH[:, 2 * g:2 * g + 2, :], XL[:, 2 * g:2 * g + 2, :])
                if g < RING:
                    lo(g)
            lo_turned(TG["p0"], HG["p0"], PH[:], PLO[:])

            def angles():
                dve.wait_ge(const_in, 8 * 16)
                two_pi = 2 * np.pi
                c1 = 6.28125
                c2 = float(np.float32(np.round((two_pi - c1) * 2 ** 17) / 2 ** 17))
                c3 = float(np.round((two_pi - c1 - c2) * 2 ** 25) / 2 ** 25)
                c4 = float(np.float32(two_pi - c1 - c2 - c3))
                link(dve.tensor_copy(SC[:, 8:10], PI[:]))
                for q in range(TT):
                    link(dve.tensor_scalar(AT[:, 0, q], AT[:, 3, q], SC[:, 8 + q:9 + q], None, ALU.mult))
                r, n_ = AT[:, 0], AT[:, 1]
                link(dve.tensor_scalar(n_, r, 1.0 / two_pi, ROUND, ALU.mult, ALU.add))
                link(dve.tensor_scalar(n_, n_, -ROUND, None, ALU.add))
                for c in (c1, c2, c3, c4):
                    link(dve.scalar_tensor_tensor(r, n_, -c, r, ALU.mult, ALU.add))
                dve.tensor_scalar(r, r, float(np.float32(3.1415925)), -float(np.float32(3.1415925)), ALU.min,
                                  ALU.max).then_inc(trig, 1)

            def cosine():
                dve.wait_ge(trig, 3)
                link(dve.tensor_tensor(CS[:, 0], CS[:, 0], CS[:, 0], ALU.mult))
                link(dve.tensor_scalar(CS[:, 0], CS[:, 0], -2.0, 1.0, ALU.mult, ALU.add))

            def rotate(src, dst, heads):
                for out_half, (first, second, op) in enumerate([(0, 1, ALU.subtract), (1, 0, ALU.add)]):
                    cos = CS[:, 0].unsqueeze(2).broadcast_to([P, TT, heads, HALF])
                    sin = CS[:, 1].unsqueeze(2).broadcast_to([P, TT, heads, HALF])
                    tmp = GTf[:, 512:512 + TT * heads * HALF].rearrange("p (t h n) -> p t h n", t=TT, h=heads)
                    link(dve.tensor_tensor(tmp, src[:, :, :, second], sin, ALU.mult))
                    link(dve.tensor_tensor(dst[:, :, :, first], src[:, :, :, first], cos, ALU.mult))
                    last = dve.tensor_tensor(dst[:, :, :, first], dst[:, :, :, first], tmp, op)
                    if out_half == 0:
                        link(last)
                return last

            def latent(b):
                dve.wait_ge(sq_sum, 2 * b + 2)
                v, y, tmp = SC[:, 4:6], SC[:, 6:8], SC[:, 10:12]
                link(dve.tensor_scalar(v, SC[:, 2 * b:2 * b + 2], 1.0 / LAT, 1e-6, ALU.mult, ALU.add))
                rsqrt(v, y, tmp, 2)
                link(dve.scalar_tensor_tensor(STG[:, b % 2, 0], A[:, b % 2, 0], y[:, 0:1], NG[:, b * LAT:(b + 1) * LAT],
                                              ALU.mult, ALU.mult))
                link(dve.scalar_tensor_tensor(STG[:, b % 2, 1], A[:, b % 2, 1], y[:, 1:2], NG[:, b * LAT:(b + 1) * LAT],
                                              ALU.mult, ALU.mult))
                dve.nop().then_inc(staged, 1)
                dve.nop().then_inc(acc_free, 1)

            for b in range(8):
                for j in range(8):
                    if 8 * b + j >= RING:
                        lo(8 * b + j)
                    if j == 0 and b == 1:
                        angles()
                    if j == 0 and b == 6:
                        cosine()
                    if j == 5 and b in (1, 2):
                        latent(b - 1)
                    if j == 5 and 3 <= b <= 6:
                        dve.wait_ge(staged, b)
                        dve.nop().then_inc(acc_free, 1)
                    if j == 7 and 1 <= b <= 6:
                        for g in range(2):
                            if b <= 2:
                                n_ = 2 * (b - 1) + g
                                lo_turned(TG["lat"] + n_, HG["lat"] + n_, LH[:, 2 * n_:2 * n_ + 2, :],
                                          LL[:, 2 * n_:2 * n_ + 2, :])
                            else:
                                n_ = 2 * (b - 3) + g
                                whole_turned(TG["qk"] + n_, QK[:, 2 * n_:2 * n_ + 2, :])
            c0 = PHASES["kpe"][2]
            for j in range(8):
                lo(c0 + j, width=ROPE)
            QB = PHASES["qb"]

            def up_turned(m):
                if m == 0:
                    g = TG["kpe"]
                    whole_turned(g, KP[:], TP[:, g % 2, 0])
                else:
                    dst, h = [(QN, 0), (QN, 4), (QP, 0), (KN, 0), (KN, 4)][m - 1]
                    g = [TG["qn"], TG["qn"] + 2, TG["qp"], TG["kn"], TG["kn"] + 2][m - 1]
                    for n_ in range(2):
                        whole_turned(g + n_, dst[:, h + 2 * n_:h + 2 * n_ + 2, :])

            for b in range(7):
                lo(QB[2] + 2 * b)
                lo(QB[2] + 2 * b + 1)
                if b == 0:
                    end("kpe", 0)
                    src = A[:, PHASES["kpe"][3] % 2, :, 0:ROPE].rearrange("p t (h c n) -> p t h c n", h=1, c=2)
                    dve.wait_ge(turn_done, TG["kpe"])
                    dst = STG[:, 0, :, 0:ROPE].rearrange("p t (h c n) -> p t h c n", h=1, c=2)
                    link(rotate(src, dst, 1))
                    link(dve.tensor_copy(STG[:, 0, :, ROPE:2 * ROPE], STG[:, 0, :, 0:ROPE]))
                    dve.nop().then_inc(staged, 1)
                    dve.nop().then_inc(acc_free, 1)
                if b in (1, 2, 4, 5):
                    dve.wait_ge(staged, 7 + b)
                    dve.nop().then_inc(acc_free, 1)
                if b == 3:
                    end("qb", 2)
                    dve.wait_ge(turn_done, TG["qn"] + 2)
                    src = A[:, (QB[3] + 2) % 2].rearrange("p t (h c n) -> p t h c n", h=HEADS, c=2)
                    dst = STG[:, 1].rearrange("p t (h c n) -> p t h c n", h=HEADS, c=2)
                    link(rotate(src, dst, HEADS))
                    dve.nop().then_inc(staged, 1)
                    dve.nop().then_inc(acc_free, 1)
                if b >= 2:
                    up_turned(b - 2)
            up_turned(5)

            c0 = PHASES["wout"][2]

            def mask_and_max(h):
                dve.wait_ge(s_done, h + 1)
                if h >= 2:
                    dve.wait_ge(p_exp, 2 * (h - 1))
                scale, slope, m = (DIL_SCALE, SLOPES[h] / DIL_SCALE, DM) if h < HEADS else (MLA_SCALE, 1.0, CM)
                dve.scalar_tensor_tensor(SM[:, h % 2], m[:], slope, A[:, 0, h % 2, 0:3 * P], ALU.mult,
                                         ALU.add).then_inc(s_masked, 1)
                dve.wait_ge(s_masked, h + 1)
                if h >= 1:
                    dve.wait_ge(nmax, h)
                dve.tensor_reduce(SC[:, 12:13], SM[:, h % 2, 0:P], AX_X, ALU.max)
                link(dve.tensor_reduce(SC[:, 13:14], SM[:, h % 2, P:3 * P], AX_X, ALU.max))
                dve.tensor_scalar(MX[:, h % 2, 0:2], SC[:, 12:14], -scale, None, ALU.mult).then_inc(nmax, 1)

            def norm_probs(h):
                dve.wait_ge(p_exp, 2 * h + 2)
                if h >= 1:
                    dve.wait_ge(p_ready, h)
                parts = [slice(0, P), slice(P, 3 * P)]
                if h < HEADS:
                    for q in range(TT):
                        link(dve.scalar_tensor_tensor(PR[:, h % 2, parts[q]], PR[:, h % 2, parts[q]], 1.0,
                                                      NM[:, parts[q]], ALU.mult, ALU.mult,
                                                      accum_out=MX[:, h % 2, 2 + q:3 + q]))
                link(dve.reciprocal(SC[:, 14:16], MX[:, h % 2, 2:4]))
                link(dve.tensor_scalar(PR[:, h % 2, parts[0]], PR[:, h % 2, parts[0]], SC[:, 14:15], None, ALU.mult))
                dve.tensor_scalar(PR[:, h % 2, parts[1]], PR[:, h % 2, parts[1]], SC[:, 15:16], None,
                                  ALU.mult).then_inc(p_ready, 1)

            def mix_low(h):
                dve.wait_ge(mix_hi, h + 1)
                dve.tensor_tensor(XL[:, h, :], A[:, 1, h % 2, 0:TOK], XH[:, h, :].bitcast(F32),
                                  ALU.subtract).then_inc(mix_ready, 1)

            for s in range(2 * HEADS + 3):
                if s < 2 * HEADS:
                    mask_and_max(s)
                if 1 <= s <= 2 * HEADS:
                    norm_probs(s - 1)
                if s >= 3:
                    mix_low(s - 3)
                if 4 <= s < 8:
                    lo(c0 + s - 4)

            def add_stats(b, q, width, n_):
                return dve.bn_stats(BS[:, q, n_, :], RES[:, q, width * b:width * (b + 1)])

            def wout_end(b):
                end("wout", b)
                cols = slice(WB * b, WB * (b + 1))
                dve.scalar_tensor_tensor(RES[:, :, cols], RES[:, :, cols], ALPHA, A[:, (PHASES["wout"][3] + b) % 2],
                                         ALU.mult, ALU.add).then_inc(acc_free, 1)
                dve.wait_ge(acc_free, PHASES["wout"][3] + b + 1)
                for q in range(TT):
                    last = add_stats(b, q, WB, b)
                last.then_inc(v_step, 1)
                step[0] += 1

            for b in range(4):
                for j in range(8):
                    if 8 * b + j >= 4:
                        lo(c0 + 8 * b + j)
                    if b and j == 4:
                        wout_end(b - 1)

            def norm_scalars(n_):
                dve.wait_ge(v_step, step[0])
                for q in range(TT):
                    last = dve.bn_aggr(MV[:, q, :], BS[:, q, 0:n_, :].rearrange("p a b -> p (a b)"))
                link(last)
                link(dve.tensor_scalar(SC[:, 18:20], MV[:, :, 1], 1e-5, None, ALU.add))
                rsqrt(SC[:, 18:20], SC[:, 16:18], SC[:, 20:22], 2)

            def norm_quarter(n_, q4):
                dve.wait_ge(gb_in, 32 * (n_ + 1))
                cols = slice(WB * q4, WB * (q4 + 1))
                for q in range(TT):
                    link(dve.scalar_tensor_tensor(RES[:, q, cols], RES[:, q, cols], MV[:, q, 0:1], GB[:, 0, cols],
                                                  ALU.subtract, ALU.mult))
                    last = dve.scalar_tensor_tensor(RES[:, q, cols], RES[:, q, cols], SC[:, 16 + q:17 + q],
                                                    GB[:, 1, cols], ALU.mult, ALU.add)
                    if q == 0:
                        last.then_inc(v_step, 1)
                        step[0] += 1
                    else:
                        last.then_inc(ln_quarter, 1)

            def feed_forward(layer):
                ln1, ln2 = 2 * layer, 2 * layer + 1
                c_ple, b_ple = PHASES[f"ple{layer}"][2:]
                g0, b0 = PHASES[f"gate{layer}"][2:]
                G = TG[f"ln1{layer}"]

                def split(g):
                    lo_turned(G + g, HG[f"ln1{layer}"] + g + (8 if layer else 0), XH[:, 2 * g:2 * g + 2, :],
                              XL[:, 2 * g:2 * g + 2, :])

                norm_quarter(ln1, 0)
                norm_quarter(ln1, 1)
                for q4 in range(4):
                    lo(g0 + 2 * q4)
                    split(2 * q4)
                    split(2 * q4 + 1)
                    lo(g0 + 2 * q4 + 1)
                    if q4 < 2:
                        norm_quarter(ln1, q4 + 2)

                def gate_end(b):
                    cols = slice(WB * b, WB * (b + 1))
                    n_ = 4 * layer + b + 1 + (8 if layer else 0)
                    dve.wait_ge(gate_act, n_)
                    dve.wait_ge(ple_ready, 4 * layer + 4)
                    g = GT[:, :, :, :].rearrange("p a t n -> p t a n")
                    pl = PL[:, :, cols].rearrange("p t (a n) -> p t a n", a=2)
                    link(dve.tensor_tensor(pl, pl, g, ALU.mult))
                    dve.scalar_tensor_tensor(RES[:, :, cols], RES[:, :, cols], ALPHA, PL[:, :, cols], ALU.mult,
                                             ALU.add).then_inc(acc_free, 1)

                for b in range(1, 4):
                    for j in range(8):
                        lo(g0 + 8 * b + j)
                        if j == 4:
                            gate_end(b - 1)

                def hidden(b, coef=0, i=None):
                    part, k = ("A", b) if b < FA else ("B", b - FA)
                    bb = PHASES[f"in{part}{layer}"][3] + k
                    done = (FA + FB) * layer + b
                    dve.wait_ge(silu_done, lin(done + 1, coef, i))
                    dve.wait_ge(turn_done, lin(TG[f"hid{layer}"] + b, coef, i))
                    dve.tensor_tensor(GT[:, 1], A[:, bb % 2, :, 256:512], GT[:, 0],
                                      ALU.mult).then_inc(hid_ready, 1)

                def hidden_free(b, coef=0, i=None):
                    part, k = ("A", b) if b < FA else ("B", b - FA)
                    done = (FA + FB) * layer + b
                    dve.wait_ge(hid_ready, lin(done + 1, coef, i))
                    dve.nop().then_inc(acc_free, 1)

                def hidden_lo(b, coef=0, i=None):
                    k = b if b < FA else b - FA
                    rows = bass.ds(lin(2 * k, 2 * coef, i), 2)
                    lo_turned(TG[f"hid{layer}"] + b, HG[f"hid{layer}"] + b + (8 if layer else 0), HH[:, rows, :],
                              HL[:, rows, :], coef, i)

                def out_end(part, b, stats):
                    bb = PHASES[f"out{part}{layer}"][3] + b
                    end(f"out{part}{layer}", b)
                    cols = slice(WB * b, WB * (b + 1))
                    dve.tensor_tensor(RES[:, :, cols], A[:, bb % 2], RES[:, :, cols], ALU.add).then_inc(acc_free, 1)
                    if stats:
                        dve.wait_ge(acc_free, bb + 1)
                        for q in range(TT):
                            last = add_stats(b, q, WB, b)
                        last.then_inc(v_step, 1)
                        step[0] += 1

                def transition():
                    dve.wait_ge(ab_turned, 1)
                    dve.tensor_copy(AB[:, 0:4:3, :], Y[:, 0, 0:PAIRS].unsqueeze(1).broadcast_to([P, 2, PAIRS])).then_inc(ab_ready, 1)
                    dve.tensor_copy(AB[:, 2, :], Y[:, 0, PAIRS:2 * PAIRS]).then_inc(ab_ready, 1)
                    dve.tensor_scalar(AB[:, 1, :], Y[:, 0, PAIRS:2 * PAIRS], -1.0, None, ALU.mult).then_inc(ab_ready, 1)
                    dve.wait_ge(ab_ready, 3)

                for part, n_in, first in (("A", FA, 0), ("B", FB, FA)):
                    _, per, c0, _ = PHASES[f"in{part}{layer}"]

                    def inner(k, i):
                        for j in range(per):
                            lo(c0 + per * k + j, 2 * per, i)
                            if k == 0 and j == 4:
                                if part == "A":
                                    gate_end(3)
                                    if layer == 0:
                                        transition()
                                else:
                                    out_end("A", 3, False)
                            if k > 0 and j == 4:
                                hidden(first + k - 1, 2, i)
                            if k > 0 and j == 5:
                                hidden_free(first + k - 1, 2, i)
                            if k > 0 and j == 7:
                                hidden_lo(first + k - 1, 2, i)
                    blocks(dve, n_in, inner)
                    nb, per, c0, _ = PHASES[f"out{part}{layer}"]
                    for b in range(nb):
                        for j in range(per):
                            lo(c0 + per * b + j)
                            if b == 0 and j == 4:
                                hidden(first + n_in - 1)
                            if b == 0 and j == 5:
                                hidden_free(first + n_in - 1)
                            if b == 0 and j == 7:
                                hidden_lo(first + n_in - 1)
                            if b and j == 4:
                                out_end(part, b - 1, part == "B")
                nxt = PHASES["glu"][2] if layer == 0 else None
                if nxt is not None:
                    for j in range(4):
                        lo(nxt + j)
                out_end("B", 3, True)
                norm_scalars(4)

            def start_ple(layer):
                for b in range(4):
                    lo(PHASES[f"ple{layer}"][2] + b)

            start_ple(0)
            wout_end(3)
            norm_scalars(4)
            feed_forward(0)

            norm_quarter(1, 0)
            for q4 in range(4):
                if q4 < 3:
                    norm_quarter(1, q4 + 1)
                for g in (2 * q4, 2 * q4 + 1):
                    whole_turned(TG["ln20"] + g, HT[:, 2 * g:2 * g + 2, :])
            lo_turned(TG["p1"], HG["p1"], PH[:], PLO[:])
            abar = AB[:, :, :].rearrange("p (o c) n -> p o c n", o=2)
            prod = GTf[:, 0:4 * PAIRS].rearrange("p (o c n) -> p o c n", o=2, c=2)
            part = GTf[:, 512:512 + 2 * PAIRS].rearrange("p (c n) -> p c n", c=2)

            def scan_step(before, now, count, coef=0, i=None):
                x = before.broadcast_to([P, 2, 2, PAIRS])
                dve.tensor_tensor(prod, abar, x, ALU.mult).then_inc(scan, 1)
                dve.wait_ge(scan, lin(count + 1, coef, i))
                dve.tensor_tensor(part, prod[:, :, 0, :], prod[:, :, 1, :], ALU.add).then_inc(scan, 1)
                dve.wait_ge(scan, lin(count + 2, coef, i))
                dve.tensor_tensor(now, now, part, ALU.add).then_inc(scan, 1)
                dve.wait_ge(scan, lin(count + 3, coef, i))

            def add_skip(seg):
                dve.wait_ge(y_done, seg + 1)
                for tile in range(KT):
                    h = HT[:, tile, SEG * seg:SEG * (seg + 1)]
                    y = Y[:, tile // 8, (tile % 8) * SEG:(tile % 8 + 1) * SEG]
                    dve.scalar_tensor_tensor(h, h, SD[:, tile:tile + 1], y, ALU.mult, ALU.add).then_inc(y_added, 1)

            for seg in range(SEGS):
                s = ST[seg % 2]
                dve.wait_ge(bu_out, 16 * (seg + 1))
                count = 3 * (SEG * seg - 1)
                if seg:
                    scan_step(ST[(seg - 1) % 2][:, SEG - 1:SEG], s[:, 0], count)
                count += 3
                per = 9
                with dve.Fori(0, (SEG - 1) // per) as i:
                    for k in range(per):
                        now = s[:, bass.ds(lin(k + 1, per, i), 1)].rearrange("p a c n -> p (a c) n")
                        scan_step(s[:, bass.ds(lin(k, per, i), 1)], now, count + 3 * k, 3 * per, i)
                if seg:
                    add_skip(seg - 1)
            add_skip(SEGS - 1)
            for g in range(8):
                dve.wait_ge(turn_hi, HG["p1"] + 1 + g + 1)
                dve.tensor_tensor(XL[:, 2 * g:2 * g + 2, :], HT[:, 2 * g:2 * g + 2, :],
                                  XH[:, 2 * g:2 * g + 2, :].bitcast(F32), ALU.subtract).then_inc(z_done, 2)

            c0, b0 = PHASES["glu"][2:]

            def glu_end(b, coef=0, i=None):
                dve.wait_ge(gate_act, lin(4 + b + 1, coef, i))
                dve.tensor_tensor(GT[:, 1], A[:, (b0 + b) % 2, :, 0:256], GT[:, 0], ALU.mult).then_inc(glu_step, 1)
                dve.wait_ge(glu_step, lin(2 * b + 1, 2 * coef, i))
                cols = RES[:, :, bass.ds(lin(256 * b, 256 * coef, i), 256)]
                dve.scalar_tensor_tensor(cols, cols, ALPHA, GT[:, 1], ALU.mult, ALU.add).then_inc(acc_free, 1)
                dve.wait_ge(acc_free, lin(b0 + b + 1, coef, i))
                for q in range(TT):
                    last = dve.bn_stats(BS[:, q, bass.ds(lin(b, coef, i), 1), :].rearrange("p a b -> p (a b)"),
                                        RES[:, q, bass.ds(lin(256 * b, 256 * coef, i), 256)])
                last.then_inc(glu_step, 1)

            def glu(k, i):
                for j in range(8):
                    if not (k == 0 and j < 4):
                        lo(c0 + 8 * k + j, 16, i)
                    if k > 0 and j == 4:
                        glu_end(k - 1, 2, i)
            blocks(dve, 8, glu)
            start_ple(1)
            glu_end(7)
            dve.wait_ge(glu_step, 16)
            norm_scalars(8)
            feed_forward(1)
            for q4 in range(4):
                norm_quarter(3, q4)

        @block.gpsimd
        def _(pool):
            count = [0]

            def link(ins):
                ins.then_inc(tab, 1)
                count[0] += 1
                pool.wait_ge(tab, count[0])

            def load_gb(n_):
                layer, which = n_ // 2, n_ % 2 + 1
                for k, name in enumerate((f"ln{which}_g", f"ln{which}_b")):
                    pool.dma_start(GB[:, k, :], t[name][layer:layer + 1, :].rearrange("a n -> (a n)").partition_broadcast(P)).then_inc(gb_in, 16)

            pool.wait_ge(w_used, PHASES["wout"][2] + 8)
            load_gb(0)
            for dst, name in [(S5[:, 2, :], "s5_are"), (S5[:, 3, :], "s5_aim"), (S5[:, 4, 0:2], "s5_ldt")]:
                pool.dma_start(dst, t[name]).then_inc(late_in, 16)
            for dst, name in [(BR[:], "s5_bre"), (BI[:], "s5_bim")]:
                pool.dma_start(dst, t[name]).then_inc(late_in, 16)
            pool.wait_ge(late_in, 5 * 16)
            ABR, ABI, ARE, AIM, LDT, DT, E, S, C, T0, T1, T2, T3 = (S5[:, k, :] for k in range(13))
            LDT2 = S5[:, 13, :]

            def tt(o, a, b, op):
                link(pool.tensor_tensor(o, a, b, op))

            def ts(o, a, s1, s2, op0, op1=None):
                if s2 is None:
                    link(pool.tensor_scalar(o, a, s1, None, op0))
                else:
                    link(pool.tensor_scalar(o, a, s1, s2, op0, op1))

            def exp(o, x):
                ln2_hi = 0.693145751953125
                ln2_lo = float(np.float32(np.log(2.0) - ln2_hi))
                ts(T0, x, -87.0, 88.0, ALU.max, ALU.min)
                ts(T1, T0, float(1 / np.log(2.0)), ROUND, ALU.mult, ALU.add)
                ts(T1, T1, -ROUND, None, ALU.add)
                ts(T2, T1, -ln2_hi, None, ALU.mult)
                tt(T0, T0, T2, ALU.add)
                ts(T2, T1, -ln2_lo, None, ALU.mult)
                tt(T0, T0, T2, ALU.add)
                ts(T2, T0, 1 / 5040.0, 1 / 720.0, ALU.mult, ALU.add)
                for c in (1 / 120.0, 1 / 24.0, 1 / 6.0, 0.5, 1.0, 1.0):
                    tt(T2, T2, T0, ALU.mult)
                    ts(T2, T2, c, None, ALU.add)
                ts(T1.bitcast(I32), T1, 127.0, float(2 ** 23), ALU.add, ALU.mult)
                tt(o, T2, T1, ALU.mult)

            def sin_cos(x):
                two_pi = 2 * np.pi
                c1 = 6.28125
                c2 = float(np.float32(np.round((two_pi - c1) * 2 ** 17) / 2 ** 17))
                c3 = float(np.round((two_pi - c1 - c2) * 2 ** 25) / 2 ** 25)
                c4 = float(np.float32(two_pi - c1 - c2 - c3))
                ts(T1, x, float(1 / two_pi), ROUND, ALU.mult, ALU.add)
                ts(T1, T1, -ROUND, None, ALU.add)
                ts(T2, T1, -c1, None, ALU.mult)
                tt(T0, x, T2, ALU.add)
                for c in (c2, c3, c4):
                    ts(T2, T1, -c, None, ALU.mult)
                    tt(T0, T0, T2, ALU.add)
                ts(T0, T0, 3.2, -3.2, ALU.min, ALU.max)
                ts(T0, T0, 0.25, None, ALU.mult)
                tt(T1, T0, T0, ALU.mult)
                ts(T2, T1, 1 / 362880.0, -1 / 5040.0, ALU.mult, ALU.add)
                for c in (1 / 120.0, -1 / 6.0, 1.0):
                    tt(T2, T2, T1, ALU.mult)
                    ts(T2, T2, c, None, ALU.add)
                tt(S, T2, T0, ALU.mult)
                ts(T2, T1, 1 / 40320.0, -1 / 720.0, ALU.mult, ALU.add)
                for c in (1 / 24.0, -0.5, 1.0):
                    tt(T2, T2, T1, ALU.mult)
                    ts(T2, T2, c, None, ALU.add)
                tt(T3, S, T2, ALU.mult)
                tt(T1, S, S, ALU.mult)
                ts(T2, T1, -2.0, 1.0, ALU.mult, ALU.add)
                ts(T3, T3, 2.0, None, ALU.mult)
                tt(S, T3, T2, ALU.mult)
                ts(S, S, 2.0, None, ALU.mult)
                tt(T1, T3, T3, ALU.mult)
                ts(C, T1, -2.0, 1.0, ALU.mult, ALU.add)

            link(pool.tensor_copy(LDT2.rearrange("r (s n) -> r s n", s=2),
                                  S5[:, 4, 0:2].unsqueeze(2).broadcast_to([64, 2, 64])))
            exp(DT, LDT2)
            tt(T3, ARE, DT, ALU.mult)
            exp(E, T3)
            tt(E + 0 if False else E, E, E, ALU.bypass) if False else None
            tt(LDT2, AIM, DT, ALU.mult)
            sin_cos(LDT2)
            tt(ABR, E, C, ALU.mult)
            tt(ABI, E, S, ALU.mult)
            tt(T0, ARE, ARE, ALU.mult)
            tt(T1, AIM, AIM, ALU.mult)
            tt(T0, T0, T1, ALU.add)
            link(pool.tensor_copy(T1, T0.bitcast(I32)))
            ts(T2.bitcast(I32), T1, -1.0, float(0x7EF311C3), ALU.mult, ALU.add)
            for _ in range(4):
                tt(T1, T0, T2, ALU.mult)
                ts(T1, T1, -1.0, 2.0, ALU.mult, ALU.add)
                tt(T2, T2, T1, ALU.mult)
            ts(T3, ABR, -1.0, None, ALU.add)
            tt(T0, T3, ARE, ALU.mult)
            tt(T1, ABI, AIM, ALU.mult)
            tt(T0, T0, T1, ALU.add)
            tt(DT, T0, T2, ALU.mult)
            tt(T0, ABI, ARE, ALU.mult)
            tt(T1, T3, AIM, ALU.mult)
            tt(T0, T0, T1, ALU.subtract)
            link(pool.tensor_tensor(E, T0, T2, ALU.mult))
            pool.sem_inc(tab_ready, 1)
            pool.dma_start(coef_dram[0], DT).then_inc(coef_out, 16)
            pool.dma_start(coef_dram[1], E).then_inc(coef_out, 16)
            pool.wait_ge(coef_out, 32)
            for n_, dst in enumerate((CR, CI)):
                for r in range(4):
                    src = coef_dram[n_].rearrange("(k r) n -> r k n", r=4)[r:r + 1].rearrange("r k n -> (r k) n")
                    pool.dma_start(dst[32 * r:32 * r + 32], src.partition_broadcast(32)).then_inc(coef_in, 16)
            pool.wait_ge(coef_in, 8 * 16)
            link(pool.tensor_tensor(TB[:], CR[:], BR[:], ALU.mult))
            link(pool.tensor_tensor(BB[:, :, 0, :], CI[:], BI[:], ALU.mult))
            link(pool.tensor_tensor(BB[:, :, 0, :], TB[:], BB[:, :, 0, :], ALU.subtract))
            link(pool.tensor_tensor(TB[:], CR[:], BI[:], ALU.mult))
            link(pool.tensor_tensor(BB[:, :, 1, :], CI[:], BR[:], ALU.mult))
            link(pool.tensor_tensor(BB[:, :, 1, :], TB[:], BB[:, :, 1, :], ALU.add))
            pool.sem_inc(tab_ready, 1)

            pool.wait_ge(ln_quarter, 4)
            load_gb(1)
            pool.wait_ge(ln_quarter, 8)
            pool.dma_start(CC[:], t["s5_c"]).then_inc(c_in, 16)
            pool.wait_ge(w_used, PHASES["glu"][2])
            pool.dma_start(PK[:], t["p"][1].rearrange("(t p) n -> p t n", p=P)).then_inc(p1_in, 16)
            pool.wait_ge(c_in, 16)
            pool.tensor_scalar(CC[:, :, 1, :], CC[:, :, 1, :], -1.0, None, ALU.mult).then_inc(c_ready, 1)
            pool.wait_ge(y_done, SEGS)
            load_gb(2)
            pool.wait_ge(ln_quarter, 12)
            load_gb(3)
            ov = out.rearrange("(t p) n -> p t n", p=P)
            for q4 in range(4):
                pool.wait_ge(ln_quarter, 12 + q4 + 1)
                cols = slice(WB * q4, WB * (q4 + 1))
                pool.dma_start(ov[:, :, cols], RES[:, :, cols]).then_inc(stored, 16)
            pool.wait_ge(stored, 64)


def chunks(w, cols):
    parts = []
    for ranges in cols:
        b = np.concatenate([w[:, a:e] for a, e in ranges], axis=1)
        r, n = b.shape
        parts.append(b.reshape(r // 256, 2, 128, n).transpose(0, 2, 1, 3).reshape(r // 256, 128, 2 * n))
    return np.ascontiguousarray(np.concatenate(parts, axis=0))


def kernel(**inputs):
    import concourse.bacc as bacc
    from concourse.bass_utils import run_bass_kernel_spmd as run

    a = {k: np.asarray(v) for k, v in inputs.items()}
    arr = {"x": a["x"][0], "p": a["p"][:, 0]}
    w = a["attn_w_in"][0]
    lat, qd, kd, vd = 0, 2 * LAT + ROPE, 2 * LAT + ROPE + 1024, 2 * LAT + ROPE + 2048
    starts = [lat, LAT, qd, qd + WB, kd, kd + WB, vd, vd + WB]
    arr["w_in"] = chunks(w, [[(s, s + WB)] for s in starts])
    arr["w_kpe"] = chunks(w, [[(2 * LAT, 2 * LAT + ROPE)]])
    wq = a["mla_w_q_b"][0].reshape(LAT, HEADS, HD + ROPE)
    wq = np.concatenate([wq[:, :, :HD].reshape(LAT, -1), wq[:, :, HD:].reshape(LAT, -1)], axis=1)
    arr["w_qb"] = chunks(wq, [[(WB * b, WB * (b + 1))] for b in range(3)])
    wk = a["mla_w_kv_b"][0].reshape(LAT, HEADS, 2 * HD)
    wk = np.concatenate([wk[:, :, :HD].reshape(LAT, -1), wk[:, :, HD:].reshape(LAT, -1)], axis=1)
    arr["w_kvb"] = chunks(wk, [[(WB * b, WB * (b + 1))] for b in range(4)])
    wo = a["attn_w_out"][0]
    arr["w_out"] = chunks(np.concatenate([wo[1024:], wo[:1024]], axis=0), [[(WB * b, WB * (b + 1))] for b in range(4)])
    arr["w_glu"] = chunks(a["s5_w_glu"][0], [[(256 * b, 256 * (b + 1)), (D + 256 * b, D + 256 * (b + 1))] for b in range(8)])
    four = [[(WB * b, WB * (b + 1))] for b in range(4)]
    for l in range(LAYERS):
        arr[f"w_ple{l}"] = chunks(a["ple_w"][l], four)
        arr[f"w_gate{l}"] = chunks(a["ple_gate_w"][l], four)
        for part, first, n in (("A", 0, FA), ("B", FA, FB)):
            arr[f"w_in{part}{l}"] = chunks(a["ffn_w_in"][l], [[(256 * b, 256 * (b + 1)), (FFN + 256 * b, FFN + 256 * (b + 1))]
                                                              for b in range(first, first + n)])
            arr[f"w_out{part}{l}"] = chunks(a["ffn_w_out"][l][256 * first:256 * (first + n)], four)
    for k in ("ln1_g", "ln1_b", "ln2_g", "ln2_b"):
        arr[k] = a[k]
    arr["norm_gain"] = np.concatenate([a["mla_q_norm"][0], a["mla_kv_norm"][0]])
    arr["pos"] = np.ascontiguousarray(a["positions"][0].reshape(TT, P).T)
    arr["s5_d"] = np.ascontiguousarray(a["s5_d"][0].reshape(KT, P).T)
    arr["s5_are"] = a["s5_a_re"][0].reshape(PAIRS, P)
    arr["s5_aim"] = a["s5_a_im"][0].reshape(PAIRS, P)
    arr["s5_ldt"] = a["s5_log_dt"][0].reshape(PAIRS, 2)
    for k in ("re", "im"):
        b = a[f"s5_b_{k}"][0].reshape(KT, 4, 2, 64, GROUP)
        z = np.zeros((4, 2, GROUP, KT, 2, 64), b.dtype)
        for g in range(2):
            z[:, g, :, :, g, :] = b[:, :, g].transpose(1, 3, 0, 2)
        arr[f"s5_b{k}"] = z.reshape(P, KT, P)
    c = np.zeros((2, 64, PAIRS, 2, 2, GROUP), a["s5_c_re"].dtype)
    for n, k in enumerate(("re", "im")):
        ck = a[f"s5_c_{k}"][0].reshape(PAIRS, 2, GROUP, 64)
        for g in range(2):
            c[g, :, :, n, g, :] = ck[:, g].transpose(2, 0, 1)
    arr["s5_c"] = c.reshape(P, PAIRS, 2, 2 * GROUP)
    arr["ident"] = np.eye(P, dtype=np.float32)
    arr["inv_freq"] = np.float32(10000.0) ** (-np.arange(HALF, dtype=np.float32) / np.float32(HALF))
    q = np.concatenate([np.arange(P)[:, None] + np.zeros((1, P), int), P + np.arange(P)[:, None] + np.zeros((1, 2 * P), int)], axis=1)
    key = np.concatenate([np.arange(P), np.arange(2 * P)])[None, :]
    dist = q - key
    n = ((dist >= 0) & (dist <= 128)) * 1.0 + ((dist >= 0) & (dist % 4 == 0)) + ((dist >= 0) & (dist % 16 == 0))
    arr["branches"] = n.astype(np.float32)
    arr["neg_dist"] = np.where(n > 0, -dist, -1e34).astype(np.float32)
    arr["causal"] = np.where(dist >= 0, 0.0, -1e30).astype(np.float32)

    nc = bacc.Bacc("TRN2", target_bir_lowering=False, num_devices=1)
    arr = {k: np.ascontiguousarray(v) for k, v in arr.items()}
    t = {k: nc.dram_tensor(f"in_{k}", v.shape, mybir.dt.from_np(v.dtype), kind="ExternalInput").ap() for k, v in arr.items()}
    out = nc.dram_tensor("out_h", (TOK, D), F32, kind="ExternalOutput").ap()
    build(nc, t, out)
    r = run(nc, [{f"in_{k}": v for k, v in arr.items()}], core_ids=[0])
    return r.results[0]["out_h"].reshape(1, TOK, D)
```

```python
from contextlib import ExitStack

import numpy as np

import concourse.bass as bass
from concourse import mybir

F32 = mybir.dt.float32
F32R = mybir.dt.float32r
I32 = mybir.dt.int32
ALU = mybir.AluOpType
ACT = mybir.ActivationFunctionType
AX_X = mybir.AxisListType.X

P = 128
TOK = 256
TT = TOK // P
D = 2048
KT = D // P
WB = 512
RING = 4
LAT = 512
HEADS = 8
HD = 128
ROPE = 64
HALF = ROPE // 2
FFN = 5632
FA, FB = 12, 10
PLE = 256
LAYERS = 2
ALPHA = float((2.0 * LAYERS) ** 0.25)
MLA_SCALE = float((HD + ROPE) ** -0.5)
DIL_SCALE = float(HD ** -0.5)
SLOPES = [2.0 ** (-(h + 1)) for h in range(HEADS)]
GROUP = 16
PAIRS = D // GROUP // 2
SUB = 4
SLOTS = TOK // SUB
PW = 2 * GROUP
ROUND = 12582912.0

PHASES = {}
_c = _b = 0
for _name, _n, _per in [("win", 8, 8), ("kpe", 1, 8), ("qb", 3, 2), ("kvb", 4, 2), ("wout", 4, 8),
                        ("ple0", 4, 1), ("gate0", 4, 8), ("inA0", FA, 8), ("outA0", 4, FA), ("inB0", FB, 8), ("outB0", 4, FB),
                        ("glu", 8, 8),
                        ("ple1", 4, 1), ("gate1", 4, 8), ("inA1", FA, 8), ("outA1", 4, FA), ("inB1", FB, 8), ("outB1", 4, FB)]:
    PHASES[_name] = (_n, _per, _c, _b)
    _c += _n * _per
    _b += _n if not _name.startswith("ple") else 0


def lin(const, coef=0, i=None):
    return const if i is None else i * coef + const


def blocks(eng, n, body):
    body(0, None)
    if n >= 6:
        with eng.Fori(0, (n - 2) // 2) as i:
            body(1, i)
            body(2, i)
    else:
        for k in range(1, n - 1):
            body(k, None)
    body(n - 1, None)


def build(nc, t, out):
    KB = 1024
    base = 16512
    with ExitStack() as ctx:
        def at(name, shape, kb, dt=F32):
            return nc.alloc_sbuf_tensor_at(name, shape, dt, offset=base + int(kb * KB))

        def sem(name):
            return ctx.enter_context(nc.semaphore(name))

        RAW = at("raw", [P, RING, 2, WB], 0)
        WH = at("w_hi", [P, RING, 2, WB], 16, F32R)
        WL = at("w_lo", [P, RING, 2, WB], 32, F32R)
        XH = at("x_hi", [P, KT, TOK], 48, F32R)
        XL = at("x_lo", [P, KT, TOK], 64, F32R)
        RES = at("res", [P, TT, D], 80)
        GB = at("gb", [P, 2, D], 96)
        HH = at("hid_hi", [P, 2 * FA, TOK], 112, F32R)
        HL = at("hid_lo", [P, 2 * FA, TOK], 136, F32R)
        PL = at("ple", [P, TT, D], 160)
        QK = at("qk_dil", [P, 2 * HEADS, TOK], 96)
        VD = at("v_dil", [P, TT, HEADS * HD], 112)
        LH = at("lat_hi", [P, 8, TOK], 120, F32R)
        LL = at("lat_lo", [P, 8, TOK], 128, F32R)
        QN = at("q_nope", [P, HEADS, TOK], 136)
        QP = at("q_pe", [P, HEADS // 2, TOK], 144)
        KP = at("k_pe", [P, TOK], 148)
        KN = at("k_nope", [P, HEADS, TOK], 152)
        VM = at("v_mla", [P, TT, HEADS * HD], 160)
        STG = at("stage", [P, 2, TT, WB], 168)
        SM = at("s_masked", [P, 2, 3 * P], 176)
        PR = at("probs", [P, 2, 3 * P], 179)
        PT = at("probs_t", [P, 2, 3 * P], 182)
        NG = at("norm_gain", [P, 2 * LAT], 185)
        CS = at("cos_sin", [P, 2, TT, HALF], 189)
        AT = at("angle_tmp", [P, 4, TT, HALF], 190)
        S5 = at("s5_small", [PAIRS, 32, P], 144)
        EC = at("s5_coef", [P, 4, 2, P], 160)
        EB = at("s5_b", [P, 4, 2, P], 164)
        ET = at("s5_e_tmp", [P, 4, P], 168)
        EO = at("s5_e", [P, 4, 2, P], 170)
        CO = at("s5_c_pow", [P, 2, 8, SUB + 1, PW], 160)
        CR = at("s5_c", [P, 8, 2, PW], 170)
        CT = at("s5_c_tmp", [P, 8, SUB + 1, PW], 172)
        BR = at("s5_bt_raw", [P, 8, 2, PW], 177)
        BT = at("s5_bt", [P, 8, 2, PW], 179)
        BX = at("s5_bt_tmp", [P, 8, PW], 181)
        DG = at("s5_skip", [P, KT, PW], 182)
        KTAB = at("s5_k", [P, KT, SUB, PW], 184)
        PW_T = at("s5_pow", [P, 18, PAIRS], 192.5)
        KK = at("s5_toeplitz", [P, PAIRS, P], 48)
        H4 = at("h_steps", [SLOTS, PAIRS, SUB, PW], 112)
        HQ = [at(f"h_quarter{n}", [SLOTS, SUB, WB], kb) for n, kb in enumerate((192.5, 176))]
        ST = at("states", [P, SLOTS, 2, PAIRS], 112)
        U4 = at("u", [P, PAIRS, SLOTS], 144)
        Z4 = at("z", [P, 8, WB], 144)
        slot_kb = [160, 164, 168, 172, 176, 180, 96, 100, 104, 108]
        TS = [at(f"s5_table{n}", [P, 4, 2, P], kb) for n, kb in enumerate(slot_kb)]
        PK = at("p_tok", [P, TT, PLE], 160)
        ID = at("ident", [P, P], 192)
        DM = at("neg_dist", [P, 3 * P], 192.5)
        NM = at("branches", [P, 3 * P], 194)
        CM = at("causal", [P, 3 * P], 195.5)
        GT = at("gated", [P, 2, TT, 256], 197)
        AB = at("a_bar", [P, 4, PAIRS], 201)
        PH = at("p_hi", [P, 2, TOK], 202, F32R)
        PLO = at("p_lo", [P, 2, TOK], 204, F32R)
        BS = at("bn_stats", [P, TT, 8, 6], 206)
        MV = at("mean_var", [P, TT, 2], 206.5)
        SC = at("small", [P, 24], 206.625)
        SI = at("small_int", [P, 8], 206.75, I32)
        PI = at("positions", [P, TT], 206.875, I32)
        MX = at("row_max", [P, 2, 4], 206.9375)
        GTf = GT[:, :, :, :].rearrange("p a t n -> p (a t n)")

        PS = ctx.enter_context(nc.psum_tensor("ps", [P, 8, WB], F32))
        A = PS[:, 0:4, :].rearrange("p (a t) n -> p a t n", t=TT)
        TP = PS[:, 4:6, :].rearrange("p a (k n) -> p a k n", k=2)
        Y = PS[:, 6:8, :]

        coef_dram = nc.dram_tensor("s5_coef_dram", (PAIRS, SUB * 2 * P), F32, kind="Internal").ap()
        e_dram = nc.dram_tensor("s5_e_dram", (KT, P, 4 * 2 * P), F32, kind="Internal").ap()
        c_dram = nc.dram_tensor("s5_c_dram", (KT, P, 4 * 2 * P), F32, kind="Internal").ap()

        raw_full = [sem(f"raw_full{s}") for s in range(RING)]
        hi_ready, lo_ready, w_used = sem("hi_ready"), sem("lo_ready"), sem("w_used")
        x_in, p_in, p1_in, const_in, gb_in, late_in = sem("x_in"), sem("p_in"), sem("p1_in"), sem("const_in"), sem("gb_in"), sem("late_in")
        acc_free = sem("acc_free")
        turn_done = sem("turn_done")
        turn_hi = sem("turn_hi")
        turned = sem("turned")
        staged = sem("staged")
        v_step = sem("v_step")
        sq_sum = sem("sq_sum")
        trig = sem("trig")
        s_done, s_masked, nmax, p_exp, p_ready = sem("s_done"), sem("s_masked"), sem("nmax"), sem("p_exp"), sem("p_ready")
        p_turned, pt_ready, pv_done, mix_hi, mix_ready = sem("p_turned"), sem("pt_ready"), sem("pv_done"), sem("mix_hi"), sem("mix_ready")
        ln_quarter = sem("ln_quarter")
        ple_ready, gate_act, silu_done, hid_ready = sem("ple_ready"), sem("gate_act"), sem("silu_done"), sem("hid_ready")
        glu_step = sem("glu_step")
        tab, tab_ready, coef_out, ab_turned, ab_ready = sem("tab"), sem("tab_ready"), sem("coef_out"), sem("ab_turned"), sem("ab_ready")
        e_raw, e_stored, c_raw, c_stored = sem("e_raw"), sem("e_stored"), sem("c_raw"), sem("c_stored")
        k_input, k_done, k_out, kk_zero, kk_in = sem("k_input"), sem("k_done"), sem("k_out"), sem("kk_zero"), sem("kk_in")
        h4_in, h4_split, u_turned, u_ready, slot_zero = [sem("h4_in0"), sem("h4_in1")], sem("h4_split"), sem("u_turned"), sem("u_ready"), sem("slot_zero")
        ts_in = [sem(f"ts_in{n}") for n in range(10)]
        e_done, e_out_act, e_out_dve, scan = sem("e_done"), sem("e_out_act"), sem("e_out_dve"), sem("scan")
        y_done, z_half, z_act, z_turned, z_hi, z_split = sem("y_done"), sem("z_half"), sem("z_act"), sem("z_turned"), sem("z_hi"), sem("z_split")
        stored = sem("stored")

        TG = {}
        n = 0
        for name, count in [("x", 8), ("p0", 1), ("lat", 4), ("qk", 8), ("kpe", 1), ("qn", 4), ("qp", 2), ("kn", 4),
                            ("ln10", 8), ("hid0", FA + FB), ("p1", 1), ("ln11", 8),
                            ("hid1", FA + FB)]:
            TG[name] = n
            n += count
        HG = {}
        n = 0
        for name, count in [("x", 8), ("p0", 1), ("lat", 4), ("ln10", 8), ("hid0", FA + FB), ("p1", 1), ("ln11", 8),
                            ("hid1", FA + FB)]:
            HG[name] = n
            n += count

        block = ctx.enter_context(nc.Block())

        @block.sync
        def _(sp):
            sp.dma_start(RES[:], t["x"].rearrange("(t p) n -> p t n", p=P)).then_inc(x_in, 16)
            sp.dma_start(ID[:], t["ident"]).then_inc(x_in, 16)

            def load(w, local, c, coef, i, width):
                if c >= RING:
                    sp.wait_ge(lo_ready, lin(c - RING + 1, coef, i))
                src = w[bass.ds(lin(local, coef, i), 1)].rearrange("a p (k n) -> (a p) k n", k=2)
                sp.dma_start(RAW[:, c % RING, :, 0:width], src).then_inc(raw_full[c % RING], 16)

            def phase(name, weight, width=WB, first=0):
                nb, per, c0, _ = PHASES[name]
                w, total = t[weight], nb * per
                if c0 == 0:
                    for j in range(first):
                        load(w, j, j, 0, None, width)
                if (total - first) % RING:
                    for j in range(first, total):
                        load(w, j, c0 + j, 0, None, width)
                elif total - first == RING:
                    for j in range(first, total):
                        load(w, j, c0 + j, 0, None, width)
                else:
                    with sp.Fori(0, (total - first) // RING) as i:
                        for j in range(RING):
                            load(w, first + j, c0 + first + j, RING, i, width)

            def s5_loads():
                pos = 0
                def input_table(tile):
                    sp.dma_start(TS[tile % 6][:], e_dram[tile].rearrange("p (a c n) -> p a c n", a=4, c=2)).then_inc(ts_in[tile % 6], 16)

                for tile in range(4):
                    if tile == 0:
                        sp.wait_ge(e_stored, 16 * 16)
                        sp.wait_ge(k_done, 8)
                        sp.wait_ge(c_stored, 4 * 16 * 8)
                        sp.wait_ge(k_out, 2 * 8)
                    input_table(tile)
                sp.wait_ge(w_used, PHASES["glu"][2])
                for q4 in range(4):
                    sp.wait_ge(ln_quarter, 4 + q4 + 1)
                    if q4 >= 2:
                        sp.wait_ge(h4_split, q4 - 1)
                    cols = slice(WB * q4, WB * (q4 + 1))
                    for q in range(TT):
                        sp.dma_start(HQ[q4 % 2][32 * q:32 * q + 32, :, :], RES[:, q, cols]).then_inc(h4_in[q4 % 2], 16)
                sp.wait_ge(h4_split, 4)
                for tile in range(4, KT):
                    if tile >= 6:
                        sp.wait_ge(e_done, tile - 5)
                    input_table(tile)
                for n in range(KT):
                    if n < 6:
                        sp.wait_ge(e_done, KT)
                    elif n >= 10:
                        sp.wait_ge(y_done, n - 9)
                    tile = n // 2 + 8 * (n % 2)
                    sp.dma_start(TS[n % 10][:], c_dram[tile].rearrange("p (a c n) -> p a c n", a=4, c=2)).then_inc(ts_in[n % 10], 16)

            phase("win", "w_in", first=RING)
            phase("kpe", "w_kpe", ROPE)
            phase("qb", "w_qb")
            phase("kvb", "w_kvb")
            phase("wout", "w_out")
            for layer in range(LAYERS):
                if layer:
                    for j in range(2 * RING):
                        load(t["w_glu"], j, PHASES["glu"][2] + j, 0, None, WB)
                    s5_loads()
                    phase("glu", "w_glu", first=2 * RING)
                for name in ("ple", "gate", "inA", "outA", "inB", "outB"):
                    phase(f"{name}{layer}", f"w_{name}{layer}")

        @block.tensor
        def _(pe):
            def chunk(c, coef, i, hi, lo, kt, depth, acc, width=WB):
                pe.wait_ge(lo_ready, lin(c + 1, coef, i))
                s = c % RING
                for k in range(2):
                    for q in range(TT):
                        cols = slice(q * P, (q + 1) * P)
                        o = A[:, acc, q, 0:width]
                        pe.matmul(o, hi[:, kt + k, cols], WH[:, s, k, 0:width], start=(kt + k == 0), stop=False)
                        pe.matmul(o, hi[:, kt + k, cols], WL[:, s, k, 0:width], start=False, stop=False)
                        last = pe.matmul(o, lo[:, kt + k, cols], WH[:, s, k, 0:width], start=False,
                                         stop=(kt + k == depth - 1))
                last.then_inc(w_used, 1)

            def acc_ready(b, coef=0, i=None):
                if b >= 2:
                    pe.wait_ge(acc_free, lin(b - 1, coef, i))

            def turn(g, src, col, coef=0, i=None):
                if g >= 2:
                    pe.wait_ge(turned, lin(g - 1, coef, i))
                for k in range(2):
                    for q in range(TT):
                        last = pe.transpose(TP[:, g % 2, k, q * P:(q + 1) * P],
                                            src[:, q, col + k * P:col + (k + 1) * P], ID[:])
                last.then_inc(turn_done, 1)

            pe.wait_ge(x_in, 32)
            for g in range(8):
                turn(TG["x"] + g, RES[:], 256 * g)
            pe.wait_ge(p_in, 16)
            turn(TG["p0"], PK[:], 0)

            _, per, c0, b0 = PHASES["win"]
            for b in range(8):
                acc_ready(b0 + b)
                for j in range(per):
                    if b == 0:
                        pe.wait_ge(turned, TG["x"] + j + 1)
                    chunk(c0 + per * b + j, 0, None, XH, XL, 2 * j, KT, (b0 + b) % 2)
                    if j == 3 and 1 <= b <= 6:
                        pe.wait_ge(staged, b)
                        first = TG["lat"] + 2 * (b - 1) if b <= 2 else TG["qk"] + 2 * (b - 3)
                        for g in range(2):
                            turn(first + g, STG[:, (b - 1) % 2], 256 * g)
            _, per, c0, b0 = PHASES["kpe"]
            acc_ready(b0)
            for j in range(per):
                chunk(c0 + j, 0, None, XH, XL, 2 * j, KT, b0 % 2, ROPE)

            QB, KVB = PHASES["qb"], PHASES["kvb"]
            groups = [TG["kpe"], TG["qn"], TG["qn"] + 2, TG["qp"], TG["kn"], TG["kn"] + 2]

            def turn_up(m):
                pe.wait_ge(staged, 7 + m)
                if m == 0:
                    g = TG["kpe"]
                    pe.wait_ge(turned, g - 1)
                    for q in range(TT):
                        last = pe.transpose(TP[:, g % 2, 0, q * P:(q + 1) * P], STG[:, 0, q, 0:P], ID[:])
                    last.then_inc(turn_done, 1)
                else:
                    for g in range(2):
                        turn(groups[m] + g, STG[:, m % 2], 256 * g)

            pe.wait_ge(turned, TG["qk"])
            for b in range(7):
                acc_ready(QB[3] + b)
                for j in range(2):
                    row = 2 * j
                    part = slice(0, 4) if b < 3 else slice(4, 8)
                    chunk(QB[2] + 2 * b + j, 0, None, LH[:, part], LL[:, part], row, 4, (QB[3] + b) % 2)
                if b >= 1 and b <= 6:
                    turn_up(b - 1)

            pe.wait_ge(acc_free, QB[3] + 7)
            pe.wait_ge(turned, TG["ln10"])

            def scores(h):
                if h >= 2:
                    pe.wait_ge(s_masked, h - 1)
                dst = A[:, 0, h % 2]
                for q in range(TT):
                    cols = slice(0, P) if q == 0 else slice(P, 3 * P)
                    keys = slice(0, (q + 1) * P)
                    rows = slice(q * P, (q + 1) * P)
                    if h < HEADS:
                        last = pe.matmul(dst[:, cols], QK[:, h, rows], QK[:, HEADS + h, keys], start=True, stop=True)
                    else:
                        m = h - HEADS
                        half = slice(ROPE * (m % 2), ROPE * (m % 2) + ROPE)
                        pe.matmul(dst[:, cols], QN[:, m, rows], KN[:, m, keys], start=True, stop=False)
                        last = pe.matmul(dst[:, cols], QP[half, m // 2, rows], KP[half, keys], start=False, stop=True)
                last.then_inc(s_done, 1)

            def turn_probs(h):
                pe.wait_ge(p_ready, h + 1)
                if h >= 2:
                    pe.wait_ge(pt_ready, h - 1)
                for n_, s in enumerate([0, 1, 2]):
                    last = pe.transpose(Y[:, h % 2, n_ * P:(n_ + 1) * P], PR[:, h % 2, s * P:(s + 1) * P], ID[:])
                last.then_inc(p_turned, 1)

            def values(h):
                pe.wait_ge(pt_ready, h + 1)
                if h >= 2:
                    pe.wait_ge(mix_ready, h - 1)
                v = VD if h < HEADS else VM
                d = slice((h % HEADS) * HD, (h % HEADS + 1) * HD)
                pe.matmul(A[:, 1, h % 2, 0:TOK], v[:, 0, d], PT[:, h % 2, 0:TOK], start=True, stop=False)
                pe.matmul(A[:, 1, h % 2, P:TOK], v[:, 1, d], PT[:, h % 2, TOK:3 * P], start=False,
                          stop=True).then_inc(pv_done, 1)

            scores(0)
            for s in range(2 * HEADS + 3):
                if s + 1 < 2 * HEADS:
                    scores(s + 1)
                if s >= 3:
                    values(s - 3)
                if 1 <= s <= 2 * HEADS:
                    turn_probs(s - 1)

            _, per, c0, b0 = PHASES["wout"]
            for b in range(4):
                if b:
                    acc_ready(b0 + b)
                for j in range(per):
                    if b == 0:
                        pe.wait_ge(mix_ready, 16 if j == 7 else 2 * j + 2)
                    chunk(c0 + per * b + j, 0, None, XH, XL, 2 * j, KT, (b0 + b) % 2)

            def feed_forward(layer):
                _, _, c0, b0 = PHASES[f"ple{layer}"]
                pe.wait_ge(turned, TG[f"p{layer}"] + 1)
                for b in range(4):
                    if b < 2:
                        pe.wait_ge(acc_free, b0 - 1 + b)
                    else:
                        pe.wait_ge(ple_ready, 4 * layer + b - 1)
                    chunk(c0 + b, 0, None, PH, PLO, 0, 2, (b0 + b) % 2)
                _, per, c0, b0 = PHASES[f"gate{layer}"]
                g0 = TG[f"ln1{layer}"]
                for b in range(4):
                    acc_ready(b0 + b)
                    if b < 2:
                        pe.wait_ge(ple_ready, 4 * layer + 3 + b)
                    for j in range(per):
                        if b == 0:
                            if j % 2 == 0:
                                pe.wait_ge(ln_quarter, 8 * layer + j // 2 + 1)
                                turn(g0 + j, RES[:], 256 * j)
                                turn(g0 + j + 1, RES[:], 256 * (j + 1))
                            pe.wait_ge(turned, g0 + j + 1)
                        chunk(c0 + per * b + j, 0, None, XH, XL, 2 * j, KT, (b0 + b) % 2)

                if layer == 0:
                    pe.wait_ge(tab_ready, 1)
                    for n_ in range(8):
                        pe.transpose(Y[:, 0, n_ * PAIRS:(n_ + 1) * PAIRS], S5[:, 8 + n_, :], ID[0:PAIRS, 0:PAIRS])
                    for n_ in range(2):
                        last = pe.transpose(Y[:, 1, n_ * PAIRS:(n_ + 1) * PAIRS], S5[:, 6 + n_, :], ID[0:PAIRS, 0:PAIRS])
                    last.then_inc(ab_turned, 1)

                def response(it):
                    pe.wait_ge(k_input, it + 1)
                    pe.wait_ge(ab_ready, 9)
                    if it >= 2:
                        pe.wait_ge(k_out, 2 * (it - 1))
                    for a in range(8):
                        o = Y[32 * (a % 4):32 * (a % 4) + 32, it % 2, P * (a // 4):P * (a // 4 + 1)]
                        for ri in range(2):
                            last = pe.matmul(o, BT[:, a, ri, :], CO[:, ri, a, 0:SUB, :], start=(ri == 0), stop=(ri == 1))
                    last.then_inc(k_done, 1)

                def hidden_turn(b, coef=0, i=None):
                    done = (FA + FB) * layer + b
                    pe.wait_ge(hid_ready, lin(done + 1, coef, i))
                    turn(TG[f"hid{layer}"] + b, GT[:, 1], 0, coef, i)

                for part, n_in, first in (("A", FA, 0), ("B", FB, FA)):
                    _, per, c0, b0 = PHASES[f"in{part}{layer}"]

                    def inner(k, i):
                        acc_ready(b0 + k, 2, i)
                        for j in range(per):
                            chunk(c0 + per * k + j, 2 * per, i, XH, XL, 2 * j, KT, (b0 + k) % 2)
                            if j == 3 and k > 0:
                                hidden_turn(first + k - 1, 2, i)
                    blocks(pe, n_in, inner)
                    _, per, c0, b0 = PHASES[f"out{part}{layer}"]
                    for b in range(4):
                        acc_ready(b0 + b)
                        for j in range(per):
                            if b == 0 and j == per - 1:
                                pe.wait_ge(turned, TG[f"hid{layer}"] + first + n_in)
                            elif b == 0 and j == 0:
                                pe.wait_ge(turned, TG[f"hid{layer}"] + first + n_in - 1)
                            chunk(c0 + per * b + j, 0, None, HH, HL, 2 * j, 2 * n_in, (b0 + b) % 2)
                            if b == 0 and j == 3:
                                hidden_turn(first + n_in - 1)
                        if layer == 0:
                            response(b if part == "A" else 4 + b)

            feed_forward(0)

            pe.wait_ge(acc_free, PHASES["outB0"][3] + 4)
            pe.wait_ge(turned, TG["p1"])
            pe.wait_ge(k_out, 2 * 8)
            for n_ in range(8):
                if n_ % 2 == 0:
                    pe.wait_ge(h4_split, n_ // 2 + 1)
                for a in range(8):
                    last = pe.transpose(PS[:, n_, a * SLOTS:(a + 1) * SLOTS],
                                        H4[:, 8 * n_ + a].rearrange("p s c -> p (s c)"), ID[0:SLOTS, 0:SLOTS])
                last.then_inc(u_turned, 1)
            pe.wait_ge(u_ready, 8)
            for tile in range(KT):
                pe.wait_ge(ts_in[tile % 6], 16 * (tile // 6 + 1))
                if tile >= 8:
                    pe.wait_ge(e_out_dve if tile % 2 else e_out_act, (tile - 8) // 2 + 1)
                for a in range(4):
                    for ri in range(2):
                        o = (2 * a + ri) * SLOTS
                        last = pe.matmul(PS[:, tile % 8, o:o + SLOTS - 1], TS[tile % 6][:, a, ri, :],
                                         U4[:, 4 * tile + a, 0:SLOTS - 1], start=True, stop=True)
                last.then_inc(e_done, 1)
            pe.wait_ge(e_out_act, 8)
            pe.wait_ge(e_out_dve, 8)
            pe.wait_ge(kk_in, 16 * 16)

            def bank_of(pair):
                tile, a = pair // 4, pair % 4
                half = SLOTS * (tile // 8)
                return PS[half:half + SLOTS, tile % 8, P * a:P * (a + 1)]

            for pair in range(PAIRS):
                pe.matmul(bank_of(pair), U4[:, pair, :], KK[:, pair, :], start=(pair % 4 == 0), stop=False,
                          skip_group_check=True)
            pe.wait_ge(scan, 6 * (SLOTS - 2))

            def read_out(n_):
                tile = n_ // 2 + 8 * (n_ % 2)
                count = 16 * (n_ // 10 + 1) + (16 * (3 if n_ % 10 < 4 else 2) if n_ % 10 < 6 else 0)
                pe.wait_ge(ts_in[n_ % 10], count)
                for a in range(4):
                    pair = 4 * tile + a
                    for ri in range(2):
                        last = pe.matmul(bank_of(pair), ST[:, :, ri, pair], TS[n_ % 10][:, a, ri, :], start=False,
                                         stop=(ri == 1), skip_group_check=True)
                last.then_inc(y_done, 1)

            def turn_z(b):
                pe.wait_ge(z_act, b + 1)
                for half in range(2):
                    rows = slice(SLOTS * half, SLOTS * (half + 1))
                    for s in range(SUB):
                        o = TOK * half + SLOTS * s
                        if half and s == 0:
                            pe.wait_ge(z_half, b + 1)
                        last = pe.transpose(PS[:, b, o:o + SLOTS], Z4[rows, b, P * s:P * (s + 1)], ID[rows, rows])
                    last.then_inc(z_turned if half else z_half, 1)

            for b in range(8):
                read_out(2 * b)
                read_out(2 * b + 1)
                if b >= 2:
                    turn_z(b - 2)
            turn_z(6)
            turn_z(7)

            _, per, c0, b0 = PHASES["glu"]
            pe.wait_ge(z_split, 4)

            def glu(k, i):
                acc_ready(b0 + k, 2, i)
                for j in range(per):
                    if k == 0:
                        pe.wait_ge(z_split, j + 1)
                    chunk(c0 + per * k + j, 2 * per, i, XH, XL, 2 * j, KT, (b0 + k) % 2)
                    if k == 0 and j == 7:
                        pe.wait_ge(p1_in, 16)
                        turn(TG["p1"], PK[:], 0)
            blocks(pe, 8, glu)
            feed_forward(1)

        @block.scalar
        def _(act):
            for dst, name in [(DM[:], "neg_dist"), (NM[:], "branches"), (CM[:], "causal"), (PI[:], "pos")]:
                act.dma_start(dst, t[name]).then_inc(const_in, 16)
            act.dma_start(NG[:], t["norm_gain"].partition_broadcast(P)).then_inc(const_in, 16)
            for q in range(TT):
                act.dma_start(AT[:, 3, q, :], t["inv_freq"].partition_broadcast(P)).then_inc(const_in, 16)
            act.dma_start(PK[:], t["p"][0].rearrange("(t p) n -> p t n", p=P)).then_inc(p_in, 16)

            def hi(c, coef=0, i=None, width=WB):
                s = c % RING
                act.wait_ge(raw_full[s], lin(16 * (c // RING + 1), 16 * coef // RING, i))
                if c >= RING:
                    act.wait_ge(w_used, lin(c - RING + 1, coef, i))
                act.activation(WH[:, s, :, 0:width], RAW[:, s, :, 0:width], ACT.Copy).then_inc(hi_ready, 1)

            def hi_turned(g, dst, coef=0, i=None):
                act.wait_ge(turn_done, lin(g + 1, coef, i))
                act.activation(dst, TP[:, g % 2], ACT.Copy).then_inc(turn_hi, 1)

            def end(name, b, coef=0, i=None):
                _, per, c0, _ = PHASES[name]
                act.wait_ge(w_used, lin(c0 + per * (b + 1), per * coef, i))

            _, _, c0, b0 = PHASES["win"]
            for g in range(8):
                hi_turned(TG["x"] + g, XH[:, 2 * g:2 * g + 2, :])
                if g < RING:
                    hi(g)
            hi_turned(TG["p0"], PH[:])

            def stage(m, name, b, parity):
                end(name, b)
                if m >= 2:
                    pass
                act.activation(STG[:, m % 2], A[:, parity], ACT.Copy).then_inc(staged, 1)

            def win_end(b):
                end("win", b)
                if b < 2:
                    if b == 0:
                        act.wait_ge(const_in, 7 * 16)
                    else:
                        act.wait_ge(sq_sum, 2 * b)
                    for q in range(TT):
                        act.activation(GTf[:, WB * q:WB * (q + 1)], A[:, b % 2, q], ACT.Square,
                                       accum_out=SC[:, 2 * b + q:2 * b + q + 1]).then_inc(sq_sum, 1)
                elif b < 6:
                    act.wait_ge(turn_done, TG["lat"] + 2 * (b - 1))
                    act.activation(STG[:, b % 2], A[:, b % 2], ACT.Copy).then_inc(staged, 1)
                else:
                    act.activation(VD[:, :, (b - 6) * WB:(b - 5) * WB], A[:, b % 2], ACT.Copy).then_inc(acc_free, 1)

            for b in range(8):
                for j in range(8):
                    c = 8 * b + j
                    if c >= RING:
                        hi(c)
                    if j == 4 and b:
                        win_end(b - 1)
                    if b == 3 and j == 6:
                        act.wait_ge(trig, 1)
                        act.activation(CS[:, 1], AT[:, 0], ACT.Sin).then_inc(trig, 1)
                        act.activation(CS[:, 0], AT[:, 0], ACT.Sin, scale=0.5).then_inc(trig, 1)
                    if b >= 1 and j == 7 and b <= 2:
                        for g in range(2):
                            n_ = 2 * (b - 1) + g
                            hi_turned(TG["lat"] + n_, LH[:, 2 * n_:2 * n_ + 2, :])
            c0 = PHASES["kpe"][2]
            for j in range(8):
                hi(c0 + j, width=ROPE)
                if j == 4:
                    win_end(7)
            QB, KVB = PHASES["qb"], PHASES["kvb"]

            def up_end(m):
                b = m - 1
                act.wait_ge(w_used, QB[2] + 2 * (b + 1))
                if m in (1, 2, 4, 5):
                    if m <= 2:
                        if m == 2:
                            act.wait_ge(turn_done, TG["kpe"] + 1)
                    else:
                        act.wait_ge(turn_done, TG["qn"] + 2 * (m - 2))
                    act.activation(STG[:, m % 2], A[:, (QB[3] + b) % 2], ACT.Copy).then_inc(staged, 1)
                elif m >= 6:
                    act.activation(VM[:, :, (m - 6) * WB:(m - 5) * WB], A[:, (QB[3] + b) % 2],
                                   ACT.Copy).then_inc(acc_free, 1)

            for b in range(7):
                hi(QB[2] + 2 * b)
                hi(QB[2] + 2 * b + 1)
                if b >= 1:
                    up_end(b)
            up_end(7)

            c0 = PHASES["wout"][2]

            def exps(h):
                act.wait_ge(nmax, h + 1)
                if h >= 2:
                    act.wait_ge(p_turned, h - 1)
                scale = DIL_SCALE if h < HEADS else MLA_SCALE
                for q in range(TT):
                    cols = slice(0, P) if q == 0 else slice(P, 3 * P)
                    sums = {} if h < HEADS else {"accum_out": MX[:, h % 2, 2 + q:3 + q]}
                    act.activation(PR[:, h % 2, cols], SM[:, h % 2, cols], ACT.Exp, bias=MX[:, h % 2, q:q + 1],
                                   scale=scale, **sums).then_inc(p_exp, 1)

            def probs_out(h):
                act.wait_ge(p_turned, h + 1)
                if h >= 2:
                    act.wait_ge(pv_done, h - 1)
                act.activation(PT[:, h % 2], Y[:, h % 2, 0:3 * P], ACT.Copy).then_inc(pt_ready, 1)

            def mix_high(h):
                act.wait_ge(pv_done, h + 1)
                act.activation(XH[:, h, :], A[:, 1, h % 2, 0:TOK], ACT.Copy).then_inc(mix_hi, 1)

            for s in range(2 * HEADS + 3):
                if s < 2 * HEADS:
                    exps(s)
                if 2 <= s < 2 * HEADS + 2:
                    probs_out(s - 2)
                if s >= 3:
                    mix_high(s - 3)
                if 4 <= s < 8:
                    hi(c0 + s - 4)
            for c in range(c0 + 4, c0 + 32):
                hi(c)

            def feed_forward(layer):
                _, _, c0, b0 = PHASES[f"ple{layer}"]
                g0 = PHASES[f"gate{layer}"][2]
                for b in range(4):
                    hi(c0 + b)
                for b in range(4):
                    end(f"ple{layer}", b)
                    act.activation(PL[:, :, b * WB:(b + 1) * WB], A[:, (b0 + b) % 2], ACT.Copy).then_inc(ple_ready, 1)
                    hi(g0 + b)
                for g in range(8):
                    hi_turned(TG[f"ln1{layer}"] + g, XH[:, 2 * g:2 * g + 2, :])
                    if g >= 1 and g < 5:
                        hi(g0 + 3 + g)

                def gate_sigmoid(b):
                    end(f"gate{layer}", b)
                    done = (4 + 4) * layer * 1 + b
                    n_ = 4 * layer + b
                    if n_:
                        act.wait_ge(acc_free, PHASES[f"gate{layer}"][3] + b)
                    act.activation(GT[:, :, :, :].rearrange("p a t n -> p t a n"),
                                   A[:, (PHASES[f"gate{layer}"][3] + b) % 2].rearrange("p t (a n) -> p t a n", a=2),
                                   ACT.Sigmoid).then_inc(gate_act, 1)

                for b in range(1, 4):
                    for j in range(8):
                        hi(g0 + 8 * b + j)
                        if j == 4:
                            gate_sigmoid(b - 1)

                def silu(b, coef=0, i=None):
                    part, k = ("A", b) if b < FA else ("B", b - FA)
                    end(f"in{part}{layer}", k, coef, i)
                    done = (FA + FB) * layer + b
                    if done:
                        act.wait_ge(hid_ready, lin(done, coef, i))
                    parity = (PHASES[f"in{part}{layer}"][3] + k) % 2
                    act.activation(GT[:, 0], A[:, parity, :, 0:256], ACT.Silu).then_inc(silu_done, 1)

                def hidden_hi(b, coef=0, i=None):
                    k = b if b < FA else b - FA
                    hi_turned(TG[f"hid{layer}"] + b, HH[:, bass.ds(lin(2 * k, 2 * coef, i), 2), :], coef, i)

                for part, n_in, first in (("A", FA, 0), ("B", FB, FA)):
                    _, per, c0, _ = PHASES[f"in{part}{layer}"]

                    def inner(k, i):
                        for j in range(per):
                            hi(c0 + per * k + j, 2 * per, i)
                            if k > 0 and j == 4:
                                silu(first + k - 1, 2, i)
                            if k == 0 and j == 4 and part == "A":
                                gate_sigmoid(3)
                            if k > 0 and j == 7:
                                hidden_hi(first + k - 1, 2, i)
                    blocks(act, n_in, inner)
                    nb, per, c0, _ = PHASES[f"out{part}{layer}"]
                    for j in range(8):
                        hi(c0 + j)
                        if j == 4:
                            silu(first + n_in - 1)
                        if j == 7:
                            hidden_hi(first + n_in - 1)
                    rest = nb * per - 8
                    with act.Fori(0, rest // RING) as i:
                        for j in range(RING):
                            hi(c0 + 8 + j, RING, i)

            feed_forward(0)
            c0 = PHASES["glu"][2]
            for j in range(4):
                hi(c0 + j)
            def by_pairs(q4):
                act.wait_ge(h4_in[q4 % 2], 32 * (q4 // 2 + 1))
                act.activation(H4[:, 16 * q4:16 * q4 + 16], HQ[q4 % 2][:].rearrange("p s (a c) -> p a s c", c=PW),
                               ACT.Copy).then_inc(h4_split, 1)

            by_pairs(0)
            by_pairs(1)
            for n_ in range(8):
                if n_ in (2, 4):
                    by_pairs(n_ // 2 + 1)
                act.wait_ge(u_turned, n_ + 1)
                act.activation(U4[:, 8 * n_:8 * n_ + 8, :], PS[:, n_, :].rearrange("p (a n) -> p a n", a=8),
                               ACT.Copy).then_inc(u_ready, 1)
            act.wait_ge(u_ready, 8)
            for tile in range(0, KT, 2):
                act.wait_ge(e_done, tile + 1)
                act.activation(ST[:, 1:SLOTS, :, 4 * tile:4 * tile + 4].rearrange("p n c a -> p a c n"),
                               PS[:, tile % 8, :].rearrange("p (a c n) -> p a c n", a=4, c=2)[:, :, :, 0:SLOTS - 1],
                               ACT.Copy).then_inc(e_out_act, 1)

            def gelu(b):
                act.wait_ge(y_done, 2 * b + 2)
                act.activation(Z4[:, b, :].rearrange("p (s a c) -> p a s c", s=SUB, a=4),
                               PS[:, b, :].rearrange("p (a s c) -> p a s c", a=4, s=SUB),
                               ACT.Gelu_apprx_tanh).then_inc(z_act, 1)

            def z_high(b):
                act.wait_ge(z_turned, b + 1)
                act.activation(XH[:, 2 * b:2 * b + 2, :].rearrange("p k (n s) -> p k s n", s=SUB),
                               PS[:, b, :].rearrange("p (k s n) -> p k s n", k=2, s=SUB), ACT.Copy).then_inc(z_hi, 1)

            for b in range(8):
                gelu(b)
                if b >= 3:
                    z_high(b - 3)
            for b in range(5, 8):
                z_high(b)

            b0 = PHASES["glu"][3]

            def glu_sigmoid(b, coef=0, i=None):
                end("glu", b, coef, i)
                act.wait_ge(acc_free, lin(b0 + b, coef, i))
                act.activation(GT[:, 0], A[:, (b0 + b) % 2, :, 256:512], ACT.Sigmoid).then_inc(gate_act, 1)

            def glu(k, i):
                for j in range(8):
                    if not (k == 0 and j < 4):
                        hi(c0 + 8 * k + j, 16, i)
                    if k > 0 and j == 4:
                        glu_sigmoid(k - 1, 2, i)
                    if k == 7 and j == 2:
                        hi_turned(TG["p1"], PH[:])
            blocks(act, 8, glu)
            glu_sigmoid(7)
            feed_forward(1)

        @block.vector
        def _(dve):
            step = [0]

            def link(ins):
                ins.then_inc(v_step, 1)
                step[0] += 1
                dve.wait_ge(v_step, step[0])

            def lo(c, coef=0, i=None, width=WB):
                s = c % RING
                dve.wait_ge(hi_ready, lin(c + 1, coef, i))
                if c >= RING:
                    dve.wait_ge(w_used, lin(c - RING + 1, coef, i))
                dve.tensor_tensor(WL[:, s, :, 0:width], RAW[:, s, :, 0:width], WH[:, s, :, 0:width].bitcast(F32),
                                  ALU.subtract).then_inc(lo_ready, 1)

            hg = [0]

            def lo_turned(g, n_hi, hi_ap, lo_ap, coef=0, i=None):
                dve.wait_ge(turn_hi, lin(n_hi + 1, coef, i))
                dve.tensor_tensor(lo_ap, TP[:, g % 2], hi_ap.bitcast(F32), ALU.subtract).then_inc(turned, 1)

            def whole_turned(g, dst, src=None):
                dve.wait_ge(turn_done, g + 1)
                dve.tensor_copy(dst, TP[:, g % 2] if src is None else src).then_inc(turned, 1)

            def end(name, b, coef=0, i=None):
                _, per, c0, _ = PHASES[name]
                dve.wait_ge(w_used, lin(c0 + per * (b + 1), per * coef, i))

            def rsqrt(v, y, tmp, n_):
                half = SI[:, 0:n_]
                link(dve.tensor_scalar(half, v.bitcast(I32), 1, None, ALU.logical_shift_right))
                link(dve.tensor_scalar(y.bitcast(I32), half, -1.0, float(0x5F3759DF), ALU.mult, ALU.add))
                for _ in range(3):
                    link(dve.scalar_tensor_tensor(tmp, y, -0.5, y, ALU.mult, ALU.mult))
                    link(dve.tensor_tensor(tmp, tmp, v, ALU.mult))
                    link(dve.scalar_tensor_tensor(y, tmp, 1.5, y, ALU.add, ALU.mult))

            for g in range(8):
                lo_turned(TG["x"] + g, HG["x"] + g, XH[:, 2 * g:2 * g + 2, :], XL[:, 2 * g:2 * g + 2, :])
                if g < RING:
                    lo(g)
            lo_turned(TG["p0"], HG["p0"], PH[:], PLO[:])

            def angles():
                dve.wait_ge(const_in, 7 * 16)
                two_pi = 2 * np.pi
                c1 = 6.28125
                c2 = float(np.float32(np.round((two_pi - c1) * 2 ** 17) / 2 ** 17))
                c3 = float(np.round((two_pi - c1 - c2) * 2 ** 25) / 2 ** 25)
                c4 = float(np.float32(two_pi - c1 - c2 - c3))
                link(dve.tensor_copy(SC[:, 8:10], PI[:]))
                for q in range(TT):
                    link(dve.tensor_scalar(AT[:, 0, q], AT[:, 3, q], SC[:, 8 + q:9 + q], None, ALU.mult))
                r, n_ = AT[:, 0], AT[:, 1]
                link(dve.tensor_scalar(n_, r, 1.0 / two_pi, ROUND, ALU.mult, ALU.add))
                link(dve.tensor_scalar(n_, n_, -ROUND, None, ALU.add))
                for c in (c1, c2, c3, c4):
                    link(dve.scalar_tensor_tensor(r, n_, -c, r, ALU.mult, ALU.add))
                dve.tensor_scalar(r, r, float(np.float32(3.1415925)), -float(np.float32(3.1415925)), ALU.min,
                                  ALU.max).then_inc(trig, 1)

            def cosine():
                dve.wait_ge(trig, 3)
                link(dve.tensor_tensor(CS[:, 0], CS[:, 0], CS[:, 0], ALU.mult))
                link(dve.tensor_scalar(CS[:, 0], CS[:, 0], -2.0, 1.0, ALU.mult, ALU.add))

            def rotate(src, dst, heads):
                for out_half, (first, second, op) in enumerate([(0, 1, ALU.subtract), (1, 0, ALU.add)]):
                    cos = CS[:, 0].unsqueeze(2).broadcast_to([P, TT, heads, HALF])
                    sin = CS[:, 1].unsqueeze(2).broadcast_to([P, TT, heads, HALF])
                    tmp = GTf[:, 512:512 + TT * heads * HALF].rearrange("p (t h n) -> p t h n", t=TT, h=heads)
                    link(dve.tensor_tensor(tmp, src[:, :, :, second], sin, ALU.mult))
                    link(dve.tensor_tensor(dst[:, :, :, first], src[:, :, :, first], cos, ALU.mult))
                    last = dve.tensor_tensor(dst[:, :, :, first], dst[:, :, :, first], tmp, op)
                    if out_half == 0:
                        link(last)
                return last

            def latent(b):
                dve.wait_ge(sq_sum, 2 * b + 2)
                v, y, tmp = SC[:, 4:6], SC[:, 6:8], SC[:, 10:12]
                link(dve.tensor_scalar(v, SC[:, 2 * b:2 * b + 2], 1.0 / LAT, 1e-6, ALU.mult, ALU.add))
                rsqrt(v, y, tmp, 2)
                link(dve.scalar_tensor_tensor(STG[:, b % 2, 0], A[:, b % 2, 0], y[:, 0:1], NG[:, b * LAT:(b + 1) * LAT],
                                              ALU.mult, ALU.mult))
                link(dve.scalar_tensor_tensor(STG[:, b % 2, 1], A[:, b % 2, 1], y[:, 1:2], NG[:, b * LAT:(b + 1) * LAT],
                                              ALU.mult, ALU.mult))
                dve.nop().then_inc(staged, 1)
                dve.nop().then_inc(acc_free, 1)

            for b in range(8):
                for j in range(8):
                    if 8 * b + j >= RING:
                        lo(8 * b + j)
                    if j == 0 and b == 1:
                        angles()
                    if j == 0 and b == 6:
                        cosine()
                    if j == 5 and b in (1, 2):
                        latent(b - 1)
                    if j == 5 and 3 <= b <= 6:
                        dve.wait_ge(staged, b)
                        dve.nop().then_inc(acc_free, 1)
                    if j == 7 and 1 <= b <= 6:
                        for g in range(2):
                            if b <= 2:
                                n_ = 2 * (b - 1) + g
                                lo_turned(TG["lat"] + n_, HG["lat"] + n_, LH[:, 2 * n_:2 * n_ + 2, :],
                                          LL[:, 2 * n_:2 * n_ + 2, :])
                            else:
                                n_ = 2 * (b - 3) + g
                                whole_turned(TG["qk"] + n_, QK[:, 2 * n_:2 * n_ + 2, :])
            c0 = PHASES["kpe"][2]
            for j in range(8):
                lo(c0 + j, width=ROPE)
            QB = PHASES["qb"]

            def up_turned(m):
                if m == 0:
                    g = TG["kpe"]
                    whole_turned(g, KP[:], TP[:, g % 2, 0])
                else:
                    dst, h = [(QN, 0), (QN, 4), (QP, 0), (KN, 0), (KN, 4)][m - 1]
                    g = [TG["qn"], TG["qn"] + 2, TG["qp"], TG["kn"], TG["kn"] + 2][m - 1]
                    for n_ in range(2):
                        whole_turned(g + n_, dst[:, h + 2 * n_:h + 2 * n_ + 2, :])

            for b in range(7):
                lo(QB[2] + 2 * b)
                lo(QB[2] + 2 * b + 1)
                if b == 0:
                    end("kpe", 0)
                    src = A[:, PHASES["kpe"][3] % 2, :, 0:ROPE].rearrange("p t (h c n) -> p t h c n", h=1, c=2)
                    dve.wait_ge(turn_done, TG["kpe"])
                    dst = STG[:, 0, :, 0:ROPE].rearrange("p t (h c n) -> p t h c n", h=1, c=2)
                    link(rotate(src, dst, 1))
                    link(dve.tensor_copy(STG[:, 0, :, ROPE:2 * ROPE], STG[:, 0, :, 0:ROPE]))
                    dve.nop().then_inc(staged, 1)
                    dve.nop().then_inc(acc_free, 1)
                if b in (1, 2, 4, 5):
                    dve.wait_ge(staged, 7 + b)
                    dve.nop().then_inc(acc_free, 1)
                if b == 3:
                    end("qb", 2)
                    dve.wait_ge(turn_done, TG["qn"] + 2)
                    src = A[:, (QB[3] + 2) % 2].rearrange("p t (h c n) -> p t h c n", h=HEADS, c=2)
                    dst = STG[:, 1].rearrange("p t (h c n) -> p t h c n", h=HEADS, c=2)
                    link(rotate(src, dst, HEADS))
                    dve.nop().then_inc(staged, 1)
                    dve.nop().then_inc(acc_free, 1)
                if b >= 2:
                    up_turned(b - 2)
            up_turned(5)

            c0 = PHASES["wout"][2]

            def mask_and_max(h):
                dve.wait_ge(s_done, h + 1)
                if h >= 2:
                    dve.wait_ge(p_exp, 2 * (h - 1))
                scale, slope, m = (DIL_SCALE, SLOPES[h] / DIL_SCALE, DM) if h < HEADS else (MLA_SCALE, 1.0, CM)
                dve.scalar_tensor_tensor(SM[:, h % 2], m[:], slope, A[:, 0, h % 2, 0:3 * P], ALU.mult,
                                         ALU.add).then_inc(s_masked, 1)
                dve.wait_ge(s_masked, h + 1)
                if h >= 1:
                    dve.wait_ge(nmax, h)
                dve.tensor_reduce(SC[:, 12:13], SM[:, h % 2, 0:P], AX_X, ALU.max)
                link(dve.tensor_reduce(SC[:, 13:14], SM[:, h % 2, P:3 * P], AX_X, ALU.max))
                dve.tensor_scalar(MX[:, h % 2, 0:2], SC[:, 12:14], -scale, None, ALU.mult).then_inc(nmax, 1)

            def norm_probs(h):
                dve.wait_ge(p_exp, 2 * h + 2)
                if h >= 1:
                    dve.wait_ge(p_ready, h)
                parts = [slice(0, P), slice(P, 3 * P)]
                if h < HEADS:
                    for q in range(TT):
                        link(dve.scalar_tensor_tensor(PR[:, h % 2, parts[q]], PR[:, h % 2, parts[q]], 1.0,
                                                      NM[:, parts[q]], ALU.mult, ALU.mult,
                                                      accum_out=MX[:, h % 2, 2 + q:3 + q]))
                link(dve.reciprocal(SC[:, 14:16], MX[:, h % 2, 2:4]))
                link(dve.tensor_scalar(PR[:, h % 2, parts[0]], PR[:, h % 2, parts[0]], SC[:, 14:15], None, ALU.mult))
                dve.tensor_scalar(PR[:, h % 2, parts[1]], PR[:, h % 2, parts[1]], SC[:, 15:16], None,
                                  ALU.mult).then_inc(p_ready, 1)

            def mix_low(h):
                dve.wait_ge(mix_hi, h + 1)
                dve.tensor_tensor(XL[:, h, :], A[:, 1, h % 2, 0:TOK], XH[:, h, :].bitcast(F32),
                                  ALU.subtract).then_inc(mix_ready, 1)

            for s in range(2 * HEADS + 4):
                if s < 2 * HEADS:
                    mask_and_max(s)
                if 1 <= s <= 2 * HEADS:
                    norm_probs(s - 1)
                if s >= 4:
                    mix_low(s - 4)
                if 4 <= s < 8:
                    lo(c0 + s - 4)

            def add_stats(b, q, width, n_):
                return dve.bn_stats(BS[:, q, n_, :], RES[:, q, width * b:width * (b + 1)])

            def wout_end(b):
                end("wout", b)
                cols = slice(WB * b, WB * (b + 1))
                dve.scalar_tensor_tensor(RES[:, :, cols], RES[:, :, cols], ALPHA, A[:, (PHASES["wout"][3] + b) % 2],
                                         ALU.mult, ALU.add).then_inc(acc_free, 1)
                dve.wait_ge(acc_free, PHASES["wout"][3] + b + 1)
                for q in range(TT):
                    last = add_stats(b, q, WB, b)
                last.then_inc(v_step, 1)
                step[0] += 1

            for b in range(4):
                for j in range(8):
                    if 8 * b + j >= 4:
                        lo(c0 + 8 * b + j)
                    if b and j == 4:
                        wout_end(b - 1)

            def norm_scalars(n_):
                dve.wait_ge(v_step, step[0])
                for q in range(TT):
                    last = dve.bn_aggr(MV[:, q, :], BS[:, q, 0:n_, :].rearrange("p a b -> p (a b)"))
                link(last)
                link(dve.tensor_scalar(SC[:, 18:20], MV[:, :, 1], 1e-5, None, ALU.add))
                rsqrt(SC[:, 18:20], SC[:, 16:18], SC[:, 20:22], 2)

            def norm_quarter(n_, q4):
                dve.wait_ge(gb_in, 32 * (n_ + 1))
                cols = slice(WB * q4, WB * (q4 + 1))
                for q in range(TT):
                    link(dve.scalar_tensor_tensor(RES[:, q, cols], RES[:, q, cols], MV[:, q, 0:1], GB[:, 0, cols],
                                                  ALU.subtract, ALU.mult))
                    last = dve.scalar_tensor_tensor(RES[:, q, cols], RES[:, q, cols], SC[:, 16 + q:17 + q],
                                                    GB[:, 1, cols], ALU.mult, ALU.add)
                    if q == 0:
                        last.then_inc(v_step, 1)
                        step[0] += 1
                    else:
                        last.then_inc(ln_quarter, 1)

            def feed_forward(layer):
                ln1, ln2 = 2 * layer, 2 * layer + 1
                c_ple, b_ple = PHASES[f"ple{layer}"][2:]
                g0, b0 = PHASES[f"gate{layer}"][2:]
                G = TG[f"ln1{layer}"]

                def split(g):
                    lo_turned(G + g, HG[f"ln1{layer}"] + g, XH[:, 2 * g:2 * g + 2, :],
                              XL[:, 2 * g:2 * g + 2, :])

                norm_quarter(ln1, 0)
                norm_quarter(ln1, 1)
                for q4 in range(4):
                    lo(g0 + 2 * q4)
                    split(2 * q4)
                    split(2 * q4 + 1)
                    lo(g0 + 2 * q4 + 1)
                    if q4 < 2:
                        norm_quarter(ln1, q4 + 2)

                def gate_end(b):
                    cols = slice(WB * b, WB * (b + 1))
                    n_ = 4 * layer + b + 1 + (8 if layer else 0)
                    dve.wait_ge(gate_act, n_)
                    dve.wait_ge(ple_ready, 4 * layer + 4)
                    g = GT[:, :, :, :].rearrange("p a t n -> p t a n")
                    pl = PL[:, :, cols].rearrange("p t (a n) -> p t a n", a=2)
                    link(dve.tensor_tensor(pl, pl, g, ALU.mult))
                    dve.scalar_tensor_tensor(RES[:, :, cols], RES[:, :, cols], ALPHA, PL[:, :, cols], ALU.mult,
                                             ALU.add).then_inc(acc_free, 1)

                for b in range(1, 4):
                    for j in range(8):
                        lo(g0 + 8 * b + j)
                        if j == 4:
                            gate_end(b - 1)

                def hidden(b, coef=0, i=None):
                    part, k = ("A", b) if b < FA else ("B", b - FA)
                    bb = PHASES[f"in{part}{layer}"][3] + k
                    done = (FA + FB) * layer + b
                    dve.wait_ge(silu_done, lin(done + 1, coef, i))
                    dve.wait_ge(turn_done, lin(TG[f"hid{layer}"] + b, coef, i))
                    dve.tensor_tensor(GT[:, 1], A[:, bb % 2, :, 256:512], GT[:, 0],
                                      ALU.mult).then_inc(hid_ready, 1)

                def hidden_free(b, coef=0, i=None):
                    part, k = ("A", b) if b < FA else ("B", b - FA)
                    done = (FA + FB) * layer + b
                    dve.wait_ge(hid_ready, lin(done + 1, coef, i))
                    dve.nop().then_inc(acc_free, 1)

                def hidden_lo(b, coef=0, i=None):
                    k = b if b < FA else b - FA
                    rows = bass.ds(lin(2 * k, 2 * coef, i), 2)
                    lo_turned(TG[f"hid{layer}"] + b, HG[f"hid{layer}"] + b, HH[:, rows, :],
                              HL[:, rows, :], coef, i)

                def out_end(part, b, stats):
                    bb = PHASES[f"out{part}{layer}"][3] + b
                    end(f"out{part}{layer}", b)
                    cols = slice(WB * b, WB * (b + 1))
                    dve.tensor_tensor(RES[:, :, cols], A[:, bb % 2], RES[:, :, cols], ALU.add).then_inc(acc_free, 1)
                    if stats:
                        dve.wait_ge(acc_free, bb + 1)
                        for q in range(TT):
                            last = add_stats(b, q, WB, b)
                        last.then_inc(v_step, 1)
                        step[0] += 1

                def transition():
                    dve.wait_ge(ab_turned, 1)
                    dve.wait_ge(tab_ready, 2)
                    pw = Y[:, 0, :].rearrange("p (k c n) -> p k c n", k=SUB, c=2)
                    re, im = pw[:, :, 0, :], pw[:, :, 1, :]
                    cf = Y[:, 1, 0:2 * PAIRS].rearrange("p (c n) -> p c n", c=2)
                    dve.memset(PW_T[:, 0, :], 1.0)
                    dve.memset(PW_T[:, 1, :], 0.0)
                    dve.memset(PW_T[:, 2, :], -1.0).then_inc(ab_ready, 1)
                    dve.tensor_copy(PW_T[:, 3:15:3, :], re).then_inc(ab_ready, 1)
                    dve.tensor_scalar(PW_T[:, 4:15:3, :], im, -1.0, None, ALU.mult).then_inc(ab_ready, 1)
                    dve.tensor_scalar(PW_T[:, 5:15:3, :], re, -1.0, None, ALU.mult).then_inc(ab_ready, 1)
                    dve.tensor_copy(PW_T[:, 15:17, :], cf).then_inc(ab_ready, 1)
                    dve.tensor_scalar(PW_T[:, 17, :], cf[:, 1, :], -1.0, None, ALU.mult).then_inc(ab_ready, 1)
                    dve.tensor_copy(AB[:, 0:4:3, :], re[:, SUB - 1, :].unsqueeze(1).broadcast_to([P, 2, PAIRS])).then_inc(ab_ready, 1)
                    dve.tensor_copy(AB[:, 2, :], im[:, SUB - 1, :]).then_inc(ab_ready, 1)
                    dve.tensor_scalar(AB[:, 1, :], im[:, SUB - 1, :], -1.0, None, ALU.mult).then_inc(ab_ready, 1)
                    dve.wait_ge(ab_ready, 9)

                def response_out(it):
                    dve.wait_ge(k_done, it + 1)
                    y = Y[:, it % 2, 0:TOK].rearrange("p (k s c) -> p k s c", k=2, s=SUB)
                    dst = KTAB[:, 2 * it:2 * it + 2, :, :]
                    dve.tensor_tensor(dst[:, :, 0, :], y[:, :, 0, :], DG[:, 2 * it:2 * it + 2, :], ALU.add).then_inc(k_out, 1)
                    dve.tensor_copy(dst[:, :, 1:SUB, :], y[:, :, 1:SUB, :]).then_inc(k_out, 1)

                for part, n_in, first in (("A", FA, 0), ("B", FB, FA)):
                    _, per, c0, _ = PHASES[f"in{part}{layer}"]

                    def inner(k, i):
                        for j in range(per):
                            lo(c0 + per * k + j, 2 * per, i)
                            if k == 0 and j == 4:
                                if part == "A":
                                    gate_end(3)
                                    if layer == 0:
                                        transition()
                                else:
                                    out_end("A", 3, False)
                            if k > 0 and j == 4:
                                hidden(first + k - 1, 2, i)
                            if k > 0 and j == 5:
                                hidden_free(first + k - 1, 2, i)
                            if k > 0 and j == 7:
                                hidden_lo(first + k - 1, 2, i)
                            if k == 0 and j == 7 and part == "B" and layer == 0:
                                response_out(3)
                    blocks(dve, n_in, inner)
                    nb, per, c0, _ = PHASES[f"out{part}{layer}"]
                    for b in range(nb):
                        for j in range(per):
                            lo(c0 + per * b + j)
                            if b == 0 and j == 4:
                                hidden(first + n_in - 1)
                            if b == 0 and j == 5:
                                hidden_free(first + n_in - 1)
                            if b == 0 and j == 7:
                                hidden_lo(first + n_in - 1)
                            if b and j == 4:
                                out_end(part, b - 1, part == "B")
                            if b and j == 7 and layer == 0:
                                response_out((b if part == "A" else 4 + b) - 1)
                nxt = PHASES["glu"][2] if layer == 0 else None
                if nxt is not None:
                    for j in range(4):
                        lo(nxt + j)
                out_end("B", 3, True)
                norm_scalars(4)
                if layer == 0:
                    response_out(7)

            def start_ple(layer):
                for b in range(4):
                    lo(PHASES[f"ple{layer}"][2] + b)

            start_ple(0)
            wout_end(3)
            norm_scalars(4)
            feed_forward(0)

            for q4 in range(4):
                norm_quarter(1, q4)
            dve.wait_ge(u_ready, 8)
            dve.memset(ST[:, 0, :, :], 0.0).then_inc(slot_zero, 1)
            for tile in range(1, KT, 2):
                dve.wait_ge(e_done, tile + 1)
                dve.tensor_copy(ST[:, 1:SLOTS, :, 4 * tile:4 * tile + 4].rearrange("p n c a -> p a c n"),
                                PS[:, tile % 8, :].rearrange("p (a c n) -> p a c n", a=4, c=2)[:, :, :, 0:SLOTS - 1]).then_inc(e_out_dve, 1)
            dve.wait_ge(e_out_act, 8)
            dve.wait_ge(e_out_dve, 8)
            dve.wait_ge(slot_zero, 1)
            half = PAIRS // 2
            abar = AB[:, :, :].rearrange("p (o c) n -> p o c n", o=2)
            prod = [GTf[:, 256 * h:256 * h + 4 * half].rearrange("p (o c n) -> p o c n", o=2, c=2) for h in range(2)]
            part = [GTf[:, 512 + 128 * h:512 + 128 * h + 2 * half].rearrange("p (c n) -> p c n", c=2) for h in range(2)]

            def scan_step(before, now, count, coef=0, i=None):
                for n_ in range(3):
                    for h in range(2):
                        m = slice(half * h, half * (h + 1))
                        done = count + 2 * n_ + h - 1
                        if done > 0 or i is not None:
                            dve.wait_ge(scan, lin(done, coef, i))
                        x, y = before[:, :, m], now[:, :, m]
                        if n_ == 0:
                            ins = dve.tensor_tensor(prod[h], abar[:, :, :, m], x.unsqueeze(1).broadcast_to([P, 2, 2, half]), ALU.mult)
                        elif n_ == 1:
                            ins = dve.tensor_tensor(part[h], prod[h][:, :, 0, :], prod[h][:, :, 1, :], ALU.add)
                        else:
                            ins = dve.tensor_tensor(y, y, part[h], ALU.add)
                        ins.then_inc(scan, 1)

            alone, per = 6, 8
            for n_ in range(alone):
                scan_step(ST[:, n_ + 1], ST[:, n_ + 2], 6 * n_)
            with dve.Fori(0, (SLOTS - 2 - alone) // per) as i:
                for n_ in range(per):
                    at_slot = [ST[:, bass.ds(lin(alone + n_ + k, per, i), 1)].rearrange("p a c n -> p (a c) n") for k in (1, 2)]
                    scan_step(*at_slot, 6 * (alone + n_), 6 * per, i)
            for b in range(8):
                dve.wait_ge(z_hi, b + 1)
                hi_ap = XH[:, 2 * b:2 * b + 2, :].bitcast(F32).rearrange("p k (n s) -> p k s n", s=SUB)
                dve.tensor_tensor(XL[:, 2 * b:2 * b + 2, :].rearrange("p k (n s) -> p k s n", s=SUB),
                                  PS[:, b, :].rearrange("p (k s n) -> p k s n", k=2, s=SUB), hi_ap,
                                  ALU.subtract).then_inc(z_split, 1)

            c0, b0 = PHASES["glu"][2:]

            def glu_end(b, coef=0, i=None):
                dve.wait_ge(gate_act, lin(4 + b + 1, coef, i))
                dve.tensor_tensor(GT[:, 1], A[:, (b0 + b) % 2, :, 0:256], GT[:, 0], ALU.mult).then_inc(glu_step, 1)
                dve.wait_ge(glu_step, lin(2 * b + 1, 2 * coef, i))
                cols = RES[:, :, bass.ds(lin(256 * b, 256 * coef, i), 256)]
                dve.scalar_tensor_tensor(cols, cols, ALPHA, GT[:, 1], ALU.mult, ALU.add).then_inc(acc_free, 1)
                dve.wait_ge(acc_free, lin(b0 + b + 1, coef, i))
                for q in range(TT):
                    last = dve.bn_stats(BS[:, q, bass.ds(lin(b, coef, i), 1), :].rearrange("p a b -> p (a b)"),
                                        RES[:, q, bass.ds(lin(256 * b, 256 * coef, i), 256)])
                last.then_inc(glu_step, 1)

            def glu(k, i):
                for j in range(8):
                    if not (k == 0 and j < 4):
                        lo(c0 + 8 * k + j, 16, i)
                    if k > 0 and j == 4:
                        glu_end(k - 1, 2, i)
                    if k == 7 and j == 2:
                        lo_turned(TG["p1"], HG["p1"], PH[:], PLO[:])
            blocks(dve, 8, glu)
            start_ple(1)
            glu_end(7)
            dve.wait_ge(glu_step, 16)
            norm_scalars(8)
            feed_forward(1)
            for q4 in range(4):
                norm_quarter(3, q4)

        @block.gpsimd
        def _(pool):
            count = [0]

            def link(ins):
                ins.then_inc(tab, 1)
                count[0] += 1
                pool.wait_ge(tab, count[0])

            def load_gb(n_):
                layer, which = n_ // 2, n_ % 2 + 1
                for k, name in enumerate((f"ln{which}_g", f"ln{which}_b")):
                    pool.dma_start(GB[:, k, :], t[name][layer:layer + 1, :].rearrange("a n -> (a n)").partition_broadcast(P)).then_inc(gb_in, 16)

            pool.wait_ge(w_used, PHASES["wout"][2] + 8)
            load_gb(0)
            ARE, AIM, LDT, DT, E, S, C, T0, T1, T2, T3, LDT2, INV = (S5[:, 16 + k, :] for k in range(13))
            power = [[None, None]] + [[S5[:, 8 + 2 * k + c, :] for c in range(2)] for k in range(SUB)]
            coef = [[S5[:, 2 * k + c, :] for c in range(2)] for k in range(SUB)]
            for dst, name in [(ARE, "s5_are"), (AIM, "s5_aim"), (S5[:, 18, 0:2], "s5_ldt")]:
                pool.dma_start(dst, t[name]).then_inc(late_in, 16)
            pool.wait_ge(late_in, 3 * 16)

            def tt(o, a, b, op):
                link(pool.tensor_tensor(o, a, b, op))

            def ts(o, a, s1, s2, op0, op1=None):
                if s2 is None:
                    link(pool.tensor_scalar(o, a, s1, None, op0))
                else:
                    link(pool.tensor_scalar(o, a, s1, s2, op0, op1))

            def exp(o, x):
                ln2_hi = 0.693145751953125
                ln2_lo = float(np.float32(np.log(2.0) - ln2_hi))
                ts(T0, x, -87.0, 88.0, ALU.max, ALU.min)
                ts(T1, T0, float(1 / np.log(2.0)), ROUND, ALU.mult, ALU.add)
                ts(T1, T1, -ROUND, None, ALU.add)
                ts(T2, T1, -ln2_hi, None, ALU.mult)
                tt(T0, T0, T2, ALU.add)
                ts(T2, T1, -ln2_lo, None, ALU.mult)
                tt(T0, T0, T2, ALU.add)
                ts(T2, T0, 1 / 5040.0, 1 / 720.0, ALU.mult, ALU.add)
                for c in (1 / 120.0, 1 / 24.0, 1 / 6.0, 0.5, 1.0, 1.0):
                    tt(T2, T2, T0, ALU.mult)
                    ts(T2, T2, c, None, ALU.add)
                ts(T1.bitcast(I32), T1, 127.0, float(2 ** 23), ALU.add, ALU.mult)
                tt(o, T2, T1, ALU.mult)

            def sin_cos(x):
                two_pi = 2 * np.pi
                c1 = 6.28125
                c2 = float(np.float32(np.round((two_pi - c1) * 2 ** 17) / 2 ** 17))
                c3 = float(np.round((two_pi - c1 - c2) * 2 ** 25) / 2 ** 25)
                c4 = float(np.float32(two_pi - c1 - c2 - c3))
                ts(T1, x, float(1 / two_pi), ROUND, ALU.mult, ALU.add)
                ts(T1, T1, -ROUND, None, ALU.add)
                ts(T2, T1, -c1, None, ALU.mult)
                tt(T0, x, T2, ALU.add)
                for c in (c2, c3, c4):
                    ts(T2, T1, -c, None, ALU.mult)
                    tt(T0, T0, T2, ALU.add)
                ts(T0, T0, 3.2, -3.2, ALU.min, ALU.max)
                ts(T0, T0, 0.25, None, ALU.mult)
                tt(T1, T0, T0, ALU.mult)
                ts(T2, T1, 1 / 362880.0, -1 / 5040.0, ALU.mult, ALU.add)
                for c in (1 / 120.0, -1 / 6.0, 1.0):
                    tt(T2, T2, T1, ALU.mult)
                    ts(T2, T2, c, None, ALU.add)
                tt(S, T2, T0, ALU.mult)
                ts(T2, T1, 1 / 40320.0, -1 / 720.0, ALU.mult, ALU.add)
                for c in (1 / 24.0, -0.5, 1.0):
                    tt(T2, T2, T1, ALU.mult)
                    ts(T2, T2, c, None, ALU.add)
                tt(T3, S, T2, ALU.mult)
                tt(T1, S, S, ALU.mult)
                ts(T2, T1, -2.0, 1.0, ALU.mult, ALU.add)
                ts(T3, T3, 2.0, None, ALU.mult)
                tt(S, T3, T2, ALU.mult)
                ts(S, S, 2.0, None, ALU.mult)
                tt(T1, T3, T3, ALU.mult)
                ts(C, T1, -2.0, 1.0, ALU.mult, ALU.add)

            link(pool.tensor_copy(LDT2.rearrange("r (s n) -> r s n", s=2),
                                  S5[:, 18, 0:2].unsqueeze(2).broadcast_to([64, 2, 64])))
            exp(DT, LDT2)
            tt(T3, ARE, DT, ALU.mult)
            exp(E, T3)
            tt(LDT2, AIM, DT, ALU.mult)
            sin_cos(LDT2)
            tt(power[1][0], E, C, ALU.mult)
            tt(power[1][1], E, S, ALU.mult)

            def product(o, a, b):
                tt(T0, a[0], b[0], ALU.mult)
                tt(T1, a[1], b[1], ALU.mult)
                tt(o[0], T0, T1, ALU.subtract)
                tt(T0, a[0], b[1], ALU.mult)
                tt(T1, a[1], b[0], ALU.mult)
                tt(o[1], T0, T1, ALU.add)

            product(power[2], power[1], power[1])
            product(power[3], power[2], power[1])
            product(power[4], power[2], power[2])
            tt(T0, ARE, ARE, ALU.mult)
            tt(T1, AIM, AIM, ALU.mult)
            tt(T0, T0, T1, ALU.add)
            link(pool.tensor_copy(T1, T0.bitcast(I32)))
            ts(INV.bitcast(I32), T1, -1.0, float(0x7EF311C3), ALU.mult, ALU.add)
            for _ in range(4):
                tt(T1, T0, INV, ALU.mult)
                ts(T1, T1, -1.0, 2.0, ALU.mult, ALU.add)
                tt(INV, INV, T1, ALU.mult)
            ts(T3, power[1][0], -1.0, None, ALU.add)
            tt(T0, T3, ARE, ALU.mult)
            tt(T1, power[1][1], AIM, ALU.mult)
            tt(T0, T0, T1, ALU.add)
            tt(coef[3][0], T0, INV, ALU.mult)
            tt(T0, power[1][1], ARE, ALU.mult)
            tt(T1, T3, AIM, ALU.mult)
            tt(T0, T0, T1, ALU.subtract)
            tt(coef[3][1], T0, INV, ALU.mult)
            for k in (2, 1, 0):
                product(coef[k], coef[3], power[3 - k])
            pool.sem_inc(tab_ready, 1)
            pool.dma_start(coef_dram, S5[:, 0:8, :].rearrange("r k n -> r (k n)")).then_inc(coef_out, 16)
            pool.wait_ge(coef_out, 16)
            pool.sem_inc(tab_ready, 1)

            pool.wait_ge(w_used, PHASES["inA0"][2] + 8)
            n_raw = [0, 0]

            def input_matrices(tile):
                if tile:
                    pool.wait_ge(e_stored, 16 * tile)
                for s in range(SUB):
                    src = coef_dram[4 * tile:4 * tile + 4, 2 * P * s:2 * P * (s + 1)].partition_broadcast(PW)
                    pool.dma_start(EC[PW * s:PW * (s + 1)].rearrange("p a c n -> p a (c n)"), src).then_inc(e_raw, 16)
                pool.dma_start(EB[:], t["s5_b"][:, 4 * tile:4 * tile + 4]).then_inc(e_raw, 16)
                pool.wait_ge(e_raw, 5 * 16 * (tile + 1))
                cr, ci, br, bi = EC[:, :, 0], EC[:, :, 1], EB[:, :, 0], EB[:, :, 1]
                tt(ET[:], cr, br, ALU.mult)
                tt(EO[:, :, 0], ci, bi, ALU.mult)
                tt(EO[:, :, 0], ET[:], EO[:, :, 0], ALU.subtract)
                tt(ET[:], cr, bi, ALU.mult)
                tt(EO[:, :, 1], ci, br, ALU.mult)
                tt(EO[:, :, 1], ET[:], EO[:, :, 1], ALU.add)
                pool.dma_start(e_dram[tile], EO[:].rearrange("p a c n -> p (a c n)")).then_inc(e_stored, 16)

            def output_matrices(it):
                pairs = slice(8 * it, 8 * it + 8)
                if it:
                    pool.wait_ge(k_done, it)
                    pool.wait_ge(c_stored, 4 * 16 * it)
                pool.dma_start(CR[:], t["s5_c"][:, pairs]).then_inc(c_raw, 16)
                pool.dma_start(BR[:], t["s5_bt"][:, pairs]).then_inc(c_raw, 16)
                if it == 0:
                    pool.dma_start(DG[:], t["s5_skip"]).then_inc(c_raw, 16)
                pool.wait_ge(c_raw, 16 * (2 * it + 3))
                shape = [P, 8, SUB + 1, PW]
                re, nim, nre = (PW_T[:, k:15:3, pairs].rearrange("p k a -> p a k").unsqueeze(3).broadcast_to(shape) for k in range(3))
                cr, ci = (CR[:, :, k, :].unsqueeze(2).broadcast_to(shape) for k in range(2))
                tt(CT[:], cr, re, ALU.mult)
                tt(CO[:, 0], ci, nim, ALU.mult)
                tt(CO[:, 0], CT[:], CO[:, 0], ALU.add)
                tt(CT[:], cr, nim, ALU.mult)
                tt(CO[:, 1], ci, nre, ALU.mult)
                tt(CO[:, 1], CT[:], CO[:, 1], ALU.add)
                kr, ki, nki = (PW_T[:, k, pairs].unsqueeze(2).broadcast_to([P, 8, PW]) for k in (15, 16, 17))
                tt(BX[:], BR[:, :, 0], kr, ALU.mult)
                tt(BT[:, :, 0], BR[:, :, 1], nki, ALU.mult)
                tt(BT[:, :, 0], BX[:], BT[:, :, 0], ALU.add)
                tt(BX[:], BR[:, :, 0], ki, ALU.mult)
                tt(BT[:, :, 1], BR[:, :, 1], kr, ALU.mult)
                tt(BT[:, :, 1], BX[:], BT[:, :, 1], ALU.add)
                pool.sem_inc(k_input, 1)
                for k in range(2):
                    for c in range(2):
                        dst = c_dram[2 * it + k].rearrange("p (a c n) -> p a c n", a=4, c=2)[:, :, c, :]
                        pool.dma_start(dst, CO[:, c, 4 * k:4 * k + 4, 1:, :].rearrange("p a s n -> p a (s n)")).then_inc(c_stored, 16)

            for tile in range(8):
                input_matrices(tile)
            pool.wait_ge(e_stored, 8 * 16)
            for it in range(4):
                output_matrices(it)
            pool.wait_ge(k_done, 4)
            pool.wait_ge(c_stored, 4 * 4 * 16)
            for tile in range(8, KT):
                input_matrices(tile)
            pool.wait_ge(e_stored, KT * 16)
            for it in range(4, 8):
                output_matrices(it)

            pool.wait_ge(ln_quarter, 4)
            load_gb(1)
            pool.wait_ge(w_used, PHASES["outB0"][2] + 1)
            pool.memset(KK[:], 0.0).then_inc(kk_zero, 1)
            pool.wait_ge(kk_zero, 1)
            pool.wait_ge(k_out, 2 * 8)
            for s in range(SUB):
                for r in range(4):
                    pool.dma_start(KK[PW * s:PW * (s + 1), r::4, PW * s:P],
                                   KTAB[PW * r:PW * (r + 1), :, 0:SUB - s, :].rearrange("p k s n -> p k (s n)")).then_inc(kk_in, 16)
            pool.wait_ge(y_done, KT)
            pool.dma_start(PK[:], t["p"][1].rearrange("(t p) n -> p t n", p=P)).then_inc(p1_in, 16)
            load_gb(2)
            pool.wait_ge(ln_quarter, 12)
            load_gb(3)
            ov = out.rearrange("(t p) n -> p t n", p=P)
            for q4 in range(4):
                pool.wait_ge(ln_quarter, 12 + q4 + 1)
                cols = slice(WB * q4, WB * (q4 + 1))
                pool.dma_start(ov[:, :, cols], RES[:, :, cols]).then_inc(stored, 16)
            pool.wait_ge(stored, 64)


def chunks(w, cols):
    parts = []
    for ranges in cols:
        b = np.concatenate([w[:, a:e] for a, e in ranges], axis=1)
        r, n = b.shape
        parts.append(b.reshape(r // 256, 2, 128, n).transpose(0, 2, 1, 3).reshape(r // 256, 128, 2 * n))
    return np.ascontiguousarray(np.concatenate(parts, axis=0))


def kernel(**inputs):
    import concourse.bacc as bacc
    from concourse.bass_utils import run_bass_kernel_spmd as run

    a = {k: np.asarray(v) for k, v in inputs.items()}
    arr = {"x": a["x"][0], "p": a["p"][:, 0]}
    w = a["attn_w_in"][0]
    lat, qd, kd, vd = 0, 2 * LAT + ROPE, 2 * LAT + ROPE + 1024, 2 * LAT + ROPE + 2048
    starts = [lat, LAT, qd, qd + WB, kd, kd + WB, vd, vd + WB]
    arr["w_in"] = chunks(w, [[(s, s + WB)] for s in starts])
    arr["w_kpe"] = chunks(w, [[(2 * LAT, 2 * LAT + ROPE)]])
    wq = a["mla_w_q_b"][0].reshape(LAT, HEADS, HD + ROPE)
    wq = np.concatenate([wq[:, :, :HD].reshape(LAT, -1), wq[:, :, HD:].reshape(LAT, -1)], axis=1)
    arr["w_qb"] = chunks(wq, [[(WB * b, WB * (b + 1))] for b in range(3)])
    wk = a["mla_w_kv_b"][0].reshape(LAT, HEADS, 2 * HD)
    wk = np.concatenate([wk[:, :, :HD].reshape(LAT, -1), wk[:, :, HD:].reshape(LAT, -1)], axis=1)
    arr["w_kvb"] = chunks(wk, [[(WB * b, WB * (b + 1))] for b in range(4)])
    wo = a["attn_w_out"][0]
    arr["w_out"] = chunks(np.concatenate([wo[1024:], wo[:1024]], axis=0), [[(WB * b, WB * (b + 1))] for b in range(4)])
    wg = a["s5_w_glu"][0].reshape(2, 8, 128, 2 * D).transpose(1, 0, 2, 3).reshape(D, 2 * D)
    arr["w_glu"] = chunks(wg, [[(256 * b, 256 * (b + 1)), (D + 256 * b, D + 256 * (b + 1))] for b in range(8)])
    four = [[(WB * b, WB * (b + 1))] for b in range(4)]
    for l in range(LAYERS):
        arr[f"w_ple{l}"] = chunks(a["ple_w"][l], four)
        arr[f"w_gate{l}"] = chunks(a["ple_gate_w"][l], four)
        for part, first, n in (("A", 0, FA), ("B", FA, FB)):
            arr[f"w_in{part}{l}"] = chunks(a["ffn_w_in"][l], [[(256 * b, 256 * (b + 1)), (FFN + 256 * b, FFN + 256 * (b + 1))]
                                                              for b in range(first, first + n)])
            arr[f"w_out{part}{l}"] = chunks(a["ffn_w_out"][l][256 * first:256 * (first + n)], four)
    for k in ("ln1_g", "ln1_b", "ln2_g", "ln2_b"):
        arr[k] = a[k]
    arr["norm_gain"] = np.concatenate([a["mla_q_norm"][0], a["mla_kv_norm"][0]])
    arr["pos"] = np.ascontiguousarray(a["positions"][0].reshape(TT, P).T)
    arr["s5_are"] = a["s5_a_re"][0].reshape(PAIRS, P)
    arr["s5_aim"] = a["s5_a_im"][0].reshape(PAIRS, P)
    arr["s5_ldt"] = a["s5_log_dt"][0].reshape(PAIRS, 2)
    b4 = np.zeros((SUB, 2, GROUP, PAIRS, 2, 2, 64), a["s5_b_re"].dtype)
    c = np.zeros((2, 64, PAIRS, 2, 2, GROUP), a["s5_c_re"].dtype)
    bt = np.zeros((2, 64, PAIRS, 2, 2, GROUP), a["s5_b_re"].dtype)
    for n, k in enumerate(("re", "im")):
        bk = a[f"s5_b_{k}"][0].reshape(PAIRS, 2, 64, GROUP)
        ck = a[f"s5_c_{k}"][0].reshape(PAIRS, 2, GROUP, 64)
        for g in range(2):
            b4[:, g, :, :, n, g, :] = bk[:, g].transpose(2, 0, 1)[None]
            bt[g, :, :, n, g, :] = bk[:, g].transpose(1, 0, 2)
            c[g, :, :, n, g, :] = ck[:, g].transpose(2, 0, 1)
    arr["s5_b"] = b4.reshape(P, PAIRS, 2, P)
    arr["s5_c"] = c.reshape(P, PAIRS, 2, 2 * GROUP)
    arr["s5_bt"] = bt.reshape(P, PAIRS, 2, 2 * GROUP)
    d = np.zeros((4, PW, KT, PW), a["s5_d"].dtype)
    for n in range(PW):
        d[:, n, :, n] = a["s5_d"][0].reshape(KT, 4, PW)[:, :, n].T
    arr["s5_skip"] = d.reshape(P, KT, PW)
    arr["ident"] = np.eye(P, dtype=np.float32)
    arr["inv_freq"] = np.float32(10000.0) ** (-np.arange(HALF, dtype=np.float32) / np.float32(HALF))
    q = np.concatenate([np.arange(P)[:, None] + np.zeros((1, P), int), P + np.arange(P)[:, None] + np.zeros((1, 2 * P), int)], axis=1)
    key = np.concatenate([np.arange(P), np.arange(2 * P)])[None, :]
    dist = q - key
    n = ((dist >= 0) & (dist <= 128)) * 1.0 + ((dist >= 0) & (dist % 4 == 0)) + ((dist >= 0) & (dist % 16 == 0))
    arr["branches"] = n.astype(np.float32)
    arr["neg_dist"] = np.where(n > 0, -dist, -1e34).astype(np.float32)
    arr["causal"] = np.where(dist >= 0, 0.0, -1e30).astype(np.float32)

    nc = bacc.Bacc("TRN2", target_bir_lowering=False, num_devices=1)
    arr = {k: np.ascontiguousarray(v) for k, v in arr.items()}
    t = {k: nc.dram_tensor(f"in_{k}", v.shape, mybir.dt.from_np(v.dtype), kind="ExternalInput").ap() for k, v in arr.items()}
    out = nc.dram_tensor("out_h", (TOK, D), F32, kind="ExternalOutput").ap()
    build(nc, t, out)
    r = run(nc, [{f"in_{k}": v for k, v in arr.items()}], core_ids=[0])
    return r.results[0]["out_h"].reshape(1, TOK, D)
```

```python
from contextlib import ExitStack

import numpy as np

import concourse.bass as bass
from concourse import mybir

F32 = mybir.dt.float32
F32R = mybir.dt.float32r
I32 = mybir.dt.int32
ALU = mybir.AluOpType
ACT = mybir.ActivationFunctionType
AX_X = mybir.AxisListType.X

P = 128
TOK = 256
TT = TOK // P
D = 2048
KT = D // P
WB = 512
RING = 4
LAT = 512
HEADS = 8
HD = 128
ROPE = 64
HALF = ROPE // 2
FFN = 5632
FA, FB = 12, 10
PLE = 256
LAYERS = 2
ALPHA = float((2.0 * LAYERS) ** 0.25)
MLA_SCALE = float((HD + ROPE) ** -0.5)
DIL_SCALE = float(HD ** -0.5)
SLOPES = [2.0 ** (-(h + 1)) for h in range(HEADS)]
GROUP = 16
PAIRS = D // GROUP // 2
SUB = 4
SLOTS = TOK // SUB
PW = 2 * GROUP
ROUND = 12582912.0

PHASES = {}
_c = _b = 0
for _name, _n, _per in [("win", 8, 8), ("kpe", 1, 8), ("qb", 3, 2), ("kvb", 4, 2), ("wout", 4, 8),
                        ("ple0", 4, 1), ("gate0", 4, 8), ("inA0", FA, 8), ("outA0", 4, FA), ("inB0", FB, 8), ("outB0", 4, FB),
                        ("glu", 8, 8),
                        ("ple1", 4, 1), ("gate1", 4, 8), ("inA1", FA, 8), ("outA1", 4, FA), ("inB1", FB, 8), ("outB1", 4, FB)]:
    PHASES[_name] = (_n, _per, _c, _b)
    _c += _n * _per
    _b += _n if not _name.startswith("ple") else 0


def lin(const, coef=0, i=None):
    return const if i is None else i * coef + const


def blocks(eng, n, body):
    body(0, None)
    if n >= 6:
        with eng.Fori(0, (n - 2) // 2) as i:
            body(1, i)
            body(2, i)
    else:
        for k in range(1, n - 1):
            body(k, None)
    body(n - 1, None)


def build(nc, t, out):
    KB = 1024
    base = 16512
    with ExitStack() as ctx:
        def at(name, shape, kb, dt=F32):
            return nc.alloc_sbuf_tensor_at(name, shape, dt, offset=base + int(kb * KB))

        def sem(name):
            return ctx.enter_context(nc.semaphore(name))

        RAW = at("raw", [P, RING, 2, WB], 0)
        WH = at("w_hi", [P, RING, 2, WB], 16, F32R)
        WL = at("w_lo", [P, RING, 2, WB], 32, F32R)
        XH = at("x_hi", [P, KT, TOK], 48, F32R)
        XL = at("x_lo", [P, KT, TOK], 64, F32R)
        RES = at("res", [P, TT, D], 80)
        GB = at("gb", [P, 2, D], 96)
        HH = at("hid_hi", [P, 2 * FA, TOK], 112, F32R)
        HL = at("hid_lo", [P, 2 * FA, TOK], 136, F32R)
        PL = at("ple", [P, TT, D], 160)
        QK = at("qk_dil", [P, 2 * HEADS, TOK], 96)
        VD = at("v_dil", [P, TT, HEADS * HD], 112)
        LH = at("lat_hi", [P, 8, TOK], 120, F32R)
        LL = at("lat_lo", [P, 8, TOK], 128, F32R)
        QN = at("q_nope", [P, HEADS, TOK], 136)
        QP = at("q_pe", [P, HEADS // 2, TOK], 144)
        KP = at("k_pe", [P, TOK], 148)
        KN = at("k_nope", [P, HEADS, TOK], 152)
        VM = at("v_mla", [P, TT, HEADS * HD], 160)
        STG = at("stage", [P, 2, TT, WB], 168)
        SM = at("s_masked", [P, 2, 3 * P], 176)
        PR = at("probs", [P, 2, 3 * P], 179)
        PT = at("probs_t", [P, 2, 3 * P], 182)
        NG = at("norm_gain", [P, 2 * LAT], 185)
        CS = at("cos_sin", [P, 2, TT, HALF], 189)
        AT = at("angle_tmp", [P, 4, TT, HALF], 190)
        S5 = at("s5_small", [PAIRS, 32, P], 144)
        EC = [at(f"s5_coef{n}", [P, 4, 2, P], 160 + 8 * n) for n in range(2)]
        EB = [at(f"s5_b{n}", [P, 4, 2, P], 164 + 8 * n) for n in range(2)]
        ET = at("s5_e_tmp", [P, 4, P], 176)
        EO = at("s5_e", [P, 4, 2, P], 178)
        CO = at("s5_c_pow", [P, 2, 8, SUB + 1, PW], 160)
        CR = at("s5_c", [P, 8, 2, PW], 170)
        CT = at("s5_c_tmp", [P, 8, SUB + 1, PW], 172)
        BR = at("s5_bt_raw", [P, 8, 2, PW], 177)
        BT = at("s5_bt", [P, 8, 2, PW], 179)
        BX = at("s5_bt_tmp", [P, 8, PW], 181)
        DG = at("s5_skip", [P, KT, PW], 182)
        KTAB = at("s5_k", [P, KT, SUB, PW], 184)
        PW_T = at("s5_pow", [P, 18, PAIRS], 192.5)
        KK = at("s5_toeplitz", [P, PAIRS, P], 48)
        H4 = at("h_steps", [SLOTS, PAIRS, SUB, PW], 112)
        HQ = [at(f"h_quarter{n}", [SLOTS, SUB, WB], kb) for n, kb in enumerate((192.5, 176))]
        ST = at("states", [P, SLOTS, 2, PAIRS], 112)
        U4 = at("u", [P, PAIRS, SLOTS], 144)
        EM = [at(f"e_slots{n}", [SLOTS, 4, 2, P], 96 + 4 * n) for n in range(2)]
        Z4 = at("z", [P, 8, WB], 144)
        slot_kb = [160, 164, 168, 172, 176, 180, 96, 100, 104, 108]
        TS = [at(f"s5_table{n}", [P, 4, 2, P], kb) for n, kb in enumerate(slot_kb)]
        PK = at("p_tok", [P, TT, PLE], 160)
        ID = at("ident", [P, P], 192)
        B0 = at("dil_bias_first", [P, 2, 3 * P], 192.5)
        B2 = at("dil_bias_rest", [P, HEADS - 2, 3 * P], 120)
        CM = at("causal", [P, 3 * P], 195.5)
        GT = at("gated", [P, 2, TT, 256], 197)
        AB = at("a_bar", [P, 4, PAIRS], 201)
        PH = at("p_hi", [P, 2, TOK], 202, F32R)
        PLO = at("p_lo", [P, 2, TOK], 204, F32R)
        BS = at("bn_stats", [P, TT, 8, 6], 206)
        MV = at("mean_var", [P, TT, 2], 206.5)
        SC = at("small", [P, 24], 206.625)
        SI = at("small_int", [P, 8], 206.75, I32)
        PI = at("positions", [P, TT], 206.875, I32)
        MX = at("row_max", [P, 2, 4], 206.9375)
        GTf = GT[:, :, :, :].rearrange("p a t n -> p (a t n)")

        PS = ctx.enter_context(nc.psum_tensor("ps", [P, 8, WB], F32))
        A = PS[:, 0:4, :].rearrange("p (a t) n -> p a t n", t=TT)
        TP = PS[:, 4:6, :].rearrange("p a (k n) -> p a k n", k=2)
        Y = PS[:, 6:8, :]

        coef_dram = nc.dram_tensor("s5_coef_dram", (PAIRS, SUB * 2 * P), F32, kind="Internal").ap()
        e_dram = nc.dram_tensor("s5_e_dram", (KT, P, 4 * 2 * P), F32, kind="Internal").ap()
        c_dram = nc.dram_tensor("s5_c_dram", (KT, P, 4 * 2 * P), F32, kind="Internal").ap()

        def states_of(tile):
            return ST[:, 1:SLOTS, :, 4 * tile:4 * tile + 4].rearrange("p n c a -> p a c n")

        def turned_of(tile):
            return PS[:, 4 + tile % 4, :].rearrange("p (a c n) -> p a c n", a=4, c=2)[:, :, :, 0:SLOTS - 1]

        raw_full = [sem(f"raw_full{s}") for s in range(RING)]
        hi_ready, lo_ready, w_used = sem("hi_ready"), sem("lo_ready"), sem("w_used")
        x_in = [sem(f"x_in{n}") for n in range(4)]
        bias_in = sem("bias_in")
        ident_in, p_in, p1_in, const_in, gb_in, late_in = sem("ident_in"), sem("p_in"), sem("p1_in"), sem("const_in"), sem("gb_in"), sem("late_in")
        acc_free = sem("acc_free")
        turn_done = sem("turn_done")
        turn_hi = sem("turn_hi")
        turned = sem("turned")
        staged = sem("staged")
        v_step = sem("v_step")
        sq_sum = sem("sq_sum")
        trig = sem("trig")
        s_done, s_masked, nmax, p_exp, p_ready = sem("s_done"), sem("s_masked"), sem("nmax"), sem("p_exp"), sem("p_ready")
        p_turned, pt_ready, pv_done, mix_hi, mix_ready = sem("p_turned"), sem("pt_ready"), sem("pv_done"), sem("mix_hi"), sem("mix_ready")
        ln_quarter = sem("ln_quarter")
        ln_scalars = sem("ln_scalars")
        ln_act, ln_pool = sem("ln_act"), sem("ln_pool")
        ple_ready, gate_act, silu_done, hid_ready = sem("ple_ready"), sem("gate_act"), sem("silu_done"), sem("hid_ready")
        glu_step = sem("glu_step")
        tab, tab_ready, coef_out, ab_turned, ab_ready = sem("tab"), sem("tab_ready"), sem("coef_out"), sem("ab_turned"), sem("ab_ready")
        e_raw = [sem("e_raw0"), sem("e_raw1")]
        e_stored, c_raw, c_stored = sem("e_stored"), sem("c_raw"), sem("c_stored")
        k_input, k_done, k_out, kk_zero, kk_in = sem("k_input"), sem("k_done"), sem("k_out"), sem("kk_zero"), sem("kk_in")
        h4_in, h4_split, u_turned, u_ready, slot_zero = [sem("h4_in0"), sem("h4_in1")], sem("h4_split"), sem("u_turned"), sem("u_ready"), sem("slot_zero")
        ts_in = [sem(f"ts_in{n}") for n in range(10)]
        e_done, e_mid, e_turned, e_out_act, e_out_dve = sem("e_done"), sem("e_mid"), sem("e_turned"), sem("e_out_act"), sem("e_out_dve")
        scan = [sem("scan_low"), sem("scan_high")]
        y_done, z_half, z_act, z_turned, z_hi, z_split = sem("y_done"), sem("z_half"), sem("z_act"), sem("z_turned"), sem("z_hi"), sem("z_split")
        stored = sem("stored")

        TG = {}
        n = 0
        for name, count in [("x", 8), ("p0", 1), ("lat", 4), ("qk", 8), ("kpe", 1), ("qn", 4), ("qp", 2), ("kn", 4),
                            ("ln10", 8), ("hid0", FA + FB), ("p1", 1), ("ln11", 8),
                            ("hid1", FA + FB)]:
            TG[name] = n
            n += count
        HG = {}
        n = 0
        for name, count in [("x", 8), ("p0", 1), ("lat", 4), ("ln10", 8), ("hid0", FA + FB), ("p1", 1), ("ln11", 8),
                            ("hid1", FA + FB)]:
            HG[name] = n
            n += count

        def quarter_normed(eng, n_):
            eng.wait_ge(ln_quarter, n_)
            by_pool = 3 * ((n_ - 1) // 4 - 1) + (n_ - 1) % 4
            if by_pool > 0:
                eng.wait_ge(ln_pool, by_pool)

        block = ctx.enter_context(nc.Block())

        @block.sync
        def _(sp):
            xv = t["x"].rearrange("(t p) n -> p t n", p=P)

            def load_x(q4):
                cols = slice(WB * q4, WB * (q4 + 1))
                sp.dma_start(RES[:, :, cols], xv[:, :, cols]).then_inc(x_in[q4], 16)

            load_x(0)
            load_x(1)

            def load(w, local, c, coef, i, width):
                if c >= RING:
                    sp.wait_ge(lo_ready, lin(c - RING + 1, coef, i))
                src = w[bass.ds(lin(local, coef, i), 1)].rearrange("a p (k n) -> (a p) k n", k=2)
                sp.dma_start(RAW[:, c % RING, :, 0:width], src).then_inc(raw_full[c % RING], 16)

            def phase(name, weight, width=WB, first=0):
                nb, per, c0, _ = PHASES[name]
                w, total = t[weight], nb * per
                if c0 == 0:
                    for j in range(first):
                        load(w, j, j, 0, None, width)
                        if j < 2:
                            load_x(2 + j)
                if (total - first) % RING:
                    for j in range(first, total):
                        load(w, j, c0 + j, 0, None, width)
                elif total - first == RING:
                    for j in range(first, total):
                        load(w, j, c0 + j, 0, None, width)
                else:
                    with sp.Fori(0, (total - first) // RING) as i:
                        for j in range(RING):
                            load(w, first + j, c0 + first + j, RING, i, width)

            def s5_loads():
                def glu_chunks(first, last):
                    for j in range(first, last):
                        load(t["w_glu"], j, PHASES["glu"][2] + j, 0, None, WB)

                def input_table(tile):
                    sp.dma_start(TS[tile % 6][:], e_dram[tile].rearrange("p (a c n) -> p a c n", a=4, c=2)).then_inc(ts_in[tile % 6], 16)

                glu_chunks(0, RING)
                for tile in range(4):
                    if tile == 0:
                        sp.wait_ge(e_stored, 16 * 16)
                        sp.wait_ge(k_done, 8)
                        sp.wait_ge(c_stored, 4 * 16 * 8)
                        sp.wait_ge(k_out, 2 * 8)
                    input_table(tile)
                glu_chunks(RING, 2 * RING - 1)
                sp.wait_ge(w_used, PHASES["glu"][2])
                for q4 in range(4):
                    quarter_normed(sp, 4 + q4 + 1)
                    if q4 >= 2:
                        sp.wait_ge(h4_split, q4 - 1)
                    cols = slice(WB * q4, WB * (q4 + 1))
                    for q in range(TT):
                        sp.dma_start(HQ[q4 % 2][32 * q:32 * q + 32, :, :], RES[:, q, cols]).then_inc(h4_in[q4 % 2], 16)
                glu_chunks(2 * RING - 1, 2 * RING)
                sp.wait_ge(h4_split, 4)
                for tile in range(4, KT):
                    if tile >= 6:
                        sp.wait_ge(e_done, tile - 5)
                    input_table(tile)
                for n in range(KT):
                    if n < 6:
                        sp.wait_ge(e_done, KT)
                    elif n == 6:
                        sp.wait_ge(e_turned, KT)
                    elif n >= 10:
                        sp.wait_ge(y_done, n - 9)
                    sp.dma_start(TS[n % 10][:], c_dram[n].rearrange("p (a c n) -> p a c n", a=4, c=2)).then_inc(ts_in[n % 10], 16)

            phase("win", "w_in", first=RING)
            phase("kpe", "w_kpe", ROPE)
            phase("qb", "w_qb")
            phase("kvb", "w_kvb")
            phase("wout", "w_out")
            for layer in range(LAYERS):
                if layer:
                    s5_loads()
                    phase("glu", "w_glu", first=2 * RING)
                for name in ("ple", "gate", "inA", "outA", "inB", "outB"):
                    phase(f"{name}{layer}", f"w_{name}{layer}")
            ov = out.rearrange("(t p) n -> p t n", p=P)
            for q4 in range(4):
                quarter_normed(sp, 12 + q4 + 1)
                cols = slice(WB * q4, WB * (q4 + 1))
                sp.dma_start(ov[:, :, cols], RES[:, :, cols]).then_inc(stored, 16)
            sp.wait_ge(stored, 64)

        @block.tensor
        def _(pe):
            def chunk(c, coef, i, hi, lo, kt, depth, acc, width=WB):
                pe.wait_ge(lo_ready, lin(c + 1, coef, i))
                s = c % RING
                for k in range(2):
                    for q in range(TT):
                        cols = slice(q * P, (q + 1) * P)
                        o = A[:, acc, q, 0:width]
                        pe.matmul(o, hi[:, kt + k, cols], WH[:, s, k, 0:width], start=(kt + k == 0), stop=False)
                        pe.matmul(o, hi[:, kt + k, cols], WL[:, s, k, 0:width], start=False, stop=False)
                        last = pe.matmul(o, lo[:, kt + k, cols], WH[:, s, k, 0:width], start=False,
                                         stop=(kt + k == depth - 1))
                last.then_inc(w_used, 1)

            def acc_ready(b, coef=0, i=None):
                if b >= 2:
                    pe.wait_ge(acc_free, lin(b - 1, coef, i))

            def turn(g, src, col, coef=0, i=None):
                if g >= 2:
                    pe.wait_ge(turned, lin(g - 1, coef, i))
                for k in range(2):
                    for q in range(TT):
                        last = pe.transpose(TP[:, g % 2, k, q * P:(q + 1) * P],
                                            src[:, q, col + k * P:col + (k + 1) * P], ID[:])
                last.then_inc(turn_done, 1)

            pe.wait_ge(ident_in, 16)

            def turn_x(g):
                if g % 2 == 0:
                    pe.wait_ge(x_in[g // 2], 16)
                turn(TG["x"] + g, RES[:], 256 * g)

            turn_x(0)
            turn_x(1)

            _, per, c0, b0 = PHASES["win"]
            for b in range(8):
                acc_ready(b0 + b)
                for j in range(per):
                    if b == 0:
                        if j < 6:
                            turn_x(j + 2)
                        elif j == 6:
                            pe.wait_ge(p_in, 16)
                            turn(TG["p0"], PK[:], 0)
                        pe.wait_ge(turned, TG["x"] + j + 1)
                    chunk(c0 + per * b + j, 0, None, XH, XL, 2 * j, KT, (b0 + b) % 2)
                    if j == 3 and 1 <= b <= 6:
                        pe.wait_ge(staged, b)
                        first = TG["lat"] + 2 * (b - 1) if b <= 2 else TG["qk"] + 2 * (b - 3)
                        for g in range(2):
                            turn(first + g, STG[:, (b - 1) % 2], 256 * g)
            _, per, c0, b0 = PHASES["kpe"]
            acc_ready(b0)
            for j in range(per):
                chunk(c0 + j, 0, None, XH, XL, 2 * j, KT, b0 % 2, ROPE)

            QB, KVB = PHASES["qb"], PHASES["kvb"]
            groups = [TG["kpe"], TG["qn"], TG["qn"] + 2, TG["qp"], TG["kn"], TG["kn"] + 2]

            def turn_up(m):
                pe.wait_ge(staged, 7 + m)
                if m == 0:
                    g = TG["kpe"]
                    pe.wait_ge(turned, g - 1)
                    for q in range(TT):
                        last = pe.transpose(TP[:, g % 2, 0, q * P:(q + 1) * P], STG[:, 0, q, 0:P], ID[:])
                    last.then_inc(turn_done, 1)
                else:
                    for g in range(2):
                        turn(groups[m] + g, STG[:, m % 2], 256 * g)

            pe.wait_ge(turned, TG["qk"])
            for b in range(7):
                acc_ready(QB[3] + b)
                for j in range(2):
                    row = 2 * j
                    part = slice(0, 4) if b < 3 else slice(4, 8)
                    chunk(QB[2] + 2 * b + j, 0, None, LH[:, part], LL[:, part], row, 4, (QB[3] + b) % 2)
                if b >= 1 and b <= 6:
                    turn_up(b - 1)

            pe.wait_ge(acc_free, QB[3] + 7)
            pe.wait_ge(turned, TG["ln10"])

            def scores(h):
                if h >= 2:
                    pe.wait_ge(s_masked, h - 1)
                dst = A[:, 0, h % 2]
                for q in range(TT):
                    cols = slice(0, P) if q == 0 else slice(P, 3 * P)
                    keys = slice(0, (q + 1) * P)
                    rows = slice(q * P, (q + 1) * P)
                    if h < HEADS:
                        last = pe.matmul(dst[:, cols], QK[:, h, rows], QK[:, HEADS + h, keys], start=True, stop=True)
                    else:
                        m = h - HEADS
                        half = slice(ROPE * (m % 2), ROPE * (m % 2) + ROPE)
                        pe.matmul(dst[:, cols], QN[:, m, rows], KN[:, m, keys], start=True, stop=False)
                        last = pe.matmul(dst[:, cols], QP[half, m // 2, rows], KP[half, keys], start=False, stop=True)
                last.then_inc(s_done, 1)

            def turn_probs(h):
                pe.wait_ge(p_ready, h + 1)
                if h >= 2:
                    pe.wait_ge(pt_ready, h - 1)
                for n_, s in enumerate([0, 1, 2]):
                    last = pe.transpose(Y[:, h % 2, n_ * P:(n_ + 1) * P], PR[:, h % 2, s * P:(s + 1) * P], ID[:])
                last.then_inc(p_turned, 1)

            def values(h):
                pe.wait_ge(pt_ready, h + 1)
                if h >= 2:
                    pe.wait_ge(mix_ready, h - 1)
                v = VD if h < HEADS else VM
                d = slice((h % HEADS) * HD, (h % HEADS + 1) * HD)
                pe.matmul(A[:, 1, h % 2, 0:TOK], v[:, 0, d], PT[:, h % 2, 0:TOK], start=True, stop=False)
                pe.matmul(A[:, 1, h % 2, P:TOK], v[:, 1, d], PT[:, h % 2, TOK:3 * P], start=False,
                          stop=True).then_inc(pv_done, 1)

            scores(0)
            for s in range(2 * HEADS + 3):
                if s + 1 < 2 * HEADS:
                    scores(s + 1)
                if s >= 3:
                    values(s - 3)
                if 1 <= s <= 2 * HEADS:
                    turn_probs(s - 1)

            _, per, c0, b0 = PHASES["wout"]
            for b in range(4):
                if b:
                    acc_ready(b0 + b)
                for j in range(per):
                    if b == 0:
                        pe.wait_ge(mix_ready, 16 if j == 7 else 2 * j + 2)
                    chunk(c0 + per * b + j, 0, None, XH, XL, 2 * j, KT, (b0 + b) % 2)

            def feed_forward(layer):
                _, _, c0, b0 = PHASES[f"ple{layer}"]
                pe.wait_ge(turned, TG[f"p{layer}"] + 1)
                for b in range(4):
                    if b < 2:
                        pe.wait_ge(acc_free, b0 - 1 + b)
                    else:
                        pe.wait_ge(ple_ready, 4 * layer + b - 1)
                    chunk(c0 + b, 0, None, PH, PLO, 0, 2, (b0 + b) % 2)
                _, per, c0, b0 = PHASES[f"gate{layer}"]
                g0 = TG[f"ln1{layer}"]
                for b in range(4):
                    acc_ready(b0 + b)
                    if b < 2:
                        pe.wait_ge(ple_ready, 4 * layer + 3 + b)
                    for j in range(per):
                        if b == 0:
                            if j % 2 == 0:
                                quarter_normed(pe, 8 * layer + j // 2 + 1)
                                turn(g0 + j, RES[:], 256 * j)
                                turn(g0 + j + 1, RES[:], 256 * (j + 1))
                            pe.wait_ge(turned, g0 + j + 1)
                        chunk(c0 + per * b + j, 0, None, XH, XL, 2 * j, KT, (b0 + b) % 2)

                if layer == 0:
                    pe.wait_ge(tab_ready, 1)
                    for n_ in range(8):
                        pe.transpose(Y[:, 0, n_ * PAIRS:(n_ + 1) * PAIRS], S5[:, 8 + n_, :], ID[0:PAIRS, 0:PAIRS])
                    for n_ in range(2):
                        last = pe.transpose(Y[:, 1, n_ * PAIRS:(n_ + 1) * PAIRS], S5[:, 6 + n_, :], ID[0:PAIRS, 0:PAIRS])
                    last.then_inc(ab_turned, 1)

                def response(it):
                    pe.wait_ge(k_input, it + 1)
                    pe.wait_ge(ab_ready, 9)
                    if it >= 2:
                        pe.wait_ge(k_out, 2 * (it - 1))
                    for a in range(8):
                        o = Y[32 * (a % 4):32 * (a % 4) + 32, it % 2, P * (a // 4):P * (a // 4 + 1)]
                        for ri in range(2):
                            last = pe.matmul(o, BT[:, a, ri, :], CO[:, ri, a, 0:SUB, :], start=(ri == 0), stop=(ri == 1))
                    last.then_inc(k_done, 1)

                def hidden_turn(b, coef=0, i=None):
                    done = (FA + FB) * layer + b
                    pe.wait_ge(hid_ready, lin(done + 1, coef, i))
                    turn(TG[f"hid{layer}"] + b, GT[:, 1], 0, coef, i)

                for part, n_in, first in (("A", FA, 0), ("B", FB, FA)):
                    _, per, c0, b0 = PHASES[f"in{part}{layer}"]

                    def inner(k, i):
                        acc_ready(b0 + k, 2, i)
                        for j in range(per):
                            chunk(c0 + per * k + j, 2 * per, i, XH, XL, 2 * j, KT, (b0 + k) % 2)
                            if j == 3 and k > 0:
                                hidden_turn(first + k - 1, 2, i)
                        if layer == 0 and k == n_in - 1:
                            response(0 if part == "A" else 5)
                    blocks(pe, n_in, inner)
                    _, per, c0, b0 = PHASES[f"out{part}{layer}"]
                    for b in range(4):
                        acc_ready(b0 + b)
                        for j in range(per):
                            if b == 0 and j == per - 1:
                                pe.wait_ge(turned, TG[f"hid{layer}"] + first + n_in)
                            elif b == 0 and j == 0:
                                pe.wait_ge(turned, TG[f"hid{layer}"] + first + n_in - 1)
                            chunk(c0 + per * b + j, 0, None, HH, HL, 2 * j, 2 * n_in, (b0 + b) % 2)
                            if b == 0 and j == 3:
                                hidden_turn(first + n_in - 1)
                            if layer == 0 and part == "B" and j == 2 and b in (1, 2):
                                response(5 + b)
                        if layer == 0 and part == "A":
                            response(1 + b)

            feed_forward(0)

            pe.wait_ge(acc_free, PHASES["outB0"][3] + 4)
            pe.wait_ge(turned, TG["p1"])
            pe.wait_ge(k_out, 2 * 8)
            for n_ in range(8):
                if n_ % 2 == 0:
                    pe.wait_ge(h4_split, n_ // 2 + 1)
                for a in range(8):
                    last = pe.transpose(PS[:, n_, a * SLOTS:(a + 1) * SLOTS],
                                        H4[:, 8 * n_ + a].rearrange("p s c -> p (s c)"), ID[0:SLOTS, 0:SLOTS])
                last.then_inc(u_turned, 1)
            pe.wait_ge(u_ready, 8)
            for m in range(KT + 1):
                if m < KT:
                    tile = m
                    pe.wait_ge(ts_in[tile % 6], 16 * (tile // 6 + 1))
                    if tile >= 2:
                        pe.wait_ge(e_mid, tile - 1)
                    for a in range(4):
                        last = pe.matmul(PS[0:SLOTS, 2 * (tile % 2) + a // 2, TOK * (a % 2):TOK * (a % 2 + 1)],
                                         U4[:, 4 * tile + a, :], TS[tile % 6][:, a].rearrange("p c n -> p (c n)"),
                                         start=True, stop=True)
                    last.then_inc(e_done, 1)
                if m >= 1:
                    tile = m - 1
                    pe.wait_ge(e_mid, tile + 1)
                    if 4 <= tile < 12:
                        pe.wait_ge(e_out_dve, tile - 3)
                    elif tile >= 12:
                        pe.wait_ge(e_out_act, tile - 11)
                    for a in range(4):
                        for ri in range(2):
                            o = (2 * a + ri) * SLOTS
                            last = pe.transpose(PS[:, 4 + tile % 4, o:o + SLOTS], EM[tile % 2][:, a, ri, :],
                                                ID[0:SLOTS, 0:SLOTS])
                    last.then_inc(e_turned, 1)
            pe.wait_ge(e_out_act, 8)
            pe.wait_ge(e_out_dve, 8)
            pe.wait_ge(kk_in, 16 * 16)

            def bank_of(pair):
                tile, a = pair // 4, pair % 4
                half = SLOTS * (tile // 8)
                return PS[half:half + SLOTS, tile % 8, P * a:P * (a + 1)]

            for pair in range(PAIRS):
                pe.matmul(bank_of(pair), U4[:, pair, :], KK[:, pair, :], start=(pair % 4 == 0), stop=False,
                          skip_group_check=True)
            def read_out(n_):
                tile = n_
                count = 16 * (n_ // 10 + 1) + (16 * (3 if n_ % 10 < 4 else 2) if n_ % 10 < 6 else 0)
                pe.wait_ge(ts_in[n_ % 10], count)
                for a in range(4):
                    pair = 4 * tile + a
                    for ri in range(2):
                        last = pe.matmul(bank_of(pair), ST[:, :, ri, pair], TS[n_ % 10][:, a, ri, :], start=False,
                                         stop=(ri == 1), skip_group_check=True)
                last.then_inc(y_done, 1)

            def turn_z(b):
                pe.wait_ge(z_act, b + 1)
                for half in range(2):
                    rows = slice(SLOTS * half, SLOTS * (half + 1))
                    for s in range(SUB):
                        o = TOK * half + SLOTS * s
                        if half and s == 0:
                            pe.wait_ge(z_half, b + 1)
                        last = pe.transpose(PS[:, b, o:o + SLOTS], Z4[rows, b, P * s:P * (s + 1)], ID[rows, rows])
                    last.then_inc(z_turned if half else z_half, 1)

            pe.wait_ge(scan[0], 3 * (SLOTS - 2))
            for b in range(8):
                read_out(b)
            pe.wait_ge(scan[1], 3 * (SLOTS - 2))
            for b in range(8):
                read_out(8 + b)
                if b >= 2:
                    turn_z(b - 2)
            turn_z(6)
            turn_z(7)

            _, per, c0, b0 = PHASES["glu"]
            pe.wait_ge(z_split, 4)

            def glu(k, i):
                acc_ready(b0 + k, 2, i)
                for j in range(per):
                    if k == 0:
                        pe.wait_ge(z_split, j + 1)
                    chunk(c0 + per * k + j, 2 * per, i, XH, XL, 2 * j, KT, (b0 + k) % 2)
                    if k == 0 and j == 7:
                        pe.wait_ge(p1_in, 16)
                        turn(TG["p1"], PK[:], 0)
            blocks(pe, 8, glu)
            feed_forward(1)

        @block.scalar
        def _(act):
            act.dma_start(ID[:], t["ident"]).then_inc(ident_in, 16)
            for dst, name in [(CM[:], "causal"), (PI[:], "pos")]:
                act.dma_start(dst, t[name]).then_inc(const_in, 16)
            act.dma_start(B0[:], t["dil_bias"][:, 0:2]).then_inc(const_in, 16)
            act.dma_start(NG[:], t["norm_gain"].partition_broadcast(P)).then_inc(const_in, 16)
            for q in range(TT):
                act.dma_start(AT[:, 3, q, :], t["inv_freq"].partition_broadcast(P)).then_inc(const_in, 16)
            act.dma_start(PK[:], t["p"][0].rearrange("(t p) n -> p t n", p=P)).then_inc(p_in, 16)

            def hi(c, coef=0, i=None, width=WB):
                s = c % RING
                act.wait_ge(raw_full[s], lin(16 * (c // RING + 1), 16 * coef // RING, i))
                if c >= RING:
                    act.wait_ge(w_used, lin(c - RING + 1, coef, i))
                act.activation(WH[:, s, :, 0:width], RAW[:, s, :, 0:width], ACT.Copy).then_inc(hi_ready, 1)

            def hi_turned(g, dst, coef=0, i=None):
                act.wait_ge(turn_done, lin(g + 1, coef, i))
                act.activation(dst, TP[:, g % 2], ACT.Copy).then_inc(turn_hi, 1)

            def end(name, b, coef=0, i=None):
                _, per, c0, _ = PHASES[name]
                act.wait_ge(w_used, lin(c0 + per * (b + 1), per * coef, i))

            _, _, c0, b0 = PHASES["win"]

            def win_end(b):
                end("win", b)
                if b < 2:
                    if b == 0:
                        act.wait_ge(const_in, 6 * 16)
                    else:
                        act.wait_ge(sq_sum, 2 * b)
                    for q in range(TT):
                        act.activation(GTf[:, WB * q:WB * (q + 1)], A[:, b % 2, q], ACT.Square,
                                       accum_out=SC[:, 2 * b + q:2 * b + q + 1]).then_inc(sq_sum, 1)
                elif b < 6:
                    act.wait_ge(turn_done, TG["lat"] + 2 * (b - 1))
                    act.activation(STG[:, b % 2], A[:, b % 2], ACT.Copy).then_inc(staged, 1)
                else:
                    act.activation(VD[:, :, (b - 6) * WB:(b - 5) * WB], A[:, b % 2], ACT.Copy).then_inc(acc_free, 1)

            for b in range(8):
                for j in range(8):
                    if b == 0:
                        hi_turned(TG["x"] + j, XH[:, 2 * j:2 * j + 2, :])
                    hi(8 * b + j)
                    if b == 0 and j == 7:
                        hi_turned(TG["p0"], PH[:])
                    if j == 4 and b:
                        win_end(b - 1)
                    if b == 3 and j == 6:
                        act.wait_ge(trig, 1)
                        act.activation(CS[:, 1], AT[:, 0], ACT.Sin).then_inc(trig, 1)
                        act.activation(CS[:, 0], AT[:, 0], ACT.Sin, scale=0.5).then_inc(trig, 1)
                    if b >= 1 and j == 7 and b <= 2:
                        for g in range(2):
                            n_ = 2 * (b - 1) + g
                            hi_turned(TG["lat"] + n_, LH[:, 2 * n_:2 * n_ + 2, :])
            c0 = PHASES["kpe"][2]
            for j in range(8):
                hi(c0 + j, width=ROPE)
                if j == 4:
                    win_end(7)
            QB, KVB = PHASES["qb"], PHASES["kvb"]

            def up_end(m):
                b = m - 1
                act.wait_ge(w_used, QB[2] + 2 * (b + 1))
                if m in (1, 2, 4, 5):
                    if m <= 2:
                        if m == 2:
                            act.wait_ge(turn_done, TG["kpe"] + 1)
                    else:
                        act.wait_ge(turn_done, TG["qn"] + 2 * (m - 2))
                    act.activation(STG[:, m % 2], A[:, (QB[3] + b) % 2], ACT.Copy).then_inc(staged, 1)
                elif m >= 6:
                    act.activation(VM[:, :, (m - 6) * WB:(m - 5) * WB], A[:, (QB[3] + b) % 2],
                                   ACT.Copy).then_inc(acc_free, 1)

            for b in range(7):
                hi(QB[2] + 2 * b)
                hi(QB[2] + 2 * b + 1)
                if b >= 1:
                    up_end(b)
            up_end(7)

            c0 = PHASES["wout"][2]

            def exps(h):
                act.wait_ge(nmax, h + 1)
                if h >= 2:
                    act.wait_ge(p_turned, h - 1)
                scale = DIL_SCALE if h < HEADS else MLA_SCALE
                for q in range(TT):
                    cols = slice(0, P) if q == 0 else slice(P, 3 * P)
                    act.activation(PR[:, h % 2, cols], SM[:, h % 2, cols], ACT.Exp, bias=MX[:, h % 2, q:q + 1],
                                   scale=scale, accum_out=MX[:, h % 2, 2 + q:3 + q]).then_inc(p_exp, 1)

            def probs_out(h):
                act.wait_ge(p_turned, h + 1)
                if h >= 2:
                    act.wait_ge(pv_done, h - 1)
                act.activation(PT[:, h % 2], Y[:, h % 2, 0:3 * P], ACT.Copy).then_inc(pt_ready, 1)

            def mix_high(h):
                act.wait_ge(pv_done, h + 1)
                act.activation(XH[:, h, :], A[:, 1, h % 2, 0:TOK], ACT.Copy).then_inc(mix_hi, 1)

            for s in range(2 * HEADS + 3):
                if s < 2 * HEADS:
                    exps(s)
                if 2 <= s < 2 * HEADS + 2:
                    probs_out(s - 2)
                if s >= 3:
                    mix_high(s - 3)
                if 4 <= s < 8:
                    hi(c0 + s - 4)
            for c in range(c0 + 4, c0 + 32):
                hi(c)

            def norm_part(n_):
                act.wait_ge(ln_scalars, n_ + 1)
                for q4 in range(1, 4):
                    part = RES[:, 1, WB * q4:WB * (q4 + 1)]
                    act.activation(part, part, ACT.Identity, bias=SC[:, 23:24], scale=SC[:, 17:18]).then_inc(ln_act, 1)

            def feed_forward(layer):
                _, _, c0, b0 = PHASES[f"ple{layer}"]
                g0 = PHASES[f"gate{layer}"][2]
                for b in range(4):
                    hi(c0 + b)
                for b in range(4):
                    end(f"ple{layer}", b)
                    act.activation(PL[:, :, b * WB:(b + 1) * WB], A[:, (b0 + b) % 2], ACT.Copy).then_inc(ple_ready, 1)
                    hi(g0 + b)
                if layer:
                    norm_part(2)
                for g in range(8):
                    hi_turned(TG[f"ln1{layer}"] + g, XH[:, 2 * g:2 * g + 2, :])
                    if g >= 1 and g < 5:
                        hi(g0 + 3 + g)

                def gate_sigmoid(b):
                    end(f"gate{layer}", b)
                    if layer or b:
                        act.wait_ge(acc_free, PHASES[f"gate{layer}"][3] + b)
                    act.activation(GT[:, :, :, :].rearrange("p a t n -> p t a n"),
                                   A[:, (PHASES[f"gate{layer}"][3] + b) % 2].rearrange("p t (a n) -> p t a n", a=2),
                                   ACT.Sigmoid).then_inc(gate_act, 1)

                for b in range(1, 4):
                    for j in range(8):
                        hi(g0 + 8 * b + j)
                        if j == 4:
                            gate_sigmoid(b - 1)

                def silu(b, coef=0, i=None):
                    part, k = ("A", b) if b < FA else ("B", b - FA)
                    end(f"in{part}{layer}", k, coef, i)
                    done = (FA + FB) * layer + b
                    if done:
                        act.wait_ge(hid_ready, lin(done, coef, i))
                    parity = (PHASES[f"in{part}{layer}"][3] + k) % 2
                    act.activation(GT[:, 0], A[:, parity, :, 0:256], ACT.Silu).then_inc(silu_done, 1)

                def hidden_hi(b, coef=0, i=None):
                    k = b if b < FA else b - FA
                    hi_turned(TG[f"hid{layer}"] + b, HH[:, bass.ds(lin(2 * k, 2 * coef, i), 2), :], coef, i)

                for part, n_in, first in (("A", FA, 0), ("B", FB, FA)):
                    _, per, c0, _ = PHASES[f"in{part}{layer}"]

                    def inner(k, i):
                        for j in range(per):
                            hi(c0 + per * k + j, 2 * per, i)
                            if k > 0 and j == 4:
                                silu(first + k - 1, 2, i)
                            if k == 0 and j == 4 and part == "A":
                                gate_sigmoid(3)
                            if k > 0 and j == 7:
                                hidden_hi(first + k - 1, 2, i)
                    blocks(act, n_in, inner)
                    nb, per, c0, _ = PHASES[f"out{part}{layer}"]
                    for j in range(8):
                        hi(c0 + j)
                        if j == 4:
                            silu(first + n_in - 1)
                        if j == 7:
                            hidden_hi(first + n_in - 1)
                    rest = nb * per - 8
                    with act.Fori(0, rest // RING) as i:
                        for j in range(RING):
                            hi(c0 + 8 + j, RING, i)

            feed_forward(0)
            c0 = PHASES["glu"][2]
            for j in range(4):
                hi(c0 + j)
            def by_pairs(q4):
                act.wait_ge(h4_in[q4 % 2], 32 * (q4 // 2 + 1))
                act.activation(H4[:, 16 * q4:16 * q4 + 16], HQ[q4 % 2][:].rearrange("p s (a c) -> p a s c", c=PW),
                               ACT.Copy).then_inc(h4_split, 1)

            norm_part(1)
            by_pairs(0)
            by_pairs(1)
            for n_ in range(8):
                if n_ in (2, 4):
                    by_pairs(n_ // 2 + 1)
                act.wait_ge(u_turned, n_ + 1)
                act.activation(U4[:, 8 * n_:8 * n_ + 8, :], PS[:, n_, :].rearrange("p (a n) -> p a n", a=8),
                               ACT.Copy).then_inc(u_ready, 1)
            act.wait_ge(u_ready, 8)
            for m in range(KT + 1):
                if m < KT:
                    act.wait_ge(e_done, m + 1)
                    if m >= 2:
                        act.wait_ge(e_turned, m - 1)
                    act.activation(EM[m % 2][:].rearrange("p a c n -> p (a c n)"),
                                   PS[0:SLOTS, 2 * (m % 2):2 * (m % 2) + 2, :].rearrange("p b n -> p (b n)"), ACT.Copy).then_inc(e_mid, 1)
                if m >= 9:
                    tile = m - 1
                    act.wait_ge(e_turned, tile + 1)
                    act.activation(states_of(tile), turned_of(tile), ACT.Copy).then_inc(e_out_act, 1)

            def gelu(b):
                act.wait_ge(y_done, 8 + b + 1)
                act.activation(Z4[:, b, :].rearrange("p (s a c) -> p a s c", s=SUB, a=4),
                               PS[:, b, :].rearrange("p (a s c) -> p a s c", a=4, s=SUB),
                               ACT.Gelu_apprx_tanh).then_inc(z_act, 1)

            def z_high(b):
                act.wait_ge(z_turned, b + 1)
                act.activation(XH[:, 2 * b:2 * b + 2, :].rearrange("p k (n s) -> p k s n", s=SUB),
                               PS[:, b, :].rearrange("p (k s n) -> p k s n", k=2, s=SUB), ACT.Copy).then_inc(z_hi, 1)

            for b in range(8):
                gelu(b)
                if b >= 3:
                    z_high(b - 3)
            for b in range(5, 8):
                z_high(b)

            b0 = PHASES["glu"][3]

            def glu_sigmoid(b, coef=0, i=None):
                end("glu", b, coef, i)
                act.wait_ge(acc_free, lin(b0 + b, coef, i))
                act.activation(GT[:, 0], A[:, (b0 + b) % 2, :, 256:512], ACT.Sigmoid).then_inc(gate_act, 1)

            def glu(k, i):
                for j in range(8):
                    if not (k == 0 and j < 4):
                        hi(c0 + 8 * k + j, 16, i)
                    if k > 0 and j == 4:
                        glu_sigmoid(k - 1, 2, i)
                    if k == 7 and j == 2:
                        hi_turned(TG["p1"], PH[:])
            blocks(act, 8, glu)
            glu_sigmoid(7)
            feed_forward(1)
            norm_part(3)

        @block.vector
        def _(dve):
            step = [0]

            def link(ins):
                ins.then_inc(v_step, 1)
                step[0] += 1
                dve.wait_ge(v_step, step[0])

            def lo(c, coef=0, i=None, width=WB):
                s = c % RING
                dve.wait_ge(hi_ready, lin(c + 1, coef, i))
                if c >= RING:
                    dve.wait_ge(w_used, lin(c - RING + 1, coef, i))
                dve.tensor_tensor(WL[:, s, :, 0:width], RAW[:, s, :, 0:width], WH[:, s, :, 0:width].bitcast(F32),
                                  ALU.subtract).then_inc(lo_ready, 1)

            def lo_turned(g, n_hi, hi_ap, lo_ap, coef=0, i=None):
                dve.wait_ge(turn_hi, lin(n_hi + 1, coef, i))
                dve.tensor_tensor(lo_ap, TP[:, g % 2], hi_ap.bitcast(F32), ALU.subtract).then_inc(turned, 1)

            def whole_turned(g, dst, src=None):
                dve.wait_ge(turn_done, g + 1)
                dve.tensor_copy(dst, TP[:, g % 2] if src is None else src).then_inc(turned, 1)

            def end(name, b, coef=0, i=None):
                _, per, c0, _ = PHASES[name]
                dve.wait_ge(w_used, lin(c0 + per * (b + 1), per * coef, i))

            def rsqrt(v, y, tmp, n_):
                half = SI[:, 0:n_]
                link(dve.tensor_scalar(half, v.bitcast(I32), 1, None, ALU.logical_shift_right))
                link(dve.tensor_scalar(y.bitcast(I32), half, -1.0, float(0x5F3759DF), ALU.mult, ALU.add))
                for _ in range(3):
                    link(dve.scalar_tensor_tensor(tmp, y, -0.5, y, ALU.mult, ALU.mult))
                    link(dve.tensor_tensor(tmp, tmp, v, ALU.mult))
                    link(dve.scalar_tensor_tensor(y, tmp, 1.5, y, ALU.add, ALU.mult))

            def angles():
                dve.wait_ge(const_in, 6 * 16)
                two_pi = 2 * np.pi
                c1 = 6.28125
                c2 = float(np.float32(np.round((two_pi - c1) * 2 ** 17) / 2 ** 17))
                c3 = float(np.round((two_pi - c1 - c2) * 2 ** 25) / 2 ** 25)
                c4 = float(np.float32(two_pi - c1 - c2 - c3))
                link(dve.tensor_copy(SC[:, 8:10], PI[:]))
                for q in range(TT):
                    link(dve.tensor_scalar(AT[:, 0, q], AT[:, 3, q], SC[:, 8 + q:9 + q], None, ALU.mult))
                r, n_ = AT[:, 0], AT[:, 1]
                link(dve.tensor_scalar(n_, r, 1.0 / two_pi, ROUND, ALU.mult, ALU.add))
                link(dve.tensor_scalar(n_, n_, -ROUND, None, ALU.add))
                for c in (c1, c2, c3, c4):
                    link(dve.scalar_tensor_tensor(r, n_, -c, r, ALU.mult, ALU.add))
                dve.tensor_scalar(r, r, float(np.float32(3.1415925)), -float(np.float32(3.1415925)), ALU.min,
                                  ALU.max).then_inc(trig, 1)

            def cosine():
                dve.wait_ge(trig, 3)
                link(dve.tensor_tensor(CS[:, 0], CS[:, 0], CS[:, 0], ALU.mult))
                link(dve.tensor_scalar(CS[:, 0], CS[:, 0], -2.0, 1.0, ALU.mult, ALU.add))

            def rotate(src, dst, heads):
                for out_half, (first, second, op) in enumerate([(0, 1, ALU.subtract), (1, 0, ALU.add)]):
                    cos = CS[:, 0].unsqueeze(2).broadcast_to([P, TT, heads, HALF])
                    sin = CS[:, 1].unsqueeze(2).broadcast_to([P, TT, heads, HALF])
                    tmp = GTf[:, 512:512 + TT * heads * HALF].rearrange("p (t h n) -> p t h n", t=TT, h=heads)
                    link(dve.tensor_tensor(tmp, src[:, :, :, second], sin, ALU.mult))
                    link(dve.tensor_tensor(dst[:, :, :, first], src[:, :, :, first], cos, ALU.mult))
                    last = dve.tensor_tensor(dst[:, :, :, first], dst[:, :, :, first], tmp, op)
                    if out_half == 0:
                        link(last)
                return last

            def latent(b):
                dve.wait_ge(sq_sum, 2 * b + 2)
                v, y, tmp = SC[:, 4:6], SC[:, 6:8], SC[:, 10:12]
                link(dve.tensor_scalar(v, SC[:, 2 * b:2 * b + 2], 1.0 / LAT, 1e-6, ALU.mult, ALU.add))
                rsqrt(v, y, tmp, 2)
                link(dve.scalar_tensor_tensor(STG[:, b % 2, 0], A[:, b % 2, 0], y[:, 0:1], NG[:, b * LAT:(b + 1) * LAT],
                                              ALU.mult, ALU.mult))
                link(dve.scalar_tensor_tensor(STG[:, b % 2, 1], A[:, b % 2, 1], y[:, 1:2], NG[:, b * LAT:(b + 1) * LAT],
                                              ALU.mult, ALU.mult))
                dve.nop().then_inc(staged, 1)
                dve.nop().then_inc(acc_free, 1)

            for b in range(8):
                for j in range(8):
                    if b == 0:
                        lo_turned(TG["x"] + j, HG["x"] + j, XH[:, 2 * j:2 * j + 2, :], XL[:, 2 * j:2 * j + 2, :])
                    lo(8 * b + j)
                    if b == 0 and j == 7:
                        lo_turned(TG["p0"], HG["p0"], PH[:], PLO[:])
                    if j == 0 and b == 1:
                        angles()
                    if j == 0 and b == 6:
                        cosine()
                    if j == 5 and b in (1, 2):
                        latent(b - 1)
                    if j == 5 and 3 <= b <= 6:
                        dve.wait_ge(staged, b)
                        dve.nop().then_inc(acc_free, 1)
                    if j == 7 and 1 <= b <= 6:
                        for g in range(2):
                            if b <= 2:
                                n_ = 2 * (b - 1) + g
                                lo_turned(TG["lat"] + n_, HG["lat"] + n_, LH[:, 2 * n_:2 * n_ + 2, :],
                                          LL[:, 2 * n_:2 * n_ + 2, :])
                            else:
                                n_ = 2 * (b - 3) + g
                                whole_turned(TG["qk"] + n_, QK[:, 2 * n_:2 * n_ + 2, :])
            c0 = PHASES["kpe"][2]
            for j in range(8):
                lo(c0 + j, width=ROPE)
            QB = PHASES["qb"]

            def up_turned(m):
                if m == 0:
                    g = TG["kpe"]
                    whole_turned(g, KP[:], TP[:, g % 2, 0])
                else:
                    dst, h = [(QN, 0), (QN, 4), (QP, 0), (KN, 0), (KN, 4)][m - 1]
                    g = [TG["qn"], TG["qn"] + 2, TG["qp"], TG["kn"], TG["kn"] + 2][m - 1]
                    for n_ in range(2):
                        whole_turned(g + n_, dst[:, h + 2 * n_:h + 2 * n_ + 2, :])

            for b in range(7):
                lo(QB[2] + 2 * b)
                lo(QB[2] + 2 * b + 1)
                if b == 0:
                    end("kpe", 0)
                    src = A[:, PHASES["kpe"][3] % 2, :, 0:ROPE].rearrange("p t (h c n) -> p t h c n", h=1, c=2)
                    dve.wait_ge(turn_done, TG["kpe"])
                    dst = STG[:, 0, :, 0:ROPE].rearrange("p t (h c n) -> p t h c n", h=1, c=2)
                    link(rotate(src, dst, 1))
                    link(dve.tensor_copy(STG[:, 0, :, ROPE:2 * ROPE], STG[:, 0, :, 0:ROPE]))
                    dve.nop().then_inc(staged, 1)
                    dve.nop().then_inc(acc_free, 1)
                if b in (1, 2, 4, 5):
                    dve.wait_ge(staged, 7 + b)
                    dve.nop().then_inc(acc_free, 1)
                if b == 3:
                    end("qb", 2)
                    dve.wait_ge(turn_done, TG["qn"] + 2)
                    src = A[:, (QB[3] + 2) % 2].rearrange("p t (h c n) -> p t h c n", h=HEADS, c=2)
                    dst = STG[:, 1].rearrange("p t (h c n) -> p t h c n", h=HEADS, c=2)
                    link(rotate(src, dst, HEADS))
                    dve.nop().then_inc(staged, 1)
                    dve.nop().then_inc(acc_free, 1)
                if b >= 2:
                    up_turned(b - 2)
            up_turned(5)

            c0 = PHASES["wout"][2]

            def mask_and_max(h):
                dve.wait_ge(s_done, h + 1)
                if h >= 2:
                    dve.wait_ge(p_exp, 2 * (h - 1))
                if h == 2:
                    dve.wait_ge(bias_in, 16)
                scale = DIL_SCALE if h < HEADS else MLA_SCALE
                bias = B0[:, h] if h < 2 else B2[:, h - 2] if h < HEADS else CM[:]
                dve.tensor_tensor(SM[:, h % 2], A[:, 0, h % 2, 0:3 * P], bias, ALU.add).then_inc(s_masked, 1)
                dve.wait_ge(s_masked, h + 1)
                if h >= 1:
                    dve.wait_ge(nmax, h)
                dve.tensor_reduce(SC[:, 12:13], SM[:, h % 2, 0:P], AX_X, ALU.max)
                link(dve.tensor_reduce(SC[:, 13:14], SM[:, h % 2, P:3 * P], AX_X, ALU.max))
                dve.tensor_scalar(MX[:, h % 2, 0:2], SC[:, 12:14], -scale, None, ALU.mult).then_inc(nmax, 1)

            def norm_probs(h):
                dve.wait_ge(p_exp, 2 * h + 2)
                if h >= 1:
                    dve.wait_ge(p_ready, h)
                parts = [slice(0, P), slice(P, 3 * P)]
                link(dve.reciprocal(SC[:, 14:16], MX[:, h % 2, 2:4]))
                link(dve.tensor_scalar(PR[:, h % 2, parts[0]], PR[:, h % 2, parts[0]], SC[:, 14:15], None, ALU.mult))
                dve.tensor_scalar(PR[:, h % 2, parts[1]], PR[:, h % 2, parts[1]], SC[:, 15:16], None,
                                  ALU.mult).then_inc(p_ready, 1)

            def mix_low(h):
                dve.wait_ge(mix_hi, h + 1)
                dve.tensor_tensor(XL[:, h, :], A[:, 1, h % 2, 0:TOK], XH[:, h, :].bitcast(F32),
                                  ALU.subtract).then_inc(mix_ready, 1)

            for s in range(2 * HEADS + 4):
                if s < 2 * HEADS:
                    mask_and_max(s)
                if 1 <= s <= 2 * HEADS:
                    norm_probs(s - 1)
                if s >= 4:
                    mix_low(s - 4)
                if 5 <= s < 9:
                    lo(c0 + s - 5)

            def add_stats(b, q, width, n_):
                return dve.bn_stats(BS[:, q, n_, :], RES[:, q, width * b:width * (b + 1)])

            def wout_end(b):
                end("wout", b)
                cols = slice(WB * b, WB * (b + 1))
                dve.scalar_tensor_tensor(RES[:, :, cols], RES[:, :, cols], ALPHA, A[:, (PHASES["wout"][3] + b) % 2],
                                         ALU.mult, ALU.add).then_inc(acc_free, 1)
                dve.wait_ge(acc_free, PHASES["wout"][3] + b + 1)
                for q in range(TT):
                    last = add_stats(b, q, WB, b)
                last.then_inc(v_step, 1)
                step[0] += 1

            for b in range(4):
                for j in range(8):
                    if 8 * b + j >= 4:
                        lo(c0 + 8 * b + j)
                    if b and j == 4:
                        wout_end(b - 1)

            def norm_scalars(n_):
                dve.wait_ge(v_step, step[0])
                for q in range(TT):
                    last = dve.bn_aggr(MV[:, q, :], BS[:, q, 0:n_, :].rearrange("p a b -> p (a b)"))
                link(last)
                link(dve.tensor_scalar(SC[:, 18:20], MV[:, :, 1], 1e-5, None, ALU.add))
                rsqrt(SC[:, 18:20], SC[:, 16:18], SC[:, 20:22], 2)
                dve.scalar_tensor_tensor(SC[:, 22:24], MV[:, :, 0], -1.0, SC[:, 16:18], ALU.mult, ALU.mult).then_inc(ln_scalars, 1)

            def norm_quarter(n_, q4):
                dve.wait_ge(gb_in, 32 * (n_ + 1))
                cols = slice(WB * q4, WB * (q4 + 1))
                for q in range(TT if n_ == 0 or q4 == 0 else 1):
                    link(dve.scalar_tensor_tensor(RES[:, q, cols], RES[:, q, cols], MV[:, q, 0:1], GB[:, 0, cols],
                                                  ALU.subtract, ALU.mult))
                    last = dve.scalar_tensor_tensor(RES[:, q, cols], RES[:, q, cols], SC[:, 16 + q:17 + q],
                                                    GB[:, 1, cols], ALU.mult, ALU.add)
                    if q == 0 and (n_ == 0 or q4 == 0):
                        last.then_inc(v_step, 1)
                        step[0] += 1
                    else:
                        last.then_inc(ln_quarter, 1)

            def feed_forward(layer):
                ln1 = 2 * layer
                g0, b0 = PHASES[f"gate{layer}"][2:]
                G = TG[f"ln1{layer}"]

                def split(g):
                    lo_turned(G + g, HG[f"ln1{layer}"] + g, XH[:, 2 * g:2 * g + 2, :],
                              XL[:, 2 * g:2 * g + 2, :])

                norm_quarter(ln1, 0)
                norm_quarter(ln1, 1)
                for q4 in range(4):
                    lo(g0 + 2 * q4)
                    split(2 * q4)
                    split(2 * q4 + 1)
                    lo(g0 + 2 * q4 + 1)
                    if q4 < 2:
                        norm_quarter(ln1, q4 + 2)

                def gate_end(b):
                    cols = slice(WB * b, WB * (b + 1))
                    dve.wait_ge(gate_act, (4 + 8) * layer + b + 1)
                    dve.wait_ge(ple_ready, 4 * layer + 4)
                    g = GT[:, :, :, :].rearrange("p a t n -> p t a n")
                    pl = PL[:, :, cols].rearrange("p t (a n) -> p t a n", a=2)
                    link(dve.tensor_tensor(pl, pl, g, ALU.mult))
                    dve.scalar_tensor_tensor(RES[:, :, cols], RES[:, :, cols], ALPHA, PL[:, :, cols], ALU.mult,
                                             ALU.add).then_inc(acc_free, 1)

                for b in range(1, 4):
                    for j in range(8):
                        lo(g0 + 8 * b + j)
                        if j == 4:
                            gate_end(b - 1)

                def hidden(b, coef=0, i=None):
                    part, k = ("A", b) if b < FA else ("B", b - FA)
                    bb = PHASES[f"in{part}{layer}"][3] + k
                    done = (FA + FB) * layer + b
                    dve.wait_ge(silu_done, lin(done + 1, coef, i))
                    dve.wait_ge(turn_done, lin(TG[f"hid{layer}"] + b, coef, i))
                    dve.tensor_tensor(GT[:, 1], A[:, bb % 2, :, 256:512], GT[:, 0],
                                      ALU.mult).then_inc(hid_ready, 1)

                def hidden_free(b, coef=0, i=None):
                    part, k = ("A", b) if b < FA else ("B", b - FA)
                    done = (FA + FB) * layer + b
                    dve.wait_ge(hid_ready, lin(done + 1, coef, i))
                    dve.nop().then_inc(acc_free, 1)

                def hidden_lo(b, coef=0, i=None):
                    k = b if b < FA else b - FA
                    rows = bass.ds(lin(2 * k, 2 * coef, i), 2)
                    lo_turned(TG[f"hid{layer}"] + b, HG[f"hid{layer}"] + b, HH[:, rows, :],
                              HL[:, rows, :], coef, i)

                def out_end(part, b, stats):
                    bb = PHASES[f"out{part}{layer}"][3] + b
                    end(f"out{part}{layer}", b)
                    cols = slice(WB * b, WB * (b + 1))
                    dve.tensor_tensor(RES[:, :, cols], A[:, bb % 2], RES[:, :, cols], ALU.add).then_inc(acc_free, 1)
                    if stats:
                        dve.wait_ge(acc_free, bb + 1)
                        for q in range(TT):
                            last = add_stats(b, q, WB, b)
                        last.then_inc(v_step, 1)
                        step[0] += 1

                def transition():
                    dve.wait_ge(ab_turned, 1)
                    dve.wait_ge(tab_ready, 2)
                    pw = Y[:, 0, :].rearrange("p (k c n) -> p k c n", k=SUB, c=2)
                    re, im = pw[:, :, 0, :], pw[:, :, 1, :]
                    cf = Y[:, 1, 0:2 * PAIRS].rearrange("p (c n) -> p c n", c=2)
                    dve.memset(PW_T[:, 0, :], 1.0)
                    dve.memset(PW_T[:, 1, :], 0.0)
                    dve.memset(PW_T[:, 2, :], -1.0).then_inc(ab_ready, 1)
                    dve.tensor_copy(PW_T[:, 3:15:3, :], re).then_inc(ab_ready, 1)
                    dve.tensor_scalar(PW_T[:, 4:15:3, :], im, -1.0, None, ALU.mult).then_inc(ab_ready, 1)
                    dve.tensor_scalar(PW_T[:, 5:15:3, :], re, -1.0, None, ALU.mult).then_inc(ab_ready, 1)
                    dve.tensor_copy(PW_T[:, 15:17, :], cf).then_inc(ab_ready, 1)
                    dve.tensor_scalar(PW_T[:, 17, :], cf[:, 1, :], -1.0, None, ALU.mult).then_inc(ab_ready, 1)
                    dve.tensor_copy(AB[:, 0:4:3, :], re[:, SUB - 1, :].unsqueeze(1).broadcast_to([P, 2, PAIRS])).then_inc(ab_ready, 1)
                    dve.tensor_copy(AB[:, 2, :], im[:, SUB - 1, :]).then_inc(ab_ready, 1)
                    dve.tensor_scalar(AB[:, 1, :], im[:, SUB - 1, :], -1.0, None, ALU.mult).then_inc(ab_ready, 1)
                    dve.wait_ge(ab_ready, 9)

                def response_out(it):
                    dve.wait_ge(k_done, it + 1)
                    y = Y[:, it % 2, 0:TOK].rearrange("p (k s c) -> p k s c", k=2, s=SUB)
                    dst = KTAB[:, 2 * it:2 * it + 2, :, :]
                    dve.tensor_tensor(dst[:, :, 0, :], y[:, :, 0, :], DG[:, 2 * it:2 * it + 2, :], ALU.add).then_inc(k_out, 1)
                    dve.tensor_copy(dst[:, :, 1:SUB, :], y[:, :, 1:SUB, :]).then_inc(k_out, 1)

                for part, n_in, first in (("A", FA, 0), ("B", FB, FA)):
                    _, per, c0, _ = PHASES[f"in{part}{layer}"]

                    def inner(k, i):
                        for j in range(per):
                            lo(c0 + per * k + j, 2 * per, i)
                            if k == 0 and j == 4:
                                if part == "A":
                                    gate_end(3)
                                    if layer == 0:
                                        transition()
                                else:
                                    out_end("A", 3, False)
                            if k > 0 and j == 4:
                                hidden(first + k - 1, 2, i)
                            if k > 0 and j == 5:
                                hidden_free(first + k - 1, 2, i)
                            if k > 0 and j == 7:
                                hidden_lo(first + k - 1, 2, i)
                            if k == 0 and j == 7 and part == "B" and layer == 0:
                                response_out(4)
                    blocks(dve, n_in, inner)
                    nb, per, c0, _ = PHASES[f"out{part}{layer}"]
                    for b in range(nb):
                        for j in range(per):
                            lo(c0 + per * b + j)
                            if b == 0 and j == 4:
                                hidden(first + n_in - 1)
                            if b == 0 and j == 5:
                                hidden_free(first + n_in - 1)
                            if b == 0 and j == 7:
                                hidden_lo(first + n_in - 1)
                            if b and j == 4:
                                out_end(part, b - 1, part == "B")
                            if j == 6 and layer == 0 and (part == "A" or b < 3):
                                response_out(b if part == "A" else 5 + b)
                nxt = PHASES["glu"][2] if layer == 0 else None
                if nxt is not None:
                    for j in range(RING - 1):
                        lo(nxt + j)
                out_end("B", 3, True)
                norm_scalars(4)
                if nxt is not None:
                    lo(nxt + RING - 1)

            def start_ple(layer, chunk_range):
                for b in chunk_range:
                    lo(PHASES[f"ple{layer}"][2] + b)

            start_ple(0, range(RING - 1))
            wout_end(3)
            norm_scalars(4)
            start_ple(0, range(RING - 1, RING))
            feed_forward(0)

            for q4 in range(4):
                norm_quarter(1, q4)
            dve.wait_ge(u_ready, 8)
            dve.memset(ST[:, 0, :, :], 0.0).then_inc(slot_zero, 1)
            for tile in range(8):
                dve.wait_ge(e_turned, tile + 1)
                dve.tensor_copy(states_of(tile), turned_of(tile)).then_inc(e_out_dve, 1)
            dve.wait_ge(e_out_dve, 8)
            dve.wait_ge(slot_zero, 1)
            half = PAIRS // 2
            abar = AB[:, :, :].rearrange("p (o c) n -> p o c n", o=2)
            prod = [GTf[:, 256 * h:256 * h + 4 * half].rearrange("p (o c n) -> p o c n", o=2, c=2) for h in range(2)]
            part = [GTf[:, 512 + 128 * h:512 + 128 * h + 2 * half].rearrange("p (c n) -> p c n", c=2) for h in range(2)]

            def scan_op(h, n_, k, per=0, i=None):
                done = 3 * k + n_
                if done > 0:
                    dve.wait_ge(scan[h], lin(done, 3 * per, i))
                m = slice(half * h, half * (h + 1))
                x, y = (ST[:, bass.ds(lin(k + d, per, i), 1)].rearrange("p a c n -> p (a c) n")[:, :, m] for d in (1, 2))
                if n_ == 0:
                    ins = dve.tensor_tensor(prod[h], abar[:, :, :, m], x.unsqueeze(1).broadcast_to([P, 2, 2, half]), ALU.mult)
                elif n_ == 1:
                    ins = dve.tensor_tensor(part[h], prod[h][:, :, 0, :], prod[h][:, :, 1, :], ALU.add)
                else:
                    ins = dve.tensor_tensor(y, y, part[h], ALU.add)
                ins.then_inc(scan[h], 1)

            steps, lag = SLOTS - 2, 17
            for n_ in range(3):
                scan_op(0, n_, 0)
            with dve.Fori(0, (lag - 1) // 8) as i:
                for k in range(8):
                    for n_ in range(3):
                        scan_op(0, n_, 1 + k, 8, i)
            dve.wait_ge(e_out_act, 8)
            for n_ in range(3):
                scan_op(0, n_, lag)
                scan_op(1, n_, 0)
            with dve.Fori(0, (steps - lag - 1) // 11) as i:
                for k in range(11):
                    for n_ in range(3):
                        scan_op(0, n_, lag + 1 + k, 11, i)
                        scan_op(1, n_, 1 + k, 11, i)
            for k in range(steps - lag, steps):
                for n_ in range(3):
                    scan_op(1, n_, k)
            for b in range(8):
                dve.wait_ge(z_hi, b + 1)
                hi_ap = XH[:, 2 * b:2 * b + 2, :].bitcast(F32).rearrange("p k (n s) -> p k s n", s=SUB)
                dve.tensor_tensor(XL[:, 2 * b:2 * b + 2, :].rearrange("p k (n s) -> p k s n", s=SUB),
                                  PS[:, b, :].rearrange("p (k s n) -> p k s n", k=2, s=SUB), hi_ap,
                                  ALU.subtract).then_inc(z_split, 1)

            c0, b0 = PHASES["glu"][2:]

            def glu_end(b, coef=0, i=None):
                dve.wait_ge(gate_act, lin(4 + b + 1, coef, i))
                dve.tensor_tensor(GT[:, 1], A[:, (b0 + b) % 2, :, 0:256], GT[:, 0], ALU.mult).then_inc(glu_step, 1)
                dve.wait_ge(glu_step, lin(2 * b + 1, 2 * coef, i))
                cols = RES[:, :, bass.ds(lin(256 * b, 256 * coef, i), 256)]
                dve.scalar_tensor_tensor(cols, cols, ALPHA, GT[:, 1], ALU.mult, ALU.add).then_inc(acc_free, 1)
                dve.wait_ge(acc_free, lin(b0 + b + 1, coef, i))
                for q in range(TT):
                    last = dve.bn_stats(BS[:, q, bass.ds(lin(b, coef, i), 1), :].rearrange("p a b -> p (a b)"),
                                        RES[:, q, bass.ds(lin(256 * b, 256 * coef, i), 256)])
                last.then_inc(glu_step, 1)

            def glu(k, i):
                for j in range(8):
                    if not (k == 0 and j < 4):
                        lo(c0 + 8 * k + j, 16, i)
                    if k > 0 and j == 4:
                        glu_end(k - 1, 2, i)
                    if k == 7 and j == 2:
                        lo_turned(TG["p1"], HG["p1"], PH[:], PLO[:])
            blocks(dve, 8, glu)
            start_ple(1, range(RING - 1))
            glu_end(7)
            dve.wait_ge(glu_step, 16)
            norm_scalars(8)
            start_ple(1, range(RING - 1, RING))
            feed_forward(1)
            for q4 in range(4):
                norm_quarter(3, q4)

        @block.gpsimd
        def _(pool):
            count = [0]

            def link(ins):
                ins.then_inc(tab, 1)
                count[0] += 1
                pool.wait_ge(tab, count[0])

            def load_gb(n_):
                layer, which = n_ // 2, n_ % 2 + 1
                for k, name in enumerate((f"ln{which}_g", f"ln{which}_b")):
                    pool.dma_start(GB[:, k, :], t[name][layer:layer + 1, :].rearrange("a n -> (a n)").partition_broadcast(P)).then_inc(gb_in, 16)

            def norm_part(n_):
                pool.wait_ge(gb_in, 32 * (n_ + 1))
                for q4 in range(1, 4):
                    pool.wait_ge(ln_act, 3 * (n_ - 1) + q4)
                    cols = slice(WB * q4, WB * (q4 + 1))
                    part = RES[:, 1, cols]
                    link(pool.tensor_tensor(part, part, GB[:, 0, cols], ALU.mult))
                    pool.tensor_tensor(part, part, GB[:, 1, cols], ALU.add).then_inc(ln_pool, 1)

            pool.wait_ge(w_used, PHASES["wout"][2])
            pool.dma_start(B2[:], t["dil_bias"][:, 2:HEADS]).then_inc(bias_in, 16)
            pool.wait_ge(w_used, PHASES["wout"][2] + 8)
            load_gb(0)
            ARE, AIM, LDT, DT, E, S, C, T0, T1, T2, T3, LDT2, INV = (S5[:, 16 + k, :] for k in range(13))
            power = [[None, None]] + [[S5[:, 8 + 2 * k + c, :] for c in range(2)] for k in range(SUB)]
            coef = [[S5[:, 2 * k + c, :] for c in range(2)] for k in range(SUB)]
            for dst, name in [(ARE, "s5_are"), (AIM, "s5_aim"), (S5[:, 18, 0:2], "s5_ldt")]:
                pool.dma_start(dst, t[name]).then_inc(late_in, 16)
            pool.wait_ge(late_in, 3 * 16)

            def tt(o, a, b, op):
                link(pool.tensor_tensor(o, a, b, op))

            def ts(o, a, s1, s2, op0, op1=None):
                if s2 is None:
                    link(pool.tensor_scalar(o, a, s1, None, op0))
                else:
                    link(pool.tensor_scalar(o, a, s1, s2, op0, op1))

            def exp(o, x):
                ln2_hi = 0.693145751953125
                ln2_lo = float(np.float32(np.log(2.0) - ln2_hi))
                ts(T0, x, -87.0, 88.0, ALU.max, ALU.min)
                ts(T1, T0, float(1 / np.log(2.0)), ROUND, ALU.mult, ALU.add)
                ts(T1, T1, -ROUND, None, ALU.add)
                ts(T2, T1, -ln2_hi, None, ALU.mult)
                tt(T0, T0, T2, ALU.add)
                ts(T2, T1, -ln2_lo, None, ALU.mult)
                tt(T0, T0, T2, ALU.add)
                ts(T2, T0, 1 / 5040.0, 1 / 720.0, ALU.mult, ALU.add)
                for c in (1 / 120.0, 1 / 24.0, 1 / 6.0, 0.5, 1.0, 1.0):
                    tt(T2, T2, T0, ALU.mult)
                    ts(T2, T2, c, None, ALU.add)
                ts(T1.bitcast(I32), T1, 127.0, float(2 ** 23), ALU.add, ALU.mult)
                tt(o, T2, T1, ALU.mult)

            def sin_cos(x):
                two_pi = 2 * np.pi
                c1 = 6.28125
                c2 = float(np.float32(np.round((two_pi - c1) * 2 ** 17) / 2 ** 17))
                c3 = float(np.round((two_pi - c1 - c2) * 2 ** 25) / 2 ** 25)
                c4 = float(np.float32(two_pi - c1 - c2 - c3))
                ts(T1, x, float(1 / two_pi), ROUND, ALU.mult, ALU.add)
                ts(T1, T1, -ROUND, None, ALU.add)
                ts(T2, T1, -c1, None, ALU.mult)
                tt(T0, x, T2, ALU.add)
                for c in (c2, c3, c4):
                    ts(T2, T1, -c, None, ALU.mult)
                    tt(T0, T0, T2, ALU.add)
                ts(T0, T0, 3.2, -3.2, ALU.min, ALU.max)
                ts(T0, T0, 0.25, None, ALU.mult)
                tt(T1, T0, T0, ALU.mult)
                ts(T2, T1, 1 / 362880.0, -1 / 5040.0, ALU.mult, ALU.add)
                for c in (1 / 120.0, -1 / 6.0, 1.0):
                    tt(T2, T2, T1, ALU.mult)
                    ts(T2, T2, c, None, ALU.add)
                tt(S, T2, T0, ALU.mult)
                ts(T2, T1, 1 / 40320.0, -1 / 720.0, ALU.mult, ALU.add)
                for c in (1 / 24.0, -0.5, 1.0):
                    tt(T2, T2, T1, ALU.mult)
                    ts(T2, T2, c, None, ALU.add)
                tt(T3, S, T2, ALU.mult)
                tt(T1, S, S, ALU.mult)
                ts(T2, T1, -2.0, 1.0, ALU.mult, ALU.add)
                ts(T3, T3, 2.0, None, ALU.mult)
                tt(S, T3, T2, ALU.mult)
                ts(S, S, 2.0, None, ALU.mult)
                tt(T1, T3, T3, ALU.mult)
                ts(C, T1, -2.0, 1.0, ALU.mult, ALU.add)

            link(pool.tensor_copy(LDT2.rearrange("r (s n) -> r s n", s=2),
                                  S5[:, 18, 0:2].unsqueeze(2).broadcast_to([64, 2, 64])))
            exp(DT, LDT2)
            tt(T3, ARE, DT, ALU.mult)
            exp(E, T3)
            tt(LDT2, AIM, DT, ALU.mult)
            sin_cos(LDT2)
            tt(power[1][0], E, C, ALU.mult)
            tt(power[1][1], E, S, ALU.mult)

            def product(o, a, b):
                tt(T0, a[0], b[0], ALU.mult)
                tt(T1, a[1], b[1], ALU.mult)
                tt(o[0], T0, T1, ALU.subtract)
                tt(T0, a[0], b[1], ALU.mult)
                tt(T1, a[1], b[0], ALU.mult)
                tt(o[1], T0, T1, ALU.add)

            product(power[2], power[1], power[1])
            product(power[3], power[2], power[1])
            product(power[4], power[2], power[2])
            tt(T0, ARE, ARE, ALU.mult)
            tt(T1, AIM, AIM, ALU.mult)
            tt(T0, T0, T1, ALU.add)
            link(pool.tensor_copy(T1, T0.bitcast(I32)))
            ts(INV.bitcast(I32), T1, -1.0, float(0x7EF311C3), ALU.mult, ALU.add)
            for _ in range(4):
                tt(T1, T0, INV, ALU.mult)
                ts(T1, T1, -1.0, 2.0, ALU.mult, ALU.add)
                tt(INV, INV, T1, ALU.mult)
            ts(T3, power[1][0], -1.0, None, ALU.add)
            tt(T0, T3, ARE, ALU.mult)
            tt(T1, power[1][1], AIM, ALU.mult)
            tt(T0, T0, T1, ALU.add)
            tt(coef[3][0], T0, INV, ALU.mult)
            tt(T0, power[1][1], ARE, ALU.mult)
            tt(T1, T3, AIM, ALU.mult)
            tt(T0, T0, T1, ALU.subtract)
            tt(coef[3][1], T0, INV, ALU.mult)
            for k in (2, 1, 0):
                product(coef[k], coef[3], power[3 - k])
            pool.sem_inc(tab_ready, 1)
            pool.dma_start(coef_dram, S5[:, 0:8, :].rearrange("r k n -> r (k n)")).then_inc(coef_out, 16)
            pool.wait_ge(coef_out, 16)
            pool.sem_inc(tab_ready, 1)

            pool.wait_ge(w_used, PHASES["inA0"][2] + 8)

            def load_input(tile):
                for s in range(SUB):
                    src = coef_dram[4 * tile:4 * tile + 4, 2 * P * s:2 * P * (s + 1)].partition_broadcast(PW)
                    pool.dma_start(EC[tile % 2][PW * s:PW * (s + 1)].rearrange("p a c n -> p a (c n)"), src).then_inc(e_raw[tile % 2], 16)
                pool.dma_start(EB[tile % 2][:], t["s5_b"][:, 4 * tile:4 * tile + 4]).then_inc(e_raw[tile % 2], 16)

            def input_matrices(first, last):
                load_input(first)
                for tile in range(first, last):
                    if tile + 1 < last:
                        load_input(tile + 1)
                    pool.wait_ge(e_raw[tile % 2], 5 * 16 * (tile // 2 + 1))
                    ec, eb = EC[tile % 2], EB[tile % 2]
                    cr, ci, br, bi = ec[:, :, 0], ec[:, :, 1], eb[:, :, 0], eb[:, :, 1]
                    tt(ET[:], cr, br, ALU.mult)
                    if tile:
                        pool.wait_ge(e_stored, 16 * tile)
                    tt(EO[:, :, 0], ci, bi, ALU.mult)
                    tt(EO[:, :, 0], ET[:], EO[:, :, 0], ALU.subtract)
                    tt(ET[:], cr, bi, ALU.mult)
                    tt(EO[:, :, 1], ci, br, ALU.mult)
                    tt(EO[:, :, 1], ET[:], EO[:, :, 1], ALU.add)
                    pool.dma_start(e_dram[tile], EO[:].rearrange("p a c n -> p (a c n)")).then_inc(e_stored, 16)
                pool.wait_ge(e_stored, 16 * last)

            def output_matrices(it):
                pairs = slice(8 * it, 8 * it + 8)
                if it:
                    pool.wait_ge(k_done, it)
                    pool.wait_ge(c_stored, 4 * 16 * it)
                pool.dma_start(CR[:], t["s5_c"][:, pairs]).then_inc(c_raw, 16)
                pool.dma_start(BR[:], t["s5_bt"][:, pairs]).then_inc(c_raw, 16)
                if it == 0:
                    pool.dma_start(DG[:], t["s5_skip"]).then_inc(c_raw, 16)
                pool.wait_ge(c_raw, 16 * (2 * it + 3))
                shape = [P, 8, SUB + 1, PW]
                re, nim, nre = (PW_T[:, k:15:3, pairs].rearrange("p k a -> p a k").unsqueeze(3).broadcast_to(shape) for k in range(3))
                cr, ci = (CR[:, :, k, :].unsqueeze(2).broadcast_to(shape) for k in range(2))
                tt(CT[:], cr, re, ALU.mult)
                tt(CO[:, 0], ci, nim, ALU.mult)
                tt(CO[:, 0], CT[:], CO[:, 0], ALU.add)
                tt(CT[:], cr, nim, ALU.mult)
                tt(CO[:, 1], ci, nre, ALU.mult)
                tt(CO[:, 1], CT[:], CO[:, 1], ALU.add)
                kr, ki, nki = (PW_T[:, k, pairs].unsqueeze(2).broadcast_to([P, 8, PW]) for k in (15, 16, 17))
                tt(BX[:], BR[:, :, 0], kr, ALU.mult)
                tt(BT[:, :, 0], BR[:, :, 1], nki, ALU.mult)
                tt(BT[:, :, 0], BX[:], BT[:, :, 0], ALU.add)
                tt(BX[:], BR[:, :, 0], ki, ALU.mult)
                tt(BT[:, :, 1], BR[:, :, 1], kr, ALU.mult)
                tt(BT[:, :, 1], BX[:], BT[:, :, 1], ALU.add)
                pool.sem_inc(k_input, 1)
                for k in range(2):
                    for c in range(2):
                        dst = c_dram[2 * it + k].rearrange("p (a c n) -> p a c n", a=4, c=2)[:, :, c, :]
                        pool.dma_start(dst, CO[:, c, 4 * k:4 * k + 4, 1:, :].rearrange("p a s n -> p a (s n)")).then_inc(c_stored, 16)

            pool.wait_ge(ln_quarter, 4)
            load_gb(1)
            input_matrices(0, 12)
            for it in range(5):
                output_matrices(it)
            pool.wait_ge(k_done, 5)
            pool.wait_ge(c_stored, 5 * 4 * 16)
            input_matrices(12, KT)
            for it in range(5, 8):
                output_matrices(it)

            pool.wait_ge(w_used, PHASES["outB0"][2] + 1)
            pool.memset(KK[:], 0.0).then_inc(kk_zero, 1)
            pool.wait_ge(kk_zero, 1)
            pool.wait_ge(k_out, 2 * 8)
            for s in range(SUB):
                for r in range(4):
                    pool.dma_start(KK[PW * s:PW * (s + 1), r::4, PW * s:P],
                                   KTAB[PW * r:PW * (r + 1), :, 0:SUB - s, :].rearrange("p k s n -> p k (s n)")).then_inc(kk_in, 16)
            norm_part(1)
            pool.wait_ge(y_done, KT)
            pool.dma_start(PK[:], t["p"][1].rearrange("(t p) n -> p t n", p=P)).then_inc(p1_in, 16)
            load_gb(2)
            norm_part(2)
            quarter_normed(pool, 12)
            load_gb(3)
            norm_part(3)


def chunks(w, cols):
    parts = []
    for ranges in cols:
        b = np.concatenate([w[:, a:e] for a, e in ranges], axis=1)
        r, n = b.shape
        parts.append(b.reshape(r // 256, 2, 128, n).transpose(0, 2, 1, 3).reshape(r // 256, 128, 2 * n))
    return np.ascontiguousarray(np.concatenate(parts, axis=0))


def kernel(**inputs):
    import concourse.bacc as bacc
    from concourse.bass_utils import run_bass_kernel_spmd as run

    a = {k: np.asarray(v) for k, v in inputs.items()}
    arr = {"x": a["x"][0], "p": a["p"][:, 0]}
    w = a["attn_w_in"][0]
    lat, qd, kd, vd = 0, 2 * LAT + ROPE, 2 * LAT + ROPE + 1024, 2 * LAT + ROPE + 2048
    starts = [lat, LAT, qd, qd + WB, kd, kd + WB, vd, vd + WB]
    arr["w_in"] = chunks(w, [[(s, s + WB)] for s in starts])
    arr["w_kpe"] = chunks(w, [[(2 * LAT, 2 * LAT + ROPE)]])
    wq = a["mla_w_q_b"][0].reshape(LAT, HEADS, HD + ROPE)
    wq = np.concatenate([wq[:, :, :HD].reshape(LAT, -1), wq[:, :, HD:].reshape(LAT, -1)], axis=1)
    arr["w_qb"] = chunks(wq, [[(WB * b, WB * (b + 1))] for b in range(3)])
    wk = a["mla_w_kv_b"][0].reshape(LAT, HEADS, 2 * HD)
    wk = np.concatenate([wk[:, :, :HD].reshape(LAT, -1), wk[:, :, HD:].reshape(LAT, -1)], axis=1)
    arr["w_kvb"] = chunks(wk, [[(WB * b, WB * (b + 1))] for b in range(4)])
    wo = a["attn_w_out"][0]
    arr["w_out"] = chunks(np.concatenate([wo[1024:], wo[:1024]], axis=0), [[(WB * b, WB * (b + 1))] for b in range(4)])
    wg = a["s5_w_glu"][0].reshape(2, 8, 128, 2 * D).transpose(1, 0, 2, 3).reshape(D, 2 * D)
    arr["w_glu"] = chunks(wg, [[(256 * b, 256 * (b + 1)), (D + 256 * b, D + 256 * (b + 1))] for b in range(8)])
    four = [[(WB * b, WB * (b + 1))] for b in range(4)]
    for l in range(LAYERS):
        arr[f"w_ple{l}"] = chunks(a["ple_w"][l], four)
        arr[f"w_gate{l}"] = chunks(a["ple_gate_w"][l], four)
        for part, first, n in (("A", 0, FA), ("B", FA, FB)):
            arr[f"w_in{part}{l}"] = chunks(a["ffn_w_in"][l], [[(256 * b, 256 * (b + 1)), (FFN + 256 * b, FFN + 256 * (b + 1))]
                                                              for b in range(first, first + n)])
            arr[f"w_out{part}{l}"] = chunks(a["ffn_w_out"][l][256 * first:256 * (first + n)], four)
    for k in ("ln1_g", "ln1_b", "ln2_g", "ln2_b"):
        arr[k] = a[k]
    arr["norm_gain"] = np.concatenate([a["mla_q_norm"][0], a["mla_kv_norm"][0]])
    arr["pos"] = np.ascontiguousarray(a["positions"][0].reshape(TT, P).T)
    arr["s5_are"] = a["s5_a_re"][0].reshape(PAIRS, P)
    arr["s5_aim"] = a["s5_a_im"][0].reshape(PAIRS, P)
    arr["s5_ldt"] = a["s5_log_dt"][0].reshape(PAIRS, 2)
    b4 = np.zeros((SUB, 2, GROUP, PAIRS, 2, 2, 64), a["s5_b_re"].dtype)
    c = np.zeros((2, 64, PAIRS, 2, 2, GROUP), a["s5_c_re"].dtype)
    bt = np.zeros((2, 64, PAIRS, 2, 2, GROUP), a["s5_b_re"].dtype)
    for n, k in enumerate(("re", "im")):
        bk = a[f"s5_b_{k}"][0].reshape(PAIRS, 2, 64, GROUP)
        ck = a[f"s5_c_{k}"][0].reshape(PAIRS, 2, GROUP, 64)
        for g in range(2):
            b4[:, g, :, :, n, g, :] = bk[:, g].transpose(2, 0, 1)[None]
            bt[g, :, :, n, g, :] = bk[:, g].transpose(1, 0, 2)
            c[g, :, :, n, g, :] = ck[:, g].transpose(2, 0, 1)
    arr["s5_b"] = b4.reshape(P, PAIRS, 2, P)
    arr["s5_c"] = c.reshape(P, PAIRS, 2, 2 * GROUP)
    arr["s5_bt"] = bt.reshape(P, PAIRS, 2, 2 * GROUP)
    d = np.zeros((4, PW, KT, PW), a["s5_d"].dtype)
    for n in range(PW):
        d[:, n, :, n] = a["s5_d"][0].reshape(KT, 4, PW)[:, :, n].T
    arr["s5_skip"] = d.reshape(P, KT, PW)
    arr["ident"] = np.eye(P, dtype=np.float32)
    arr["inv_freq"] = np.float32(10000.0) ** (-np.arange(HALF, dtype=np.float32) / np.float32(HALF))
    q = np.concatenate([np.arange(P)[:, None] + np.zeros((1, P), int), P + np.arange(P)[:, None] + np.zeros((1, 2 * P), int)], axis=1)
    key = np.concatenate([np.arange(P), np.arange(2 * P)])[None, :]
    dist = q - key
    n = ((dist >= 0) & (dist <= 128)) * 1.0 + ((dist >= 0) & (dist % 4 == 0)) + ((dist >= 0) & (dist % 16 == 0))
    log_n = np.log(np.maximum(n, 1.0))
    bias = [np.where(n > 0, (log_n - slope * dist) / DIL_SCALE, -1e30) for slope in SLOPES]
    arr["dil_bias"] = np.stack(bias, axis=1).astype(np.float32)
    arr["causal"] = np.where(dist >= 0, 0.0, -1e30).astype(np.float32)

    nc = bacc.Bacc("TRN2", target_bir_lowering=False, num_devices=1)
    arr = {k: np.ascontiguousarray(v) for k, v in arr.items()}
    t = {k: nc.dram_tensor(f"in_{k}", v.shape, mybir.dt.from_np(v.dtype), kind="ExternalInput").ap() for k, v in arr.items()}
    out = nc.dram_tensor("out_h", (TOK, D), F32, kind="ExternalOutput").ap()
    build(nc, t, out)
    r = run(nc, [{f"in_{k}": v for k, v in arr.items()}], core_ids=[0])
    return r.results[0]["out_h"].reshape(1, TOK, D)
```
